# Optimizing a Trainium2 kernel written in Bass

```python
import math
import numpy as np
import jax
import jax.numpy as jnp
from jax import lax

D_MODEL = 1024
BATCH = 1
SEQ = 128
DEPTH = 2
DEC_BATCH = 1
DEC_SEQ = 256
PAST_LEN = 128

F32 = jnp.float32
GRID_W = 64
ROPE_BASE = 10000.0
EPS = 1e-6
CHUNK = 64
Q_BLOCK = 128
TOK_BLOCK = 128
R_HEADS = 4
R_DK = 128
R_DV = 256
D_HEADS = 8
D_HD = 64
G_HEADS = 8
G_DK = 128
G_DV = 128
CONV_K = 7
G_QKV = G_HEADS * (2 * G_DK + G_DV)
N_BRANCH = 3
BRANCH_W = R_HEADS * R_DV
PEER_HEADS = 8
PEER_DQ = 256
N_KEYS = 128
N_EXPERTS = N_KEYS * N_KEYS
PEER_TOPK = 16
IN_SPLITS = (R_HEADS * R_DK, R_HEADS * R_DK, R_HEADS * R_DV, R_HEADS * R_DV,
             D_HEADS * 2 * D_HD, D_HEADS * 2 * D_HD, D_HEADS * 2 * D_HD,
             G_QKV, G_HEADS * G_DV, 2 * G_HEADS, 2 * G_HEADS, N_BRANCH * D_MODEL)
IN_COLS = sum(IN_SPLITS)

kernel_name = 'hybrid_ret_diffattn_gdn_peer_diffusion_step'

def rmsnorm(x, w):
    xf = x.astype(F32)
    y = xf * lax.rsqrt(jnp.mean(xf * xf, axis=-1, keepdims=True) + EPS)
    return (y * w.astype(F32)).astype(x.dtype)

def l2norm(x):
    xf = x.astype(F32)
    return (xf * lax.rsqrt(jnp.sum(xf * xf, axis=-1, keepdims=True) + EPS)).astype(x.dtype)

def flip(x):
    return jnp.flip(x, axis=1)

def axial_rope(x):
    L, dim = x.shape[1], x.shape[-1]
    n_rows = L // GRID_W
    row = jnp.repeat(jnp.arange(n_rows), GRID_W).astype(F32)
    col = jnp.tile(jnp.arange(GRID_W), n_rows).astype(F32)
    nf = dim // 4
    inv = jnp.power(ROPE_BASE, -jnp.arange(nf, dtype=F32) / nf)
    ang_r = row[:, None] * inv
    ang_c = col[:, None] * inv
    ang = jnp.concatenate([ang_r, ang_r, ang_c, ang_c], axis=-1)
    shape = (1, L) + (1,) * (x.ndim - 3) + (dim,)
    cos = jnp.cos(ang).reshape(shape)
    sin = jnp.sin(ang).reshape(shape)
    xf = x.astype(F32)
    x_r1, x_r2, x_c1, x_c2 = jnp.split(xf, 4, axis=-1)
    rot = jnp.concatenate([-x_r2, x_r1, -x_c2, x_c1], axis=-1)
    return (xf * cos + rot * sin).astype(x.dtype)

def to_chunks(x):
    B, L, H = x.shape[:3]
    x = x.reshape((B, L // CHUNK, CHUNK, H) + x.shape[3:])
    return jnp.moveaxis(x, 3, 1)

def from_chunks(x):
    x = jnp.moveaxis(x, 1, 3)
    B, N, C, H = x.shape[:4]
    return x.reshape((B, N * C, H) + x.shape[4:])

def retention_scan(q, k, v, log_gamma, s0):
    dtype = v.dtype
    q = to_chunks(q.astype(F32) * R_DK ** -0.5)
    k = to_chunks(k.astype(F32))
    v = to_chunks(v.astype(F32))
    pos = jnp.arange(CHUNK, dtype=F32)
    lg = log_gamma.astype(F32)[:, None]
    dist = pos[:, None] - pos[None, :]
    intra = jnp.exp(jnp.where(dist >= 0, lg[:, :, None] * dist, -jnp.inf))
    q_dec = jnp.exp(lg * (pos + 1.0))[:, :, None]
    k_dec = jnp.exp(lg * (CHUNK - 1.0 - pos))[:, :, None]
    c_dec = jnp.exp(lg * CHUNK)[:, :, None]

    def step(s, xs):
        qc, kc, vc = xs
        a = jnp.einsum('bhqd,bhkd->bhqk', qc, kc) * intra
        o = jnp.einsum('bhqk,bhkv->bhqv', a, vc) + jnp.einsum('bhqd,bhdv->bhqv', qc, s) * q_dec
        s = s * c_dec + jnp.einsum('bhkd,bhkv->bhdv', kc * k_dec, vc)
        return s, o

    xs = (jnp.moveaxis(q, 2, 0), jnp.moveaxis(k, 2, 0), jnp.moveaxis(v, 2, 0))
    s, o = lax.scan(step, s0.astype(F32), xs)
    return from_chunks(jnp.moveaxis(o, 0, 2)).astype(dtype), s

def gdn_scan(q, k, v, g, beta, s0):
    dtype = v.dtype
    q = to_chunks(q.astype(F32) * G_DK ** -0.5)
    k = to_chunks(k.astype(F32))
    v = to_chunks(v.astype(F32))
    g = jnp.cumsum(to_chunks(g.astype(F32)), axis=-1)
    beta = to_chunks(beta.astype(F32))
    incl = jnp.tril(jnp.ones((CHUNK, CHUNK), dtype=bool))
    strict = jnp.tril(jnp.ones((CHUNK, CHUNK), dtype=bool), -1)
    decay = jnp.exp(jnp.where(incl, g[..., :, None] - g[..., None, :], -jnp.inf))
    kb = k * beta[..., None]
    a = jnp.where(strict, jnp.einsum('bhnid,bhnjd->bhnij', kb, k) * decay, 0.0)
    eye = jnp.eye(CHUNK, dtype=F32)
    t = lax.linalg.triangular_solve(a + eye, jnp.broadcast_to(eye, a.shape), left_side=True, lower=True)
    u = t @ (v * beta[..., None])
    w = t @ (kb * jnp.exp(g)[..., None])
    qk = jnp.einsum('bhnid,bhnjd->bhnij', q, k) * decay
    qg = q * jnp.exp(g)[..., None]
    kd = k * jnp.exp(g[..., -1:] - g)[..., None]
    gl = jnp.exp(g[..., -1])[..., None, None]

    def step(s, xs):
        qg_c, kd_c, u_c, w_c, qk_c, gl_c = xs
        u_new = u_c - w_c @ s
        o = qg_c @ s + qk_c @ u_new
        s = s * gl_c + jnp.swapaxes(kd_c, -1, -2) @ u_new
        return s, o

    xs = tuple(jnp.moveaxis(arr, 2, 0) for arr in (qg, kd, u, w, qk, gl))
    s, o = lax.scan(step, s0.astype(F32), xs)
    return from_chunks(jnp.moveaxis(o, 0, 2)).astype(dtype), s

def diff_attention(q, k, v, lam):
    B, Lq = q.shape[:2]
    nb = Lq // Q_BLOCK
    qb = jnp.moveaxis(q.reshape((B, nb, Q_BLOCK) + q.shape[2:]), 1, 0)
    scale = D_HD ** -0.5

    def attend(qblk):
        s = jnp.einsum('bqhpd,bkhpd->bhpqk', qblk, k).astype(F32) * scale
        p = jax.nn.softmax(s, axis=-1)
        wts = p[:, :, 0] - lam * p[:, :, 1]
        return jnp.einsum('bhqk,bkhe->bqhe', wts.astype(v.dtype), v)

    o = lax.map(attend, qb)
    return jnp.moveaxis(o, 0, 1).reshape(B, Lq, D_HEADS, 2 * D_HD)

def centred_dwconv(x, w):
    pad = (w.shape[0] - 1) // 2
    return lax.conv_general_dilated(x, w[:, None, :].astype(x.dtype), window_strides=(1,),
                                    padding=[(pad, pad)], dimension_numbers=('NWC', 'WIO', 'NWC'),
                                    feature_group_count=x.shape[-1])

def peer_ffn(h, w_q, sub_keys, exp_u, exp_v):
    B, L, D = h.shape
    hb = h.reshape(B * L // TOK_BLOCK, TOK_BLOCK, D)

    def block(hx):
        q = (hx @ w_q).reshape(TOK_BLOCK, PEER_HEADS, 2, PEER_DQ // 2)
        s = jnp.einsum('thpd,pnd->thpn', q, sub_keys).astype(F32)
        s_top, i_top = lax.top_k(s, PEER_TOPK)
        cand_s = (s_top[:, :, 0, :, None] + s_top[:, :, 1, None, :]).reshape(TOK_BLOCK, PEER_HEADS, PEER_TOPK * PEER_TOPK)
        cand_i = (i_top[:, :, 0, :, None] * N_KEYS + i_top[:, :, 1, None, :]).reshape(TOK_BLOCK, PEER_HEADS, PEER_TOPK * PEER_TOPK)
        best_s, pos = lax.top_k(cand_s, PEER_TOPK)
        idx = jnp.take_along_axis(cand_i, pos, axis=-1)
        gate = jax.nn.softmax(best_s, axis=-1)
        act = jax.nn.gelu(jnp.einsum('thkd,td->thk', exp_u[idx], hx).astype(F32), approximate=False)
        return jnp.einsum('thk,thkd->td', (gate * act).astype(hx.dtype), exp_v[idx])

    return lax.map(block, hb).reshape(B, L, D)

def token_mixing(h, lw, li, ctx):
    B, L, _ = h.shape
    latent = ctx is not None
    proj = h @ lw['w_in']
    cuts = np.cumsum(IN_SPLITS)[:-1].tolist()
    (r_q, r_k, r_v, r_g, d_q, d_k, d_v, g_qkv, g_z, g_a, g_b, m_g) = jnp.split(proj, cuts, axis=-1)

    r_q = r_q.reshape(B, L, R_HEADS, R_DK)
    r_k = r_k.reshape(B, L, R_HEADS, R_DK)
    r_v = r_v.reshape(B, L, R_HEADS, R_DV)
    if latent:
        r_q, r_k = axial_rope(r_q), axial_rope(r_k)
        r0_f, r0_b = ctx['ret'][:, 0], ctx['ret'][:, 1]
    else:
        r0_f = r0_b = jnp.zeros((B, R_HEADS, R_DK, R_DV), F32)
    log_gamma = jax.nn.log_sigmoid(lw['ret_decay'].astype(F32))
    or_f, sr_f = retention_scan(r_q, r_k, r_v, log_gamma[0], r0_f)
    or_b, sr_b = retention_scan(flip(r_q), flip(r_k), flip(r_v), log_gamma[1], r0_b)
    o_ret = rmsnorm(or_f + flip(or_b), lw['ret_norm']).reshape(B, L, BRANCH_W) * jax.nn.silu(r_g)

    d_q = d_q.reshape(B, L, D_HEADS, 2, D_HD)
    d_k = d_k.reshape(B, L, D_HEADS, 2, D_HD)
    d_v = d_v.reshape(B, L, D_HEADS, 2 * D_HD)
    if latent:
        q_att = axial_rope(d_q)
        k_all = jnp.concatenate([axial_rope(d_k), ctx['k']], axis=1)
        v_all = jnp.concatenate([d_v, ctx['v']], axis=1)
    else:
        q_att, k_all, v_all = d_q, d_k, d_v
    lam_init = 0.8 - 0.6 * math.exp(-0.3 * li)
    lp = lw['diff_lambda'].astype(F32)
    lam = jnp.exp(jnp.sum(lp[0] * lp[1])) - jnp.exp(jnp.sum(lp[2] * lp[3])) + lam_init
    o_diff = diff_attention(q_att, k_all, v_all, lam)
    o_diff = (rmsnorm(o_diff, lw['diff_norm']) * (1.0 - lam_init)).reshape(B, L, BRANCH_W)

    g_qkv = jax.nn.silu(centred_dwconv(g_qkv, lw['gdn_conv']))
    g_q, g_k, g_v = jnp.split(g_qkv, [G_HEADS * G_DK, 2 * G_HEADS * G_DK], axis=-1)
    g_q = l2norm(g_q.reshape(B, L, G_HEADS, G_DK))
    g_k = l2norm(g_k.reshape(B, L, G_HEADS, G_DK))
    g_v = g_v.reshape(B, L, G_HEADS, G_DV)
    g_a = g_a.reshape(B, L, 2, G_HEADS).astype(F32)
    g_b = g_b.reshape(B, L, 2, G_HEADS).astype(F32)
    g_log = -jnp.exp(lw['gdn_A_log'].astype(F32)) * jax.nn.softplus(g_a + lw['gdn_dt_bias'].astype(F32))
    g_beta = jax.nn.sigmoid(g_b)
    if latent:
        g0_f, g0_b = ctx['gdn'][:, 0], ctx['gdn'][:, 1]
    else:
        g0_f = g0_b = jnp.zeros((B, G_HEADS, G_DK, G_DV), F32)
    og_f, sg_f = gdn_scan(g_q, g_k, g_v, g_log[:, :, 0], g_beta[:, :, 0], g0_f)
    og_b, sg_b = gdn_scan(flip(g_q), flip(g_k), flip(g_v), flip(g_log[:, :, 1]), flip(g_beta[:, :, 1]), g0_b)
    o_gdn = rmsnorm(og_f + flip(og_b), lw['gdn_norm']) * jax.nn.silu(g_z.reshape(B, L, G_HEADS, G_DV))
    o_gdn = o_gdn.reshape(B, L, BRANCH_W)

    branches = jnp.stack([o_ret, o_diff, o_gdn], axis=2)
    merged = jnp.einsum('blnw,nwd->blnd', branches, lw['w_branch'])
    gates = jax.nn.sigmoid(m_g.reshape(B, L, N_BRANCH, D_MODEL))
    m = jnp.sum(gates * merged, axis=2) @ lw['w_out']
    if latent:
        return m, None
    state = (d_k, d_v,
             jnp.stack([sr_f, sr_b], axis=1).astype(h.dtype),
             jnp.stack([sg_f, sg_b], axis=1).astype(h.dtype))
    return m, state

def trunk_layer(x, cond, lw, li, ctx):
    mod = jax.nn.silu(cond) @ lw['w_mod'] + lw['b_mod']
    sh1, sc1, g1, sh2, sc2, g2 = jnp.split(mod[:, None, :], 6, axis=-1)
    h = rmsnorm(x, lw['norm1']) * (1 + sc1) + sh1
    m, state = token_mixing(h, lw, li, ctx)
    x = x + g1 * m
    h = rmsnorm(x, lw['norm2']) * (1 + sc2) + sh2
    x = x + g2 * peer_ffn(h, lw['peer_wq'], lw['peer_keys'], lw['peer_u'], lw['peer_v'])
    return x, state

def setup_inputs(seed: int = 0) -> dict:
    key = jax.random.key(seed)
    ks = jax.random.split(key, 32)
    D = D_MODEL

    def nrm(k, shape, s=1.0):
        return jax.random.normal(k, shape, F32) * s

    base = 1.0 - 2.0 ** (-5.0 - np.arange(R_HEADS))
    ret_logit = jnp.asarray(np.log(base) - np.log1p(-base), F32)
    dt = jnp.exp(jax.random.uniform(ks[20], (DEPTH, 2, G_HEADS), F32, math.log(1e-3), math.log(1e-1)))
    return {
        'x_prompt': nrm(ks[0], (BATCH, SEQ, D)),
        'x_sample': nrm(ks[1], (DEC_BATCH, DEC_SEQ, D)),
        'cache_diff_k': nrm(ks[2], (DEC_BATCH, DEPTH, PAST_LEN, D_HEADS, 2, D_HD)),
        'cache_diff_v': nrm(ks[3], (DEC_BATCH, DEPTH, PAST_LEN, D_HEADS, 2 * D_HD)),
        'state_ret': nrm(ks[4], (DEC_BATCH, DEPTH, 2, R_HEADS, R_DK, R_DV), 4.0),
        'state_gdn': nrm(ks[5], (DEC_BATCH, DEPTH, 2, G_HEADS, G_DK, G_DV), 0.5),
        'c': nrm(ks[6], (DEC_BATCH, D)),
        'c_ctx': nrm(ks[7], (D,)),
        'norm1_w': 1.0 + nrm(ks[8], (DEPTH, D), 0.05),
        'norm2_w': 1.0 + nrm(ks[9], (DEPTH, D), 0.05),
        'w_mod': nrm(ks[10], (DEPTH, D, 6 * D), 0.5 * D ** -0.5),
        'b_mod': nrm(ks[11], (DEPTH, 6 * D), 0.01),
        'w_in': nrm(ks[12], (DEPTH, D, IN_COLS), D ** -0.5),
        'ret_decay': ret_logit[None, None, :] + nrm(ks[13], (DEPTH, 2, R_HEADS), 0.1),
        'ret_norm': 1.0 + nrm(ks[14], (DEPTH, R_DV), 0.05),
        'diff_lambda': nrm(ks[15], (DEPTH, 4, D_HD), 0.1),
        'diff_norm': 1.0 + nrm(ks[16], (DEPTH, 2 * D_HD), 0.05),
        'gdn_conv': nrm(ks[17], (DEPTH, CONV_K, G_QKV), CONV_K ** -0.5),
        'gdn_A_log': jnp.log(jax.random.uniform(ks[18], (DEPTH, 2, G_HEADS), F32, 1.0, 16.0)),
        'gdn_dt_bias': dt + jnp.log(-jnp.expm1(-dt)),
        'gdn_norm': 1.0 + nrm(ks[19], (DEPTH, G_DV), 0.05),
        'w_branch': nrm(ks[21], (DEPTH, N_BRANCH, BRANCH_W, D), BRANCH_W ** -0.5),
        'w_out': nrm(ks[22], (DEPTH, D, D), D ** -0.5),
        'peer_wq': nrm(ks[23], (DEPTH, D, PEER_HEADS * PEER_DQ), D ** -0.5),
        'peer_keys': nrm(ks[24], (DEPTH, 2, N_KEYS, PEER_DQ // 2), (PEER_DQ // 2) ** -0.5),
        'peer_u': nrm(ks[25], (DEPTH, N_EXPERTS, D), D ** -0.5),
        'peer_v': nrm(ks[26], (DEPTH, N_EXPERTS, D), 1.0),
        'norm_f_w': 1.0 + nrm(ks[27], (D,), 0.05),
    }

def reference(x_prompt, x_sample, cache_diff_k, cache_diff_v, state_ret, state_gdn, c, c_ctx,
              norm1_w, norm2_w, w_mod, b_mod, w_in, ret_decay, ret_norm, diff_lambda, diff_norm,
              gdn_conv, gdn_A_log, gdn_dt_bias, gdn_norm, w_branch, w_out,
              peer_wq, peer_keys, peer_u, peer_v, norm_f_w):
    layers = [dict(norm1=norm1_w[i], norm2=norm2_w[i], w_mod=w_mod[i], b_mod=b_mod[i], w_in=w_in[i],
                   ret_decay=ret_decay[i], ret_norm=ret_norm[i], diff_lambda=diff_lambda[i],
                   diff_norm=diff_norm[i], gdn_conv=gdn_conv[i], gdn_A_log=gdn_A_log[i],
                   gdn_dt_bias=gdn_dt_bias[i], gdn_norm=gdn_norm[i], w_branch=w_branch[i], w_out=w_out[i],
                   peer_wq=peer_wq[i], peer_keys=peer_keys[i], peer_u=peer_u[i], peer_v=peer_v[i])
              for i in range(DEPTH)]

    y = x_prompt
    ctx_cond = c_ctx[None, :]
    ks, vs, srs, sgs = [], [], [], []
    for li in range(DEPTH):
        y, (k_l, v_l, sr_l, sg_l) = trunk_layer(y, ctx_cond, layers[li], li, None)
        ks.append(k_l)
        vs.append(v_l)
        srs.append(sr_l)
        sgs.append(sg_l)
    y_prompt = rmsnorm(y, norm_f_w)

    z = x_sample
    for li in range(DEPTH):
        ctx = {'k': cache_diff_k[:, li], 'v': cache_diff_v[:, li], 'ret': state_ret[:, li], 'gdn': state_gdn[:, li]}
        z, _ = trunk_layer(z, c, layers[li], li, ctx)
    y_sample = rmsnorm(z, norm_f_w)

    new_cache_diff_k = jnp.stack(ks, axis=1)
    new_cache_diff_v = jnp.stack(vs, axis=1)
    new_state_ret = jnp.stack(srs, axis=1)
    new_state_gdn = jnp.stack(sgs, axis=1)
    return (y_prompt, y_sample, new_cache_diff_k, new_cache_diff_v, new_state_ret, new_state_gdn)


_drawn_inputs = setup_inputs


def setup_inputs(seed=0):
    import zlib

    import numpy as np

    out = dict(_drawn_inputs(seed))
    spreads = {}
    factors = {'ret_norm': 2.753, 'diff_lambda': 4.63}
    for name, (base, spread) in spreads.items():
        noise = np.random.default_rng([zlib.crc32(name.encode()), seed]).standard_normal(out[name].shape)
        drawn = base * np.exp(spread * noise) if base else spread * noise
        out[name] = jnp.asarray(drawn.astype(out[name].dtype))
    for name, factor in factors.items():
        out[name] = (out[name] * factor).astype(out[name].dtype)
    return out
```

```python
import math
from contextlib import ExitStack

import numpy as np

import concourse.bass as bass
from concourse import mybir

F32 = mybir.dt.float32
U32 = mybir.dt.uint32
ALU = mybir.AluOpType
ACT = mybir.ActivationFunctionType
AX = mybir.AxisListType.X
ds = bass.ds

P = 128
D = 1024
KT = D // P
DEPTH = 2
SEQ = 128
DEC_SEQ = 256
TILES = (SEQ + DEC_SEQ) // P
TOK = TILES * P
PAST = 128
GRID_W = 64
ROPE_BASE = 10000.0
EPS = 1e-6
R_HEADS, R_DK, R_DV = 4, 128, 256
D_HEADS, D_HD = 8, 64
G_HEADS, G_DK, G_DV = 8, 128, 128
CONV_K = 7
G_QKV = G_HEADS * (2 * G_DK + G_DV)
N_BRANCH = 3
PEER_HEADS, PEER_DQ, N_KEYS, TOPK = 8, 256, 128, 16
N_EXPERTS = N_KEYS * N_KEYS
SLOTS = PEER_HEADS * TOPK
MOD = 6 * D
CHUNK = 512
COL_RET = 0
COL_RET_G = 2 * R_HEADS * R_DK + R_HEADS * R_DV
COL_DIFF = COL_RET_G + R_HEADS * R_DV
COL_GDN = COL_DIFF + 3 * D_HEADS * 2 * D_HD
COL_GDN_Z = COL_GDN + G_QKV
COL_GDN_AB = COL_GDN_Z + G_HEADS * G_DV
COL_GATES = COL_GDN_AB + 4 * G_HEADS
PAD = CONV_K // 2
XC_P = PAD
XC_S = PAD + SEQ + 2 * PAD
XC_W = XC_S + DEC_SEQ + PAD
CV_W = XC_W - 2 * PAD
CV_S = XC_S - PAD
QBLK = G_QKV // P
LEVELS = 7
LATENT = (1, 2)
BIGNEG = -3.0e38
POS_QF, POS_QB, POS_KF, POS_KB, POS_IOTA = 0, 2, 4, 5, 6
TRI_POS, TRI_NEG, TRI_UP, TRI_LO, TRI_ID, TRI_ONE, TRI_OFF_F, TRI_OFF_B = range(8)


def shape_tables():
    j = np.arange(P, dtype=np.float32)[:, None]
    i = np.arange(P, dtype=np.float32)[None, :]
    tri = np.stack([np.maximum(i - j, 0), np.maximum(j - i, 0), (i >= j) * 1.0, (j >= i) * 1.0,
                    np.eye(P), np.ones((P, P)), i - j + P, j - i + P], 1).astype(np.float32)
    lvl = np.zeros((P, 2, LEVELS, P), np.float32)
    jj, ii = np.arange(P)[:, None], np.arange(P)[None, :]
    for n in range(LEVELS):
        s = 1 << n
        same = (jj // (2 * s)) == (ii // (2 * s))
        lvl[:, 0, n] = same & (jj % (2 * s) < s) & (ii % (2 * s) >= s)
        lvl[:, 1, n] = same & (ii % (2 * s) < s) & (jj % (2 * s) >= s)
    p = np.arange(P, dtype=np.float32)
    pos = np.zeros((P, POS_IOTA + TOPK), np.float32)
    pos[:, POS_QF] = p + 1
    pos[:, POS_QF + 1] = p + P + 1
    pos[:, POS_QB] = DEC_SEQ - p
    pos[:, POS_QB + 1] = DEC_SEQ - P - p
    pos[:, POS_KF] = SEQ - 1 - p
    pos[:, POS_KB] = p
    pos[:, POS_IOTA:] = np.arange(TOPK)

    def rope(dim):
        nf = dim // 4
        rows = DEC_SEQ // GRID_W
        row = np.repeat(np.arange(rows), GRID_W).astype(np.float32)
        col = np.tile(np.arange(GRID_W), rows).astype(np.float32)
        inv = np.power(np.float32(ROPE_BASE), -np.arange(nf, dtype=np.float32) / np.float32(nf)).astype(np.float32)
        r, c = row[:, None] * inv, col[:, None] * inv
        ang = np.concatenate([r, r, c, c], -1).astype(np.float64)
        sign = np.repeat([-1.0, 1.0, -1.0, 1.0], nf)
        t = np.stack([np.cos(ang), np.sin(ang) * sign], 1).astype(np.float32)
        return t.reshape(len(LATENT), P, 2, dim).transpose(1, 0, 2, 3).copy()

    lam = np.zeros((DEPTH, 4), np.float32)
    for li in range(DEPTH):
        init = 0.8 - 0.6 * math.exp(-0.3 * li)
        lam[li] = [init, 1.0 - init, li * N_EXPERTS, 0]
    return {"tri": tri, "lvl": lvl, "pos": pos, "rope_ret": rope(R_DK), "rope_diff": rope(D_HD), "layer": lam}


class Chain:

    def __init__(self, eng, sem):
        self.eng, self.sem, self.n, self.k = eng, sem, 0, 0

    def mark(self, ins):
        ins.then_inc(self.sem, 1)
        self.n = self.n + 1
        self.k += 1

    def sync(self):
        self.eng.wait_ge(self.sem, self.n)

    def link(self, ins):
        self.mark(ins)
        self.sync()

    def enter(self, i, per):
        self.base, self.per, self.k = self.n, per, 0
        self.n = self.base + i * per

    def leave(self, passes):
        assert self.k == self.per, (self.k, self.per)
        self.n = self.base + passes * self.per


def bc(ap, n):
    return ap.unsqueeze(1).to_broadcast([ap.shape[0], n, ap.shape[1]])


def bl(ap, n):
    return ap.unsqueeze(2).to_broadcast([ap.shape[0], ap.shape[1], n])


def build(nc, I, O, debug=None):
    ctx = ExitStack()
    with ctx:
        def sb(name, cols, dt=F32):
            return ctx.enter_context(nc.sbuf_tensor(name, [P, cols], dt))[:, :]

        PS = [ctx.enter_context(nc.psum_tensor(f"bank{n}", [P, 512], F32))[:, :] for n in range(8)]
        X = sb("x_residual", TILES * D).rearrange("p (t n) -> p t n", t=TILES)
        H = sb("h_tokens", TILES * D).rearrange("p (t n) -> p t n", t=TILES)
        HT = sb("h_features", KT * TOK).rearrange("p (k n) -> p k n", k=KT)
        MACC = sb("merged", TILES * D).rearrange("p (t n) -> p t n", t=TILES)
        Zf = sb("gates_z", TILES * D)
        Z = Zf.rearrange("p (t n) -> p t n", t=TILES)
        RING = sb("weight_ring", 2 * KT * CHUNK)
        RW = RING.rearrange("p (s k n) -> p s k n", s=2, k=KT)
        BIG = sb("work", 18432)
        HALF = 9216
        SST = sb("gdn_states", 2 * G_HEADS * G_DV).rearrange("p (g n) -> p g n", g=2 * G_HEADS)
        TRI = sb("triangles", 8 * P).rearrange("p (a n) -> p a n", a=8)
        LVL = sb("levels", 2 * LEVELS * P).rearrange("p (d a n) -> p d a n", d=2, a=LEVELS)
        POS = sb("positions", POS_IOTA + TOPK)
        ROPR = sb("rope_ret", 2 * 2 * R_DK).rearrange("p (t a n) -> p t a n", t=2, a=2)
        ROPD = sb("rope_diff", 2 * 2 * D_HD).rearrange("p (t a n) -> p t a n", t=2, a=2)
        LAMC = sb("layer_constants", 4)
        COND = sb("conditions", KT * 2).rearrange("p (k g) -> p k g", g=2)
        SM = sb("small", 1024)
        modd = nc.dram_tensor("mod_rows", (2, MOD), F32).ap()

        ID = TRI[:, TRI_ID, :]
        PRJ = BIG[:, 0:HALF].rearrange("p (t n) -> p t n", t=TILES)
        UP = BIG[:, HALF:2 * HALF]

        pools = [[ctx.enter_context(nc.semaphore(f"stage{n}_{k}")) for k in range(40)] for n in range(2)]
        assert all([x.num for x in pool] == list(range(pool[0].num, pool[0].num + 40)) for pool in pools)
        got = [ctx.enter_context(nc.semaphore(f"row_gathered{n}")) for n in range(16)]
        turns = [1]

        def signals(names):
            turns[0] = 1 - turns[0]
            names = names.split()
            assert len(names) <= len(pools[0])
            return dict(zip(names, pools[turns[0]]))

        def clear_last_stage(dve, s):
            other = pools[1] if any(x.num == pools[0][0].num for x in s.values()) else pools[0]
            dve.sem_clear(range(other[0].num, other[-1].num + 1))

        def sp_weights(sp, src, chunks, base, free, loaded):
            with sp.Fori(0, chunks // 2) as i:
                for j in range(2):
                    sp.wait_ge(free, base + 2 * i + j + 1)
                    sp.dma_start(RW[:, j], src(2 * i + j)).then_inc(loaded[j], 16)

        def pe_project(pe, xt, chunks, base, free, loaded, banks_free, done):
            with pe.Fori(0, chunks // 2) as i:
                for j in range(2):
                    pe.wait_ge(loaded[j], 16 * (base // 2 + 1) + 16 * i)
                    pe.wait_ge(banks_free, base + 2 * i + j + 1)
                    for t in range(TILES):
                        for k in range(KT):
                            mm = nc.tensor.matmul(PS[3 * j + t], xt[j][:, k, t * P:(t + 1) * P], RW[:, j, k, :],
                                                  start=(k == 0), stop=(k == KT - 1))
                        mm.then_inc(done, 1)
                    pe.drain().then_inc(free, 1)

        def pe_transpose_tokens(pe, src, ready, banks_free, done):
            for t in range(TILES):
                pe.wait_ge(ready, t + 1)
                for b in range(2):
                    n = 2 * t + b
                    if n >= 2:
                        pe.wait_ge(banks_free, n - 1)
                    for k in range(4):
                        kk = 4 * b + k
                        mm = nc.tensor.transpose(PS[6 + b][:, k * P:(k + 1) * P], src[:, t, kk * P:(kk + 1) * P], ID)
                    mm.then_inc(done, 1)

        def act_transposed(act, dst, done, out_sem):
            for t in range(TILES):
                for b in range(2):
                    act.wait_ge(done, 2 * t + b + 1)
                    nc.scalar.activation(dst[:, 4 * b:4 * b + 4, t * P:(t + 1) * P],
                                         PS[6 + b].rearrange("p (k n) -> p k n", k=4), ACT.Copy).then_inc(out_sem, 1)

        with nc.Block(no_gpsimd_drain=True) as block:
            s = signals("loads silu")

            @block.sync
            def _(sp):
                sp.dma_start(X[:, 0, :], I["x_prompt"][0]).then_inc(s["loads"], 16)
                sp.dma_start(X[:, 1:3, :], I["x_sample"][0].rearrange("(t p) n -> p t n", p=P)).then_inc(s["loads"], 16)
                sp.dma_start(TRI, I["tri"]).then_inc(s["loads"], 16)
                sp.dma_start(LVL, I["lvl"]).then_inc(s["loads"], 16)
                sp.dma_start(POS, I["pos"]).then_inc(s["loads"], 16)
                sp.dma_start(ROPR, I["rope_ret"]).then_inc(s["loads"], 16)
                sp.dma_start(ROPD, I["rope_diff"]).then_inc(s["loads"], 16)
                with nc.allow_non_contiguous_dma(reason="two short vectors, laid over partitions"):
                    sp.dma_start(SM[:, 0:KT], I["c_ctx"].rearrange("(k p) -> p k", p=P)).then_inc(s["loads"], 16)
                    sp.dma_start(SM[:, KT:2 * KT], I["c"][0].rearrange("(k p) -> p k", p=P)).then_inc(s["loads"], 16)

            @block.scalar
            def _(act):
                act.wait_ge(s["loads"], 9 * 16)
                for g in range(2):
                    nc.scalar.activation(COND[:, :, g], SM[:, g * KT:(g + 1) * KT], ACT.Silu).then_inc(s["silu"], 1)

        def stage_mod(l):
            s = signals("free loaded0 loaded1 banks_free done added bias stored chain")
            loaded = [s["loaded0"], s["loaded1"]]
            w = I["w_mod"].rearrange("l (k p) n -> l p k n", p=P)
            rows, bias = BIG[0:2, 0:MOD], BIG[0:2, MOD:2 * MOD]
            chunks = MOD // CHUNK
            with nc.Block(no_gpsimd_drain=True) as block:
                @block.sync
                def _(sp):
                    sp.dma_start(bias, I["b_mod"][l].partition_broadcast(2)).then_inc(s["bias"], 16)
                    sp.dma_start(LAMC, I["layer"][l].partition_broadcast(P)).then_inc(s["bias"], 16)
                    sp_weights(sp, lambda n: w[l, :, :, ds(n * CHUNK, CHUNK)], chunks, 0, s["free"], loaded)
                    sp.wait_ge(s["added"], chunks)
                    sp.dma_start(modd, rows).then_inc(s["stored"], 16)
                    sp.wait_ge(s["stored"], 16)

                @block.tensor
                def _(pe):
                    pe.sem_inc(s["free"], 2)
                    with pe.Fori(0, chunks // 2) as i:
                        for j in range(2):
                            pe.wait_ge(loaded[j], 16 + 16 * i)
                            pe.wait_ge(s["banks_free"], 2 * i + j + 1)
                            for k in range(KT):
                                mm = nc.tensor.matmul(PS[j][0:2, :], COND[:, k, :], RW[:, j, k, :],
                                                      start=(k == 0), stop=(k == KT - 1))
                            mm.then_inc(s["done"], 1)
                            pe.drain().then_inc(s["free"], 1)

                @block.vector
                def _(dve):
                    clear_last_stage(dve, s)
                    dve.sem_inc(s["banks_free"], 2)
                    dve.wait_ge(s["bias"], 32)
                    with dve.Fori(0, chunks // 2) as i:
                        for j in range(2):
                            dve.wait_ge(s["done"], 2 * i + j + 1)
                            cols = ds(2 * CHUNK * i + j * CHUNK, CHUNK)
                            nc.vector.tensor_tensor(rows[:, cols], PS[j][0:2, :], bias[:, cols], ALU.add)\
                                .then_inc(s["added"], 1)
                            dve.drain().then_inc(s["banks_free"], 1)

        def stage_norm(l, which):
            s = signals("loads squares mean root ready free done copied chain")
            norm_w = I["norm1_w"] if which == 0 else I["norm2_w"]
            NW = UP[:, 0:D]
            SH = UP[:, D:3 * D].rearrange("p (g n) -> p g n", g=2)
            SC = UP[:, 3 * D:5 * D].rearrange("p (g n) -> p g n", g=2)
            SQ = UP[:, 5 * D:8 * D].rearrange("p (t n) -> p t n", t=TILES)
            SS = SM[:, 0:TILES]
            RS = SM[:, 4:4 + TILES]
            off = 3 * D * which
            with nc.Block(no_gpsimd_drain=True) as block:
                @block.sync
                def _(sp):
                    sp.dma_start(NW, norm_w[l].partition_broadcast(P)).then_inc(s["loads"], 16)
                    for g in range(2):
                        sp.dma_start(SH[:, g, :], modd[g, off:off + D].partition_broadcast(P)).then_inc(s["loads"], 16)
                        sp.dma_start(SC[:, g, :], modd[g, off + D:off + 2 * D].partition_broadcast(P))\
                            .then_inc(s["loads"], 16)

                @block.scalar
                def _(act):
                    for t in range(TILES):
                        nc.scalar.activation(SQ[:, t, :], X[:, t, :], ACT.Square, accum_out=SS[:, t:t + 1])\
                            .then_inc(s["squares"], 1)
                    act.wait_ge(s["mean"], 1)
                    nc.scalar.activation(RS, SS, ACT.Sqrt).then_inc(s["root"], 1)
                    act_transposed(act, HT, s["done"], s["free"])

                @block.vector
                def _(dve):
                    clear_last_stage(dve, s)
                    c = Chain(dve, s["chain"])
                    dve.wait_ge(s["squares"], TILES)
                    nc.vector.tensor_scalar(SS, SS, 1.0 / D, EPS, ALU.mult, ALU.add).then_inc(s["mean"], 1)
                    dve.wait_ge(s["loads"], 5 * 16)
                    for g in range(2):
                        c.mark(nc.vector.scalar_tensor_tensor(SC[:, g, :], SC[:, g, :], 1.0, NW, ALU.add, ALU.mult))
                    dve.wait_ge(s["root"], 1)
                    c.link(nc.vector.reciprocal(RS, RS))
                    for t in range(TILES):
                        g = int(t > 0)
                        c.link(nc.vector.scalar_tensor_tensor(H[:, t, :], X[:, t, :], RS[:, t:t + 1], SC[:, g, :],
                                                              ALU.mult, ALU.mult))
                        nc.vector.tensor_tensor(H[:, t, :], H[:, t, :], SH[:, g, :], ALU.add).then_inc(s["ready"], 1)

                @block.tensor
                def _(pe):
                    pe_transpose_tokens(pe, H, s["ready"], s["free"], s["done"])

        w_in = I["w_in"].rearrange("l (k p) n -> l p k n", p=P)

        def stage_project(l, parts):
            s = signals("free loaded0 loaded1 banks_free done")
            loaded = [s["loaded0"], s["loaded1"]]
            with nc.Block(no_gpsimd_drain=True) as block:
                @block.sync
                def _(sp):
                    base = 0
                    for col, chunks, _, _ in parts:
                        sp_weights(sp, lambda n: w_in[l, :, :, ds(n * CHUNK + col, CHUNK)], chunks, base, s["free"], loaded)
                        base += chunks

                @block.tensor
                def _(pe):
                    pe.sem_inc(s["free"], 2)
                    base = 0
                    for _, chunks, _, _ in parts:
                        pe_project(pe, (HT, HT), chunks, base, s["free"], loaded, s["banks_free"], s["done"])
                        base += chunks

                @block.scalar
                def _(act):
                    act.sem_inc(s["banks_free"], 2)
                    base = 0
                    for _, chunks, dst, func in parts:
                        with act.Fori(0, chunks // 2) as i:
                            for j in range(2):
                                for t in range(TILES):
                                    act.wait_ge(s["done"], 3 * base + 6 * i + 3 * j + t + 1)
                                    nc.scalar.activation(dst[:, t, ds(2 * CHUNK * i + j * CHUNK, CHUNK)],
                                                         PS[3 * j + t], func)
                                act.drain().then_inc(s["banks_free"], 1)
                        base += chunks

                @block.vector
                def _(dve):
                    clear_last_stage(dve, s)

        def rope(dve, c, view, table, groups, dim, tmp):
            q = dim // 4
            for n, t in enumerate(LATENT):
                x4 = view(t).rearrange("p (g a b n) -> p g a b n", g=groups, a=2, b=2)
                t4 = tmp.rearrange("p (g a b n) -> p g a b n", g=groups, a=2, b=2)
                sin = table[:, n, 1, :].rearrange("p (a b n) -> p a b n", a=2, b=2)
                for b in range(2):
                    sb_ = sin[:, :, b, :].unsqueeze(1).to_broadcast([P, groups, 2, q])
                    c.mark(nc.vector.tensor_tensor(t4[:, :, :, b, :], x4[:, :, :, 1 - b, :], sb_, ALU.mult))
                c.sync()
                x3 = view(t).rearrange("p (g n) -> p g n", g=groups)
                c.link(nc.vector.tensor_tensor(x3, x3, bc(table[:, n, 0, :], groups), ALU.mult))
                c.link(nc.vector.tensor_tensor(view(t), view(t), tmp, ALU.add))

        def log1p_parts(dve, c, z, s_, tmp, out, like):
            c.link(nc.vector.tensor_scalar(s_, z, 2.0, None, ALU.add))
            c.link(nc.vector.reciprocal(s_, s_))
            c.link(nc.vector.tensor_tensor(s_, s_, z, ALU.mult))
            c.link(nc.vector.tensor_tensor(tmp, s_, s_, ALU.mult))
            terms = 8
            c.link(nc.vector.tensor_scalar(out, tmp, 1.0 / (2 * terms + 1), 1.0 / (2 * terms - 1), ALU.mult, ALU.add))
            for n in range(terms - 1, 0, -1):
                c.link(nc.vector.tensor_tensor(out, out, tmp, ALU.mult))
                c.link(nc.vector.tensor_scalar(out, out, 1.0 / (2 * n - 1), None, ALU.add))
            c.link(nc.vector.scalar_tensor_tensor(out, out, 2.0, s_, ALU.mult, ALU.mult))

        def dve_head_norm(dve, c, s, OV, width, sq, cols, w, extra):
            groups = TILES * D // width
            ov = OV.rearrange("p (g n) -> p g n", n=width)
            c.link(nc.vector.tensor_tensor(sq, OV, OV, ALU.mult))
            c.link(nc.vector.tensor_reduce(cols, sq.rearrange("p (g n) -> p g n", n=width), AX, ALU.add))
            nc.vector.tensor_scalar(cols, cols, 1.0 / width, EPS, ALU.mult, ALU.add).then_inc(s["mean"], 1)
            dve.wait_ge(s["root"], 1)
            c.link(nc.vector.reciprocal(cols, cols))
            c.link(nc.vector.tensor_tensor(ov, ov, bl(cols, width), ALU.mult))
            c.link(nc.vector.tensor_tensor(ov, ov, bc(w, groups), ALU.mult))
            if extra is not None:
                c.link(nc.vector.tensor_tensor(OV, OV, extra, ALU.mult))

        def act_head_root(act, s, cols):
            act.wait_ge(s["mean"], 1)
            nc.scalar.activation(cols, cols, ACT.Sqrt).then_inc(s["root"], 1)

        OT_ = UP[:, 0:KT * TOK].rearrange("p (k n) -> p k n", k=KT)
        Hf = H.rearrange("p t n -> p (t n)")

        def stage_retention(l):
            s = signals("loads chain mean root lgin lgexp lg tables roped transposed copied scores masked"
                           " out intra evacuated kd states statecopy stored")
            QT = UP[:, 0:1536].rearrange("p (h n) -> p h n", h=R_HEADS)
            KTT = UP[:, 1536:3072].rearrange("p (h n) -> p h n", h=R_HEADS)
            DT = UP[:, 3072:4608].rearrange("p (h a n) -> p h a n", h=R_HEADS, a=3)
            AT = UP[:, 4608:5888].rearrange("p (b n) -> p b n", b=2)
            E2 = UP[:, 5888:6400].rearrange("p (h n) -> p h n", h=R_HEADS)
            KD = UP[:, 6400:7424].rearrange("p (g n) -> p g n", g=8)
            TMP = RING[:, 0:1024]
            S0 = RING[:, 1024:3072].rearrange("p (g n) -> p g n", g=8)
            ST = RING[:, 3072:5120].rearrange("p (g n) -> p g n", g=8)
            SQ = RING[:, 5120:8192]
            LG, LZ, LS, LT = SM[:, 0:8], SM[:, 8:16], SM[:, 16:24], SM[:, 24:32]
            DEC = SM[:, 32:80].rearrange("p (g n) -> p g n", g=8)
            NWR = SM[:, 128:384]
            COLS = SM[:, 384:396]
            scale = R_DK ** -0.5
            with nc.Block(no_gpsimd_drain=True) as block:
                @block.sync
                def _(sp):
                    sp.dma_start(LG, I["ret_decay"][l].rearrange("d h -> (d h)").partition_broadcast(P))\
                        .then_inc(s["loads"], 16)
                    sp.dma_start(NWR, I["ret_norm"][l].partition_broadcast(P)).then_inc(s["loads"], 16)
                    sp.dma_start(S0, I["state_ret"][0, l].rearrange("d h k v -> k (d h) v")).then_inc(s["loads"], 16)
                    sp.wait_ge(s["statecopy"], 4)
                    sp.dma_start(O["new_state_ret"][0, l].rearrange("d h k v -> k (d h) v"), ST).then_inc(s["stored"], 16)
                    sp.wait_ge(s["stored"], 16)

                @block.scalar
                def _(act):
                    act.wait_ge(s["lgin"], 1)
                    nc.scalar.activation(LZ, LT, ACT.Exp).then_inc(s["lgexp"], 1)
                    act.wait_ge(s["lg"], 1)
                    for h in range(R_HEADS):
                        f, b = LG[:, h:h + 1], LG[:, R_HEADS + h:R_HEADS + h + 1]
                        nc.scalar.activation(DT[:, h, 1, :], TRI[:, TRI_POS, :], ACT.Exp, scale=f)
                        nc.scalar.activation(DT[:, h, 2, :], TRI[:, TRI_OFF_F, :], ACT.Exp, scale=f)
                        nc.scalar.activation(E2[:, h, :], TRI[:, TRI_NEG, :], ACT.Exp, scale=b)
                        nc.scalar.activation(DT[:, h, 0, :], TRI[:, TRI_OFF_B, :], ACT.Exp, scale=b)
                    for g in range(8):
                        ins = nc.scalar.activation(DEC[:, g, :], POS[:, 0:6], ACT.Exp, scale=LG[:, g:g + 1])
                    ins.then_inc(s["tables"], 1)
                    for n in range(2 * R_HEADS):
                        h, isk = n // 2, n % 2
                        act.wait_ge(s["transposed"], n + 1)
                        nc.scalar.activation((KTT if isk else QT)[:, h, :], PS[n % 4][:, 0:TOK], ACT.Copy,
                                             scale=1.0 if isk else scale).then_inc(s["copied"], 1)
                    for h in range(R_HEADS):
                        act.wait_ge(s["out"], h + 1)
                        hs = slice(h * R_DV, (h + 1) * R_DV)
                        nc.scalar.activation(H[:, 0, hs], PS[6][:, 0:256], ACT.Copy)
                        nc.scalar.activation(H[:, 1, hs], PS[6][:, 256:512], ACT.Copy)
                        nc.scalar.activation(H[:, 2, hs], PS[7][:, 0:256], ACT.Copy).then_inc(s["intra"], 1)
                    for b in range(4):
                        act.wait_ge(s["states"], b + 1)
                        nc.scalar.activation(ST[:, 2 * b:2 * b + 2, :], PS[2 + b].rearrange("p (g n) -> p g n", g=2),
                                             ACT.Copy).then_inc(s["statecopy"], 1)
                    act_head_root(act, s, COLS)

                @block.vector
                def _(dve):
                    clear_last_stage(dve, s)
                    c = Chain(dve, s["chain"])
                    rope(dve, c, lambda t: PRJ[:, t, 0:1024], ROPR, 8, R_DK, TMP)
                    dve.sem_inc(s["roped"], 1)
                    dve.wait_ge(s["loads"], 3 * 16)
                    c.mark(nc.vector.tensor_scalar(LS, LG, -1.0, None, ALU.mult))
                    c.sync()
                    nc.vector.tensor_tensor(LT, LG, LS, ALU.min).then_inc(s["lgin"], 1)
                    dve.wait_ge(s["lgexp"], 1)
                    c.link(nc.vector.tensor_scalar(LG, LG, 0.0, None, ALU.min))
                    W1, W2, W3 = SM[:, 80:88], SM[:, 88:96], SM[:, 96:104]
                    log1p_parts(dve, c, LZ, W1, W2, W3, None)
                    nc.vector.tensor_tensor(LG, LG, W3, ALU.subtract).then_inc(s["lg"], 1)
                    dve.wait_ge(s["tables"], 1)
                    c.mark(nc.vector.tensor_tensor(DT[:, :, 1, :], DT[:, :, 1, :], bc(TRI[:, TRI_UP, :], R_HEADS), ALU.mult))
                    c.link(nc.vector.tensor_tensor(E2, E2, bc(TRI[:, TRI_LO, :], R_HEADS), ALU.mult))
                    c.link(nc.vector.tensor_tensor(DT[:, :, 1, :], DT[:, :, 1, :], E2, ALU.add))
                    for g in range(8):
                        d, h = divmod(g, R_HEADS)
                        ins = nc.vector.tensor_scalar(KD[:, g, :], PRJ[:, 0, 512 + h * P:512 + (h + 1) * P],
                                                      DEC[:, g, POS_KF + d:POS_KF + d + 1], None, ALU.mult)
                    ins.then_inc(s["kd"], 1)

                    def mask(h):
                        dve.wait_ge(s["scores"], h + 1)
                        if h >= 2:
                            dve.wait_ge(s["out"], h - 1)
                        a = AT[:, h % 2, :]
                        nc.vector.tensor_tensor(a[:, 0:128], PS[4][:, 0:128], DT[:, h, 1, :], ALU.mult)
                        nc.vector.tensor_tensor(a[:, 128:384], PS[4][:, 128:384],
                                                DT[:, h, 1:3, :].rearrange("p a n -> p (a n)"), ALU.mult)
                        nc.vector.tensor_tensor(a[:, 384:640], PS[5][:, 0:256],
                                                DT[:, h, 0:2, :].rearrange("p a n -> p (a n)"), ALU.mult)\
                            .then_inc(s["masked"], 1)

                    mask(0)
                    for h in range(R_HEADS):
                        if h + 1 < R_HEADS:
                            mask(h + 1)
                        dve.wait_ge(s["out"], h + 1)
                        dve.wait_ge(s["intra"], h + 1)
                        hs = slice(h * R_DV, (h + 1) * R_DV)
                        for d in range(2):
                            for n, t in enumerate(LATENT):
                                col = DEC[:, d * R_HEADS + h, 2 * d + n:2 * d + n + 1]
                                ins = nc.vector.scalar_tensor_tensor(H[:, t, hs], PS[n][:, d * 256:(d + 1) * 256], col,
                                                                     H[:, t, hs], ALU.mult, ALU.add)
                                c.mark(ins)
                            c.sync()
                        dve.sem_inc(s["evacuated"], 1)
                    dve_head_norm(dve, c, s, Hf, R_DV, SQ, COLS, NWR, Zf)

                @block.tensor
                def _(pe):
                    pe.wait_ge(s["roped"], 1)
                    for n in range(2 * R_HEADS):
                        h, isk = n // 2, n % 2
                        if n >= 4:
                            pe.wait_ge(s["copied"], n - 3)
                        for t in range(TILES):
                            o = isk * 512 + h * P
                            mm = nc.tensor.transpose(PS[n % 4][:, t * P:(t + 1) * P], PRJ[:, t, o:o + P], ID)
                        mm.then_inc(s["transposed"], 1)

                    def scores(h):
                        if h == 0:
                            pe.wait_ge(s["copied"], 2 * R_HEADS)
                        else:
                            pe.wait_ge(s["masked"], h)
                        nc.tensor.matmul(PS[4][:, 0:128], KTT[:, h, 0:P], QT[:, h, 0:P], start=True, stop=True)
                        nc.tensor.matmul(PS[4][:, 128:384], KTT[:, h, P:2 * P], QT[:, h, P:TOK], start=True, stop=True)
                        nc.tensor.matmul(PS[5][:, 0:256], KTT[:, h, 2 * P:TOK], QT[:, h, P:TOK], start=True, stop=True)\
                            .then_inc(s["scores"], 1)

                    scores(0)
                    for h in range(R_HEADS):
                        pe.wait_ge(s["masked"], h + 1)
                        if h + 1 < R_HEADS:
                            scores(h + 1)
                        if h >= 1:
                            pe.wait_ge(s["evacuated"], h)
                        a = AT[:, h % 2, :]
                        v = [PRJ[:, t, 1024 + h * R_DV:1024 + (h + 1) * R_DV] for t in range(TILES)]
                        nc.tensor.matmul(PS[6][:, 0:256], a[:, 0:128], v[0], start=True, stop=True)
                        for n, t in enumerate(LATENT):
                            dst = PS[6][:, 256:512] if n == 0 else PS[7][:, 0:256]
                            nc.tensor.matmul(dst, a[:, 128 + n * P:256 + n * P], v[1], start=True, stop=False)
                            nc.tensor.matmul(dst, a[:, 384 + n * P:512 + n * P], v[2], start=False, stop=True)
                            for d in range(2):
                                mm = nc.tensor.matmul(PS[n][:, d * 256:(d + 1) * 256], QT[:, h, t * P:(t + 1) * P],
                                                      S0[:, d * R_HEADS + h, :], start=True, stop=True)
                        mm.then_inc(s["out"], 1)
                    pe.wait_ge(s["kd"], 1)
                    for g in range(8):
                        h = g % R_HEADS
                        mm = nc.tensor.matmul(PS[2 + g // 2][:, (g % 2) * 256:(g % 2) * 256 + 256], KD[:, g, :],
                                              PRJ[:, 0, 1024 + h * R_DV:1024 + (h + 1) * R_DV], start=True, stop=True)
                        if g % 2:
                            mm.then_inc(s["states"], 1)

        def stage_diff(l):
            s = signals("loads chain mean root roped transposed copied lamsum lamexp scores maxes exps"
                           " weights turned wt out ocopy stored")
            QT = UP[:, 0:3072].rearrange("p (h n) -> p h n", h=D_HEADS)
            KTT = UP[:, 3072:7168].rearrange("p (h n) -> p h n", h=D_HEADS)
            CK, CVV = UP[:, 7168:8192], UP[:, 8192:9216]
            TMP = RING[:, 0:2048]
            PP = RING[:, 2048:3584].rearrange("p (b a n) -> p b a n", b=2, a=2)
            WW = RING[:, 3584:4352].rearrange("p (b n) -> p b n", b=2)
            WT = RING[:, 4352:5120].rearrange("p (b n) -> p b n", b=2)
            SQ = RING[:, 5120:8192]
            LP = SM[:, 0:256]
            LPR = SM[:, 256:384]
            NWD = SM[:, 384:512]
            MX = SM[:, 512:560].rearrange("p (u a) -> p u a", a=2)
            SS = SM[:, 560:608].rearrange("p (u a) -> p u a", a=2)
            LSUM, NLAM = SM[:, 608:610], SM[:, 610:611]
            COLS = SM[:, 640:664]
            scale = D_HD ** -0.5
            units = [(t, h) for t in range(TILES) for h in range(D_HEADS)]
            U = len(units)

            def span(t):
                return (0, P) if t == 0 else (P, 4 * P)

            with nc.Block(no_gpsimd_drain=True) as block:
                @block.sync
                def _(sp):
                    sp.dma_start(LP, I["diff_lambda"][l].rearrange("a n -> (a n)").partition_broadcast(P)).then_inc(s["loads"], 16)
                    sp.dma_start(NWD, I["diff_norm"][l].partition_broadcast(P)).then_inc(s["loads"], 16)
                    sp.dma_start(CK, I["cache_diff_k"][0, l].rearrange("n h a d -> n (h a d)")).then_inc(s["loads"], 16)
                    sp.dma_start(CVV, I["cache_diff_v"][0, l].rearrange("n h d -> n (h d)")).then_inc(s["loads"], 16)
                    sp.dma_start(O["new_cache_diff_k"][0, l].rearrange("n h a d -> n (h a d)"), PRJ[:, 0, 1024:2048])\
                        .then_inc(s["stored"], 16)
                    sp.dma_start(O["new_cache_diff_v"][0, l].rearrange("n h d -> n (h d)"), PRJ[:, 0, 2048:3072])\
                        .then_inc(s["stored"], 16)
                    sp.wait_ge(s["stored"], 32)

                @block.scalar
                def _(act):
                    act.wait_ge(s["lamsum"], 1)
                    nc.scalar.activation(LSUM, LSUM, ACT.Exp).then_inc(s["lamexp"], 1)
                    for n in range(2 * D_HEADS):
                        h, isk = n // 2, n % 2
                        act.wait_ge(s["transposed"], n + 1)
                        w = 512 if isk else TOK
                        nc.scalar.activation((KTT if isk else QT)[:, h, :], PS[n % 4][:, 0:w], ACT.Copy).then_inc(s["copied"], 1)

                    def exps(u):
                        t, h = units[u]
                        a, b = span(t)
                        act.wait_ge(s["maxes"], u + 1)
                        if u >= 2:
                            act.wait_ge(s["weights"], u - 1)
                        for p in range(2):
                            ins = nc.scalar.activation(PP[:, u % 2, p, 0:b - a], PS[4 + 2 * (u % 2) + p][:, 0:b - a],
                                                       ACT.Exp, bias=MX[:, u, p:p + 1], scale=scale,
                                                       accum_out=SS[:, u, p:p + 1])
                        ins.then_inc(s["exps"], 1)

                    exps(0)
                    for u in range(U):
                        if u + 1 < U:
                            exps(u + 1)
                        t, h = units[u]
                        a, b = span(t)
                        act.wait_ge(s["turned"], u + 1)
                        if u >= 2:
                            act.wait_ge(s["out"], u - 1)
                        nc.scalar.activation(WT[:, u % 2, 0:b - a], PS[u % 2][:, 0:b - a], ACT.Copy).then_inc(s["wt"], 1)
                    act_head_root(act, s, COLS)

                @block.vector
                def _(dve):
                    clear_last_stage(dve, s)
                    c = Chain(dve, s["chain"])
                    dve.wait_ge(s["loads"], 4 * 16)
                    lp = LP.rearrange("p (a b n) -> p a b n", a=2, b=2)
                    c.link(nc.vector.tensor_tensor(LPR.rearrange("p (a n) -> p a n", a=2), lp[:, :, 0, :], lp[:, :, 1, :],
                                                   ALU.mult))
                    nc.vector.tensor_reduce(LSUM, LPR.rearrange("p (a n) -> p a n", a=2), AX, ALU.add).then_inc(s["lamsum"], 1)
                    rope(dve, c, lambda t: PRJ[:, t, 0:2048], ROPD, 32, D_HD, TMP)
                    dve.sem_inc(s["roped"], 1)
                    dve.wait_ge(s["lamexp"], 1)
                    c.link(nc.vector.tensor_tensor(NLAM, LSUM[:, 1:2], LSUM[:, 0:1], ALU.subtract))
                    c.link(nc.vector.tensor_tensor(NLAM, NLAM, LAMC[:, 0:1], ALU.subtract))
                    c.link(nc.vector.tensor_scalar(NWD, NWD, LAMC[:, 1:2], None, ALU.mult))

                    def maxes(u):
                        t, h = units[u]
                        a, b = span(t)
                        dve.wait_ge(s["scores"], u + 1)
                        for p in range(2):
                            c.mark(nc.vector.tensor_reduce(MX[:, u, p:p + 1], PS[4 + 2 * (u % 2) + p][:, 0:b - a], AX, ALU.max))
                        c.sync()
                        nc.vector.tensor_scalar(MX[:, u, :], MX[:, u, :], -scale, None, ALU.mult).then_inc(s["maxes"], 1)

                    def ocopy(u):
                        t, h = units[u]
                        dve.wait_ge(s["out"], u + 1)
                        nc.vector.tensor_copy(H[:, t, h * P:(h + 1) * P], PS[2 + u % 2][:, 0:P]).then_inc(s["ocopy"], 1)

                    maxes(0)
                    for u in range(U):
                        if u + 1 < U:
                            maxes(u + 1)
                        t, h = units[u]
                        a, b = span(t)
                        dve.wait_ge(s["exps"], u + 1)
                        c.link(nc.vector.reciprocal(SS[:, u, :], SS[:, u, :]))
                        c.link(nc.vector.tensor_tensor(SS[:, u, 1:2], SS[:, u, 1:2], NLAM, ALU.mult))
                        pp = PP[:, u % 2]
                        c.link(nc.vector.tensor_scalar(pp[:, 1, 0:b - a], pp[:, 1, 0:b - a], SS[:, u, 1:2], None, ALU.mult))
                        if u >= 2:
                            dve.wait_ge(s["turned"], u - 1)
                        nc.vector.scalar_tensor_tensor(WW[:, u % 2, 0:b - a], pp[:, 0, 0:b - a], SS[:, u, 0:1],
                                                       pp[:, 1, 0:b - a], ALU.mult, ALU.add).then_inc(s["weights"], 1)
                        if u >= 1:
                            ocopy(u - 1)
                    ocopy(U - 1)
                    dve.wait_ge(s["ocopy"], U)
                    dve_head_norm(dve, c, s, Hf, 2 * D_HD, SQ, COLS, NWD, None)

                @block.tensor
                def _(pe):
                    pe.wait_ge(s["roped"], 1)
                    for n in range(2 * D_HEADS):
                        h, isk = n // 2, n % 2
                        if n >= 4:
                            pe.wait_ge(s["copied"], n - 3)
                        for t in range(TILES + isk):
                            o = isk * 1024 + h * P
                            src = PRJ[:, t, o:o + P] if t < TILES else CK[:, h * P:(h + 1) * P]
                            mm = nc.tensor.transpose(PS[n % 4][:, t * P:(t + 1) * P], src, ID)
                        mm.then_inc(s["transposed"], 1)
                    pe.wait_ge(s["copied"], 2 * D_HEADS)

                    def scores(u):
                        t, h = units[u]
                        a, b = span(t)
                        if u >= 2:
                            pe.wait_ge(s["exps"], u - 1)
                        for p in range(2):
                            hp = slice(p * D_HD, (p + 1) * D_HD)
                            mm = nc.tensor.matmul(PS[4 + 2 * (u % 2) + p][:, 0:b - a], QT[hp, h, t * P:(t + 1) * P],
                                                  KTT[hp, h, a:b], start=True, stop=True)
                        mm.then_inc(s["scores"], 1)

                    def turn(u):
                        t, h = units[u]
                        a, b = span(t)
                        pe.wait_ge(s["weights"], u + 1)
                        if u >= 2:
                            pe.wait_ge(s["wt"], u - 1)
                        for n in range((b - a) // P):
                            mm = nc.tensor.transpose(PS[u % 2][:, n * P:(n + 1) * P], WW[:, u % 2, n * P:(n + 1) * P], ID)
                        mm.then_inc(s["turned"], 1)

                    def values(u):
                        t, h = units[u]
                        a, b = span(t)
                        pe.wait_ge(s["wt"], u + 1)
                        if u >= 2:
                            pe.wait_ge(s["ocopy"], u - 1)
                        n = (b - a) // P
                        for k in range(n):
                            tt = a // P + k
                            v = (PRJ[:, tt, 2048 + h * P:2048 + (h + 1) * P] if tt < TILES else CVV[:, h * P:(h + 1) * P])
                            mm = nc.tensor.matmul(PS[2 + u % 2][:, 0:P], WT[:, u % 2, k * P:(k + 1) * P], v,
                                                  start=(k == 0), stop=(k == n - 1))
                        mm.then_inc(s["out"], 1)

                    scores(0)
                    for u in range(U):
                        if u + 1 < U:
                            scores(u + 1)
                        turn(u)
                        if u >= 1:
                            values(u - 1)
                    values(U - 1)

        TMK = UP.rearrange("p (t n) -> p t n", t=TILES)
        YC = BIG[:, 0:QBLK * TOK].rearrange("p (b n) -> p b n", b=QBLK)
        KQT = BIG[:, 0:16 * TOK].rearrange("p (b n) -> p b n", b=16)
        AB = SM[:, 512:608].rearrange("p (t n) -> p t n", t=TILES)

        def stage_gdn_project(l):
            s = signals("free loaded0 loaded1 banks_free done small taps tapcopy filled conv silu zdone zfree"
                           " abload abdone chain pads cbfree")
            loaded = [s["loaded0"], s["loaded1"]]
            XC = UP[:, 0:8 * XC_W].rearrange("p (b n) -> p b n", b=8)
            CB = UP[:, 3200:3200 + 8 * CV_W].rearrange("p (b n) -> p b n", b=8)
            WC = UP[:, 6400:6656]
            TW = UP[:, 6656:6912].rearrange("p (b n) -> p b n", b=2)
            WAB = UP[:, 6912:7168].rearrange("p (k n) -> p k n", k=KT)
            rows = CONV_K * QBLK
            chunks = G_QKV // CHUNK
            zchunks = G_HEADS * G_DV // CHUNK
            taps = I["gdn_conv"].rearrange("l t (b c) -> l (t b) c", c=P)
            with nc.Block(no_gpsimd_drain=True) as block:
                @block.sync
                def _(sp):
                    sp.wait_ge(s["pads"], 1)
                    sp.dma_start(TW[:, 0, :], taps[l, 0:P, :]).then_inc(s["small"], 16)
                    sp.dma_start(TW[0:rows - P, 1, :], taps[l, P:rows, :]).then_inc(s["small"], 16)
                    sp.dma_start(WAB, w_in[l, :, :, COL_GDN_AB:COL_GDN_AB + 32]).then_inc(s["abload"], 16)
                    sp_weights(sp, lambda n: w_in[l, :, :, ds(n * CHUNK + COL_GDN, CHUNK)], chunks, 0, s["free"], loaded)
                    sp_weights(sp, lambda n: w_in[l, :, :, ds(n * CHUNK + COL_GDN_Z, CHUNK)], zchunks, chunks, s["free"], loaded)

                @block.gpsimd
                def _(pool):
                    nc.gpsimd.memset(XC, 0.0)
                    nc.gpsimd.memset(TW, 0.0).then_inc(s["pads"], 1)

                @block.tensor
                def _(pe):
                    pe.sem_inc(s["free"], 2)
                    pe.wait_ge(s["small"], 32)
                    for b in range(2):
                        mm = nc.tensor.transpose(PS[7][:, b * P:(b + 1) * P], TW[:, b, :], ID)
                    mm.then_inc(s["taps"], 1)
                    pe.wait_ge(s["tapcopy"], 1)
                    with pe.Fori(0, chunks // 2) as i:
                        for j in range(2):
                            pe.wait_ge(loaded[j], 16 + 16 * i)
                            for b in range(4):
                                pe.wait_ge(s["banks_free"], 8 * i + 4 * j + b + 1)
                                for k in range(KT):
                                    mm = nc.tensor.matmul(PS[4 * j + b][:, 0:TOK], RW[:, j, k, b * P:(b + 1) * P], HT[:, k, :],
                                                          start=(k == 0), stop=(k == KT - 1))
                                mm.then_inc(s["done"], 1)
                            pe.drain().then_inc(s["free"], 1)
                    pe.wait_ge(s["filled"], 4 * chunks)
                    pe_project(pe, (HT, HT), zchunks, chunks, s["free"], loaded, s["zfree"], s["zdone"])
                    pe.wait_ge(s["abload"], 16)
                    for t in range(TILES):
                        for k in range(KT):
                            mm = nc.tensor.matmul(PS[6][:, t * 32:(t + 1) * 32], HT[:, k, t * P:(t + 1) * P], WAB[:, k, :],
                                                  start=(k == 0), stop=(k == KT - 1))
                    mm.then_inc(s["abdone"], 1)

                @block.scalar
                def _(act):
                    act.sem_inc(s["banks_free"], 8)
                    act.sem_inc(s["silu"], 8)
                    act.sem_inc(s["zfree"], chunks + 2)
                    act.wait_ge(s["taps"], 1)
                    nc.scalar.activation(WC, PS[7][:, 0:2 * P], ACT.Copy).then_inc(s["tapcopy"], 1)
                    with act.Fori(0, chunks // 2) as i:
                        for j in range(2):
                            for b in range(4):
                                n = 4 * j + b
                                act.wait_ge(s["done"], 8 * i + n + 1)
                                act.wait_ge(s["cbfree"], 8 * i + n + 1)
                                nc.scalar.activation(XC[:, n, XC_P:XC_P + SEQ], PS[n][:, 0:SEQ], ACT.Copy)
                                nc.scalar.activation(XC[:, n, XC_S:XC_S + DEC_SEQ], PS[n][:, SEQ:TOK], ACT.Copy)\
                                    .then_inc(s["filled"], 1)
                                act.drain().then_inc(s["banks_free"], 1)
                            for b in range(4):
                                n = 4 * j + b
                                act.wait_ge(s["conv"], 8 * i + n + 1)
                                blk = 8 * i + n
                                nc.scalar.activation(YC[:, blk, 0:SEQ], CB[:, n, 0:SEQ], ACT.Silu)
                                nc.scalar.activation(YC[:, blk, SEQ:TOK], CB[:, n, CV_S:CV_S + DEC_SEQ], ACT.Silu)\
                                    .then_inc(s["silu"], 1)
                    for j in range(zchunks):
                        for t in range(TILES):
                            act.wait_ge(s["zdone"], 3 * j + t + 1)
                            nc.scalar.activation(Z[:, t, j * CHUNK:(j + 1) * CHUNK], PS[3 * j + t], ACT.Silu)
                    act.wait_ge(s["abdone"], 1)
                    nc.scalar.activation(AB, PS[6][:, 0:TILES * 32].rearrange("p (t n) -> p t n", t=TILES), ACT.Copy)

                @block.vector
                def _(dve):
                    clear_last_stage(dve, s)
                    dve.sem_inc(s["cbfree"], 8)
                    c = Chain(dve, s["chain"])
                    dve.wait_ge(s["tapcopy"], 1)
                    with dve.Fori(0, chunks // 2) as i:
                        c.enter(i, 8 * CONV_K)
                        for n in range(8):
                            dve.wait_ge(s["filled"], 8 * i + n + 1)
                            dve.wait_ge(s["silu"], 8 * i + n + 1)
                            for tap in range(CONV_K):
                                w = WC[:, ds(8 * i + n + tap * QBLK, 1)]
                                x = XC[:, n, tap:tap + CV_W]
                                if tap == 0:
                                    ins = nc.vector.tensor_scalar(CB[:, n, :], x, w, None, ALU.mult)
                                else:
                                    ins = nc.vector.scalar_tensor_tensor(CB[:, n, :], x, w, CB[:, n, :], ALU.mult, ALU.add)
                                c.link(ins)
                            dve.sem_inc(s["conv"], 1)
                            dve.sem_inc(s["cbfree"], 1)
                        c.leave(chunks // 2)

        GLG = SM[:, 0:48].rearrange("p (t n) -> p t n", t=TILES)
        BTA = SM[:, 48:96].rearrange("p (t n) -> p t n", t=TILES)
        GC = SM[:, 96:144].rearrange("p (t n) -> p t n", t=TILES)
        EG = SM[:, 144:192].rearrange("p (t n) -> p t n", t=TILES)
        NEGG = SM[:, 192:240].rearrange("p (t n) -> p t n", t=TILES)
        EKD = SM[:, 240:288].rearrange("p (t n) -> p t n", t=TILES)
        EGL = SM[:, 288:336].rearrange("p (t n) -> p t n", t=TILES)

        def stage_gdn_prepare(l):
            s = signals("loads chain turned copied squares root normed back backcopy aexp spin spexp glog sums"
                           " exponents exps beta")
            SQ = RING[:, 0:2048]
            AL, DTB = SM[:, 336:352], SM[:, 352:368]
            T1, T2, T3, T4 = [RING[:, 2048 + 48 * n:2096 + 48 * n].rearrange("p (t n) -> p t n", t=TILES) for n in range(4)]
            T5 = RING[:, 2240:2288].rearrange("p (t n) -> p t n", t=TILES)
            T6 = RING[:, 2288:2336].rearrange("p (t n) -> p t n", t=TILES)
            RN = SM[:, 640:688].rearrange("p (t n) -> p t n", t=TILES)
            with nc.Block(no_gpsimd_drain=True) as block:
                @block.sync
                def _(sp):
                    sp.dma_start(AL, I["gdn_A_log"][l].rearrange("d h -> (d h)").partition_broadcast(P)).then_inc(s["loads"], 16)
                    sp.dma_start(DTB, I["gdn_dt_bias"][l].rearrange("d h -> (d h)").partition_broadcast(P)).then_inc(s["loads"], 16)
                    for d in range(2):
                        sp.dma_start(SST[:, d * G_HEADS:(d + 1) * G_HEADS, :],
                                     I["state_gdn"][0, l, d].rearrange("h k v -> k h v")).then_inc(s["loads"], 16)

                @block.tensor
                def _(pe):
                    for t in range(TILES):
                        for b in range(QBLK // 4):
                            n = t * (QBLK // 4) + b
                            if n >= 4:
                                pe.wait_ge(s["copied"], n - 3)
                            for k in range(4):
                                mm = nc.tensor.transpose(PS[n % 4][:, k * P:(k + 1) * P], YC[:, 4 * b + k, t * P:(t + 1) * P], ID)
                            mm.then_inc(s["turned"], 1)
                    pe.wait_ge(s["glog"], 1)
                    for t in range(TILES):
                        for d in range(2):
                            nc.tensor.matmul(PS[6][:, t * 16 + d * 8:t * 16 + d * 8 + 8], TRI[:, TRI_LO if d else TRI_UP, :],
                                             GLG[:, t, d * 8:d * 8 + 8], start=True, stop=True)
                        mm = nc.tensor.matmul(PS[7][:, t * 16:t * 16 + 16], TRI[:, TRI_ONE, :], GLG[:, t, :], start=True, stop=True)
                    mm.then_inc(s["sums"], 1)
                    pe.wait_ge(s["copied"], TILES * QBLK // 4)
                    for t in range(TILES):
                        pe.wait_ge(s["normed"], t + 1)
                        for b in range(4):
                            n = 4 * t + b
                            if n >= 4:
                                pe.wait_ge(s["backcopy"], n - 3)
                            for k in range(4):
                                g = 4 * b + k
                                mm = nc.tensor.transpose(PS[n % 4][:, k * P:(k + 1) * P], TMK[:, t, g * P:(g + 1) * P], ID)
                            mm.then_inc(s["back"], 1)

                @block.scalar
                def _(act):
                    act.wait_ge(s["loads"], 4 * 16)
                    nc.scalar.activation(AL, AL, ACT.Exp).then_inc(s["aexp"], 1)
                    act.wait_ge(s["spin"], 1)
                    nc.scalar.activation(T2, T2, ACT.Exp).then_inc(s["spexp"], 1)
                    nc.scalar.activation(BTA, AB[:, :, 16:32], ACT.Sigmoid).then_inc(s["beta"], 1)
                    for t in range(TILES):
                        for b in range(QBLK // 4):
                            n = t * (QBLK // 4) + b
                            act.wait_ge(s["turned"], n + 1)
                            nc.scalar.activation(TMK[:, t, 4 * b * P:4 * (b + 1) * P], PS[n % 4], ACT.Copy).then_inc(s["copied"], 1)
                    act.wait_ge(s["squares"], TILES)
                    nc.scalar.activation(RN, RN, ACT.Sqrt).then_inc(s["root"], 1)
                    for n in range(4 * TILES):
                        t, b = divmod(n, 4)
                        act.wait_ge(s["back"], n + 1)
                        nc.scalar.activation(KQT[:, 4 * b:4 * b + 4, t * P:(t + 1) * P],
                                             PS[n % 4].rearrange("p (k n) -> p k n", k=4), ACT.Copy).then_inc(s["backcopy"], 1)
                    act.wait_ge(s["exponents"], 1)
                    nc.scalar.activation(EG, EG, ACT.Exp)
                    nc.scalar.activation(EKD, EKD, ACT.Exp)
                    nc.scalar.activation(EGL, EGL, ACT.Exp).then_inc(s["exps"], 1)

                @block.vector
                def _(dve):
                    clear_last_stage(dve, s)
                    c = Chain(dve, s["chain"])
                    dve.wait_ge(s["loads"], 4 * 16)
                    c.link(nc.vector.tensor_tensor(T1, AB[:, :, 0:16], bc(DTB, TILES), ALU.add))
                    c.link(nc.vector.tensor_scalar(T2, T1, -1.0, None, ALU.mult))
                    nc.vector.tensor_tensor(T2, T1, T2, ALU.min).then_inc(s["spin"], 1)
                    dve.wait_ge(s["spexp"], 1)
                    log1p_parts(dve, c, T2, T3, T4, T5, None)
                    c.link(nc.vector.scalar_tensor_tensor(T1, T1, 0.0, T5, ALU.max, ALU.add))
                    dve.wait_ge(s["aexp"], 1)
                    c.link(nc.vector.tensor_scalar(AL, AL, -1.0, None, ALU.mult))
                    nc.vector.tensor_tensor(GLG, T1, bc(AL, TILES), ALU.mult).then_inc(s["glog"], 1)
                    for t in range(TILES):
                        dve.wait_ge(s["copied"], (t + 1) * QBLK // 4)
                        qk = TMK[:, t, 0:2048]
                        c.link(nc.vector.tensor_tensor(SQ, qk, qk, ALU.mult))
                        c.link(nc.vector.tensor_reduce(RN[:, t, :], SQ.rearrange("p (g n) -> p g n", n=P), AX, ALU.add))
                        nc.vector.tensor_scalar(RN[:, t, :], RN[:, t, :], EPS, None, ALU.add).then_inc(s["squares"], 1)
                    dve.wait_ge(s["root"], 1)
                    c.link(nc.vector.reciprocal(RN, RN))
                    c.link(nc.vector.tensor_scalar(RN[:, :, 0:8], RN[:, :, 0:8], G_DK ** -0.5, None, ALU.mult))
                    for t in range(TILES):
                        qk = TMK[:, t, 0:2048].rearrange("p (g n) -> p g n", n=P)
                        nc.vector.tensor_tensor(qk, qk, bl(RN[:, t, :], P), ALU.mult).then_inc(s["normed"], 1)
                    dve.wait_ge(s["sums"], 1)
                    c.link(nc.vector.tensor_copy(GC, PS[6][:, 0:48].rearrange("p (t n) -> p t n", t=TILES)))
                    c.link(nc.vector.tensor_copy(EGL, PS[7][:, 0:48].rearrange("p (t n) -> p t n", t=TILES)))
                    c.mark(nc.vector.tensor_copy(EG, GC))
                    c.link(nc.vector.tensor_tensor(EKD, EGL, GC, ALU.subtract))
                    dve.sem_inc(s["exponents"], 1)
                    dve.wait_ge(s["exps"], 1)
                    c.link(nc.vector.tensor_scalar(NEGG, EG, -1.0, None, ALU.mult))

        GUNITS = [(0, 0), (0, 1), (1, 0), (2, 1), (2, 0), (1, 1)]

        def stage_gdn(l):
            s = signals("nload chain mean root mg gb dec gram pair qd lv xdone xcopy ydone updated"
                           " ks r un u out kd snew state supd stored pchain tail")
            FB = [[RING[:, (6 * hg + n) * 512:(6 * hg + n + 1) * 512].rearrange("p (h n) -> p h n", h=4) for n in range(6)]
                  for hg in range(2)]
            SQ = RING[:, 0:3072]
            NWG = SM[:, 384:512]
            COLS = SM[:, 688:712]

            def bank(n):
                return PS[n].rearrange("p (h n) -> p h n", h=4)

            U = len(GUNITS)

            def latent(v):
                return GUNITS[v][0] > 0

            def ug(v, hg):
                return 2 * v + hg

            def lev(v, n, hg):
                return v * 2 * LEVELS + 2 * n + hg + 1

            first = {}
            for v, (t, d) in enumerate(GUNITS):
                first.setdefault(t, v)

            with nc.Block(no_gpsimd_drain=True) as block:
                @block.sync
                def _(sp):
                    sp.dma_start(NWG, I["gdn_norm"][l].partition_broadcast(P)).then_inc(s["nload"], 16)
                    for v in range(2):
                        t, d = GUNITS[v]
                        sp.wait_ge(s["snew"], 2 * v + 2)
                        src = ZST[v]
                        sp.dma_start(O["new_state_gdn"][0, l, d].rearrange("h k v -> k h v"), src).then_inc(s["stored"], 16)
                    sp.wait_ge(s["stored"], 32)

                @block.gpsimd
                def _(pool):
                    for v, (t, d) in enumerate(GUNITS):
                        for hg in range(2):
                            MT, QD, MO, XS, T, TT = FB[hg]
                            if v:
                                pool.wait_ge(s["tail"], ug(v - 1, hg) + 1)
                            tri = TRI[:, TRI_LO if d else TRI_UP, :]
                            for h in range(4):
                                col = GLG[:, t, d * 8 + hg * 4 + h:d * 8 + hg * 4 + h + 1]
                                ins = nc.gpsimd.tensor_scalar(MO[:, h, :], tri, col, None, ALU.mult)
                            ins.then_inc(s["mg"], 1)
                        for n in range(LEVELS):
                            for hg in range(2):
                                MT, QD, MO, XS, T, TT = FB[hg]
                                if n == 0:
                                    pool.wait_ge(s["pair"], ug(v, hg) + 1)
                                else:
                                    pool.wait_ge(s["xdone"], lev(v, n - 1, hg))
                                if n == 1:
                                    pool.wait_ge(s["updated"], lev(v, 0, hg))
                                nc.gpsimd.tensor_tensor(MO, MT, bc(LVL[:, d, n, :], 4), ALU.mult).then_inc(s["lv"], 1)

                @block.tensor
                def _(pe):
                    for v, (t, d) in enumerate(GUNITS):
                        ts_ = slice(t * P, (t + 1) * P)
                        for hg in range(2):
                            MT, QD, MO, XS, T, TT = FB[hg]
                            pe.wait_ge(s["mg"], ug(v, hg) + 1)
                            if v:
                                pe.wait_ge(s["tail"], ug(v - 1, hg) + 1)
                            nc.tensor.matmul(PS[6 + hg], TRI[:, TRI_ONE, :], MO.rearrange("p h n -> p (h n)"),
                                             start=True, stop=True).then_inc(s["gb"], 1)
                            for h in range(4):
                                hh = hg * 4 + h
                                k = KQT[:, 8 + hh, ts_]
                                nc.tensor.matmul(PS[hg][:, h * P:(h + 1) * P], k, k, start=True, stop=True)
                                mm = nc.tensor.matmul(PS[2 + hg][:, h * P:(h + 1) * P], k, KQT[:, hh, ts_], start=True, stop=True)
                            mm.then_inc(s["gram"], 1)
                        for n in range(LEVELS):
                            for hg in range(2):
                                MT, QD, MO, XS, T, TT = FB[hg]
                                pe.wait_ge(s["lv"], lev(v, n, hg))
                                if n:
                                    pe.wait_ge(s["updated"], lev(v, n - 1, hg))
                                for h in range(4):
                                    dst = PS[hg][:, h * P:(h + 1) * P]
                                    if n == 0:
                                        mm = nc.tensor.transpose(dst, MO[:, h, :], ID)
                                    else:
                                        mm = nc.tensor.matmul(dst, MO[:, h, :], T[:, h, :], start=True, stop=True)
                                mm.then_inc(s["xdone"], 1)
                            if n:
                                for hg in range(2):
                                    MT, QD, MO, XS, T, TT = FB[hg]
                                    pe.wait_ge(s["xcopy"], v * 2 * (LEVELS - 1) + 2 * (n - 1) + hg + 1)
                                    for h in range(4):
                                        if n < LEVELS - 1:
                                            nc.tensor.matmul(PS[2 + hg][:, h * P:(h + 1) * P], TT[:, h, :], XS[:, h, :],
                                                             start=True, stop=True)
                                        mm = nc.tensor.matmul(PS[4 + hg][:, h * P:(h + 1) * P], XS[:, h, :], TT[:, h, :],
                                                              start=True, stop=True)
                                    mm.then_inc(s["ydone"], 1)
                        if latent(v):
                            for hg in range(2):
                                pe.wait_ge(s["updated"], lev(v, LEVELS - 1, hg))
                                if v >= 4:
                                    pe.wait_ge(s["state"], ug(v - 4, hg) + 1)
                                for h in range(4):
                                    hh = hg * 4 + h
                                    mm = nc.tensor.matmul(PS[hg][:, h * P:(h + 1) * P], KQT[:, 8 + hh, ts_],
                                                          SST[:, d * 8 + hh, :], start=True, stop=True)
                                mm.then_inc(s["ks"], 1)
                        for hg in range(2):
                            MT, QD, MO, XS, T, TT = FB[hg]
                            pe.wait_ge(s["updated"], lev(v, LEVELS - 1, hg))
                            pe.wait_ge(s["r"], ug(v, hg) + 1)
                            for h in range(4):
                                mm = nc.tensor.matmul(PS[2 + hg][:, h * P:(h + 1) * P], TT[:, h, :], MO[:, h, :],
                                                      start=True, stop=True)
                            mm.then_inc(s["un"], 1)
                        for hg in range(2):
                            MT, QD, MO, XS, T, TT = FB[hg]
                            pe.wait_ge(s["u"], ug(v, hg) + 1)
                            for h in range(4):
                                hh = hg * 4 + h
                                mm = nc.tensor.matmul(PS[4 + hg][:, h * P:(h + 1) * P], QD[:, h, :], XS[:, h, :],
                                                      start=True, stop=True)
                                if latent(v):
                                    mm = nc.tensor.matmul(PS[6 + hg][:, h * P:(h + 1) * P], KQT[:, hh, ts_],
                                                          SST[:, d * 8 + hh, :], start=True, stop=True)
                            mm.then_inc(s["out"], 1)
                            pe.wait_ge(s["kd"], ug(v, hg) + 1)
                            for h in range(4):
                                mm = nc.tensor.matmul(PS[hg][:, h * P:(h + 1) * P], T[:, h, :], XS[:, h, :],
                                                      start=True, stop=True)
                            mm.then_inc(s["supd"], 1)

                @block.scalar
                def _(act):
                    for v, (t, d) in enumerate(GUNITS):
                        for hg in range(2):
                            MT, QD, MO, XS, T, TT = FB[hg]
                            act.wait_ge(s["dec"], ug(v, hg) + 1)
                            nc.scalar.activation(XS, XS, ACT.Exp).then_inc(s["qd"], 1)
                        for n in range(1, LEVELS):
                            for hg in range(2):
                                MT, QD, MO, XS, T, TT = FB[hg]
                                act.wait_ge(s["xdone"], lev(v, n, hg))
                                if n == 1:
                                    act.wait_ge(s["pair"], ug(v, hg) + 1)
                                nc.scalar.activation(XS, bank(hg), ACT.Copy).then_inc(s["xcopy"], 1)
                        if t == 0:
                            for hg in range(2):
                                act.wait_ge(s["supd"], ug(v, hg) + 1)
                                nc.scalar.activation(ZST[v][:, hg * 4:hg * 4 + 4, :], bank(hg), ACT.Copy).then_inc(s["snew"], 1)
                    act_head_root(act, s, COLS)

                @block.vector
                def _(dve):
                    clear_last_stage(dve, s)
                    c = Chain(dve, s["chain"])
                    for v, (t, d) in enumerate(GUNITS):
                        idb = bc(ID, 4)
                        incl = bc(TRI[:, TRI_LO if d else TRI_UP, :], 4)
                        for hg in range(2):
                            MT, QD, MO, XS, T, TT = FB[hg]
                            dve.wait_ge(s["gb"], ug(v, hg) + 1)
                            for h in range(4):
                                g = d * 8 + hg * 4 + h
                                ins = nc.vector.tensor_scalar(XS[:, h, :], bank(6 + hg)[:, h, :], GC[:, t, g:g + 1], 0.0,
                                                              ALU.subtract, ALU.min)
                            ins.then_inc(s["dec"], 1)
                        for hg in range(2):
                            MT, QD, MO, XS, T, TT = FB[hg]
                            dve.wait_ge(s["qd"], ug(v, hg) + 1)
                            dve.wait_ge(s["gram"], ug(v, hg) + 1)
                            c.link(nc.vector.tensor_tensor(QD, XS, incl, ALU.mult))
                            b4 = bl(BTA[:, t, d * 8 + hg * 4:d * 8 + hg * 4 + 4], P)
                            c.mark(nc.vector.tensor_tensor(MT, QD, bank(hg), ALU.mult))
                            c.link(nc.vector.tensor_tensor(QD, QD, bank(2 + hg), ALU.mult))
                            nc.vector.tensor_tensor(MT, MT, b4, ALU.mult).then_inc(s["pair"], 1)
                        for n in range(LEVELS):
                            for hg in range(2):
                                MT, QD, MO, XS, T, TT = FB[hg]
                                if n == 0:
                                    dve.wait_ge(s["xdone"], lev(v, 0, hg))
                                    nc.vector.tensor_tensor(TT, idb, MO, ALU.subtract)
                                    nc.vector.tensor_tensor(T, idb, bank(hg), ALU.subtract).then_inc(s["updated"], 1)
                                else:
                                    dve.wait_ge(s["ydone"], v * 2 * (LEVELS - 1) + 2 * (n - 1) + hg + 1)
                                    if n < LEVELS - 1:
                                        nc.vector.tensor_tensor(T, T, bank(2 + hg), ALU.subtract)
                                    nc.vector.tensor_tensor(TT, TT, bank(4 + hg), ALU.subtract).then_inc(s["updated"], 1)
                        for hg in range(2):
                            MT, QD, MO, XS, T, TT = FB[hg]
                            vv = TMK[:, t, 2048 + hg * 512:2048 + hg * 512 + 512].rearrange("p (h n) -> p h n", h=4)
                            gs = slice(d * 8 + hg * 4, d * 8 + hg * 4 + 4)
                            dve.wait_ge(s["xdone"], lev(v, LEVELS - 1, hg))
                            if latent(v):
                                dve.wait_ge(s["ks"], ug(v - 2, hg) + 1)
                                c.link(nc.vector.tensor_tensor(MO, bank(hg), bl(EG[:, t, gs], P), ALU.mult))
                                nc.vector.tensor_tensor(MO, vv, MO, ALU.subtract).then_inc(s["r"], 1)
                            else:
                                nc.vector.tensor_copy(MO, vv).then_inc(s["r"], 1)
                            kk = TMK[:, t, 1024 + hg * 512:1024 + hg * 512 + 512].rearrange("p (h n) -> p h n", h=4)
                            dve.wait_ge(s["un"], ug(v, hg) + 1)
                            nc.vector.tensor_tensor(XS, bank(2 + hg), bl(BTA[:, t, gs], P), ALU.mult).then_inc(s["u"], 1)
                            nc.vector.tensor_tensor(T, kk, bl(EKD[:, t, gs], P), ALU.mult).then_inc(s["kd"], 1)
                        for hg in range(2):
                            MT, QD, MO, XS, T, TT = FB[hg]
                            gs = slice(d * 8 + hg * 4, d * 8 + hg * 4 + 4)
                            oo = H[:, t, hg * 512:hg * 512 + 512].rearrange("p (h n) -> p h n", h=4)
                            dve.wait_ge(s["out"], ug(v, hg) + 1)
                            if first[t] == v:
                                c.link(nc.vector.tensor_copy(oo, bank(4 + hg)))
                            else:
                                c.link(nc.vector.tensor_tensor(oo, oo, bank(4 + hg), ALU.add))
                            if latent(v):
                                c.link(nc.vector.tensor_tensor(MO, bank(6 + hg), bl(EG[:, t, gs], P), ALU.mult))
                                c.link(nc.vector.tensor_tensor(oo, oo, MO, ALU.add))
                                dve.wait_ge(s["supd"], ug(v, hg) + 1)
                                st = SST[:, d * 8 + hg * 4:d * 8 + hg * 4 + 4, :]
                                c.link(nc.vector.tensor_tensor(st, st, bl(EGL[:, t, gs], P), ALU.mult))
                                nc.vector.tensor_tensor(st, st, bank(hg), ALU.add).then_inc(s["state"], 1)
                                dve.wait_ge(s["state"], ug(v - 2, hg) + 1)
                            else:
                                dve.wait_ge(s["snew"], ug(v, hg) + 1)
                            dve.sem_inc(s["tail"], 1)
                    dve.wait_ge(s["nload"], 16)
                    dve_head_norm(dve, c, s, Hf, G_DV, SQ, COLS, NWG, Zf)

        def stage_merge(l, n_branch):
            s = signals("free loaded0 loaded1 banks_free done turned free2 ready gate used chain")
            loaded = [s["loaded0"], s["loaded1"]]
            GT = BIG[:, 0:TILES * CHUNK].rearrange("p (t n) -> p t n", t=TILES)
            TM = BIG[:, 1536:3072].rearrange("p (t n) -> p t n", t=TILES)
            wb = I["w_branch"].rearrange("l b (k p) n -> l b p k n", p=P)
            chunks = D // CHUNK
            col = COL_GATES + n_branch * D
            with nc.Block(no_gpsimd_drain=True) as block:
                @block.sync
                def _(sp):
                    with sp.Fori(0, chunks) as i:
                        sp.wait_ge(s["free"], 2 * i + 1)
                        sp.dma_start(RW[:, 0], w_in[l, :, :, ds(i * CHUNK + col, CHUNK)]).then_inc(loaded[0], 16)
                        sp.wait_ge(s["free"], 2 * i + 2)
                        sp.dma_start(RW[:, 1], wb[l, n_branch, :, :, ds(i * CHUNK, CHUNK)]).then_inc(loaded[1], 16)

                @block.tensor
                def _(pe):
                    pe.sem_inc(s["free"], 2)
                    pe_transpose_tokens(pe, H, s["ready"], s["free2"], s["turned"])
                    pe.wait_ge(s["free2"], 2 * TILES)
                    pe_project(pe, (HT, OT_), 2 * chunks, 0, s["free"], loaded, s["banks_free"], s["done"])

                @block.scalar
                def _(act):
                    act_transposed(act, OT_, s["turned"], s["free2"])
                    with act.Fori(0, chunks) as i:
                        act.wait_ge(s["used"], i + 1)
                        for t in range(TILES):
                            act.wait_ge(s["done"], 6 * i + t + 1)
                            nc.scalar.activation(GT[:, t, :], PS[t], ACT.Sigmoid).then_inc(s["gate"], 1)

                @block.vector
                def _(dve):
                    clear_last_stage(dve, s)
                    c = Chain(dve, s["chain"])
                    dve.sem_inc(s["ready"], TILES)
                    dve.sem_inc(s["banks_free"], 2)
                    dve.sem_inc(s["used"], 1)
                    with dve.Fori(0, chunks) as i:
                        c.enter(i, TILES if n_branch == 0 else 2 * TILES)
                        dve.wait_ge(s["gate"], 3 * i + 3)
                        dve.wait_ge(s["done"], 6 * i + 6)
                        for t in range(TILES):
                            dst = MACC[:, t, ds(i * CHUNK, CHUNK)]
                            if n_branch == 0:
                                c.mark(nc.vector.tensor_tensor(dst, GT[:, t, :], PS[3 + t], ALU.mult))
                            else:
                                c.link(nc.vector.tensor_tensor(TM[:, t, :], GT[:, t, :], PS[3 + t], ALU.mult))
                                c.mark(nc.vector.tensor_tensor(dst, dst, TM[:, t, :], ALU.add))
                        c.sync()
                        dve.sem_inc(s["banks_free"], 2)
                        dve.sem_inc(s["used"], 1)
                        c.leave(chunks)

        def stage_out(l):
            s = signals("free loaded0 loaded1 banks_free done turned free2 ready loads chain")
            loaded = [s["loaded0"], s["loaded1"]]
            G1 = BIG[:, 0:2 * D].rearrange("p (g n) -> p g n", g=2)
            TM = BIG[:, 2 * D:2 * D + 1536].rearrange("p (t n) -> p t n", t=TILES)
            wo = I["w_out"].rearrange("l (k p) n -> l p k n", p=P)
            chunks = D // CHUNK
            with nc.Block(no_gpsimd_drain=True) as block:
                @block.sync
                def _(sp):
                    for g in range(2):
                        sp.dma_start(G1[:, g, :], modd[g, 2 * D:3 * D].partition_broadcast(P)).then_inc(s["loads"], 16)
                    sp_weights(sp, lambda n: wo[l, :, :, ds(n * CHUNK, CHUNK)], chunks, 0, s["free"], loaded)

                @block.tensor
                def _(pe):
                    pe.sem_inc(s["free"], 2)
                    pe_transpose_tokens(pe, MACC, s["ready"], s["free2"], s["turned"])
                    pe.wait_ge(s["free2"], 2 * TILES)
                    pe_project(pe, (OT_, OT_), chunks, 0, s["free"], loaded, s["banks_free"], s["done"])

                @block.scalar
                def _(act):
                    act_transposed(act, OT_, s["turned"], s["free2"])

                @block.vector
                def _(dve):
                    clear_last_stage(dve, s)
                    c = Chain(dve, s["chain"])
                    dve.sem_inc(s["ready"], TILES)
                    dve.sem_inc(s["banks_free"], 2)
                    dve.wait_ge(s["loads"], 32)
                    for j in range(chunks):
                        cs = slice(j * CHUNK, (j + 1) * CHUNK)
                        for t in range(TILES):
                            dve.wait_ge(s["done"], 3 * j + t + 1)
                            c.link(nc.vector.tensor_tensor(TM[:, t, :], PS[3 * j + t], G1[:, int(t > 0), cs], ALU.mult))
                            c.mark(nc.vector.tensor_tensor(X[:, t, cs], X[:, t, cs], TM[:, t, :], ALU.add))
                    c.sync()

        PB = BIG
        SC = PB[:, 0:6144].rearrange("p (t n) -> p t n", t=TILES)
        QP = PB[:, 6144:12288].rearrange("p (b n) -> p b n", b=16)
        IDXF = Zf[:, 0:384].rearrange("p (t n) -> p t n", t=TILES)
        IDX = Zf[:, 384:768].bitcast(U32).rearrange("p (t n) -> p t n", t=TILES)
        GATE = Zf[:, 768:1152].rearrange("p (t n) -> p t n", t=TILES)
        DOTS = Zf[:, 1152:1536].rearrange("p (t n) -> p t n", t=TILES)
        NB = 8
        IDS = Zf[:, 1536:1536 + 2 * NB].bitcast(U32)
        DST = Zf[:, 1600:1600 + 2 * NB]

        def stage_route(l):
            s = signals("free loaded0 loaded1 banks_free done filled keys kturned kcopy scored scopy"
                           " chain dif exp top")
            loaded = [s["loaded0"], s["loaded1"]]
            KY = PB[:, 12288:12544].rearrange("p (a n) -> p a n", a=2)
            KYT = PB[:, 12544:12800].rearrange("p (a n) -> p a n", a=2)
            V16 = PB[:, 12800:13056].rearrange("p (g n) -> p g n", g=16)
            I16 = PB[:, 13056:13312].bitcast(U32).rearrange("p (g n) -> p g n", g=16)
            I16F = PB[:, 13312:13568].rearrange("p (g n) -> p g n", g=16)
            BV = PB[:, 13568:13696].rearrange("p (g n) -> p g n", g=8)
            BI = PB[:, 13696:13824].bitcast(U32)
            BA = PB[:, 13824:13952].bitcast(U32)
            BF = PB[:, 13952:14080]
            SEL = PB[:, 14080:14336].rearrange("p (a n) -> p a n", a=2)
            RS = PB[:, 14336:14344]
            CAND = PB[:, 14464:16512]
            OH = RING[:, 0:2048]
            CANB = PB[:, 16512:16768]
            SC2 = PB[:, 16768:16896]
            wq = I["peer_wq"].rearrange("l (k p) n -> l p k n", p=P)
            chunks = PEER_HEADS * PEER_DQ // CHUNK
            with nc.Block(no_gpsimd_drain=True) as block:
                @block.sync
                def _(sp):
                    sp.dma_start(KY, I["peer_keys"][l].rearrange("a n d -> n a d")).then_inc(s["keys"], 16)
                    sp_weights(sp, lambda n: wq[l, :, :, ds(n * CHUNK, CHUNK)], chunks, 0, s["free"], loaded)

                @block.tensor
                def _(pe):
                    pe.sem_inc(s["free"], 2)
                    pe.wait_ge(s["keys"], 16)
                    for a in range(2):
                        mm = nc.tensor.transpose(PS[7][:, a * P:(a + 1) * P], KY[:, a, :], ID)
                    mm.then_inc(s["kturned"], 1)
                    pe.wait_ge(s["kcopy"], 1)
                    with pe.Fori(0, chunks // 2) as i:
                        for j in range(2):
                            pe.wait_ge(loaded[j], 16 + 16 * i)
                            for b in range(4):
                                pe.wait_ge(s["banks_free"], 8 * i + 4 * j + b + 1)
                                for k in range(KT):
                                    mm = nc.tensor.matmul(PS[4 * j + b][:, 0:TOK], RW[:, j, k, b * P:(b + 1) * P], HT[:, k, :],
                                                          start=(k == 0), stop=(k == KT - 1))
                                mm.then_inc(s["done"], 1)
                            pe.drain().then_inc(s["free"], 1)
                    pe.wait_ge(s["filled"], 4 * chunks)
                    for t in range(TILES):
                        for b in range(4):
                            n = 4 * t + b
                            if n >= 8:
                                pe.wait_ge(s["scopy"], n - 7)
                            for k in range(4):
                                g = 4 * b + k
                                mm = nc.tensor.matmul(PS[n % 8][:, k * P:(k + 1) * P], QP[:, g, t * P:(t + 1) * P],
                                                      KYT[:, g % 2, :], start=True, stop=True)
                            mm.then_inc(s["scored"], 1)

                @block.scalar
                def _(act):
                    act.sem_inc(s["banks_free"], 8)
                    act.wait_ge(s["kturned"], 1)
                    nc.scalar.activation(KYT, PS[7][:, 0:256].rearrange("p (a n) -> p a n", a=2), ACT.Copy).then_inc(s["kcopy"], 1)
                    with act.Fori(0, chunks // 2) as i:
                        for n in range(8):
                            act.wait_ge(s["done"], 8 * i + n + 1)
                            nc.scalar.activation(QP[:, 8 * i + n, :], PS[n][:, 0:TOK], ACT.Copy).then_inc(s["filled"], 1)
                            act.drain().then_inc(s["banks_free"], 1)
                    for n in range(4 * TILES):
                        t, b = divmod(n, 4)
                        act.wait_ge(s["scored"], n + 1)
                        nc.scalar.activation(SC[:, t, b * 512:(b + 1) * 512], PS[n % 8], ACT.Copy).then_inc(s["scopy"], 1)
                    for t in range(TILES):
                        act.wait_ge(s["dif"], t + 1)
                        nc.scalar.activation(GATE[:, t, :], GATE[:, t, :], ACT.Exp).then_inc(s["exp"], 1)

                @block.vector
                def _(dve):
                    clear_last_stage(dve, s)
                    c = Chain(dve, s["chain"])

                    def top16(vals, work, v16, i16):
                        c.link(nc.vector.max(v16[:, 0:8], vals))
                        c.mark(nc.vector.max_index(i16[:, 0:8], v16[:, 0:8], vals))
                        c.link(nc.vector.match_replace(work, v16[:, 0:8], vals, BIGNEG))
                        c.link(nc.vector.max(v16[:, 8:16], work))
                        c.mark(nc.vector.max_index(i16[:, 8:16], v16[:, 8:16], work))

                    for t in range(TILES):
                        dve.wait_ge(s["scopy"], 4 * t + 4)
                        for g in range(16):
                            top16(SC[:, t, g * P:(g + 1) * P], SC2, V16[:, g, :], I16[:, g, :])
                        c.sync()
                        c.mark(nc.vector.tensor_copy(I16F, I16))
                        v4 = V16.rearrange("p (h a) n -> p h a n", a=2)
                        ca = CAND.rearrange("p (h a b) -> p h a b", h=8, a=TOPK)
                        c.link(nc.vector.tensor_tensor(ca, v4[:, :, 0, :].unsqueeze(3).to_broadcast([P, 8, TOPK, TOPK]),
                                                       v4[:, :, 1, :].unsqueeze(2).to_broadcast([P, 8, TOPK, TOPK]), ALU.add))
                        for h in range(8):
                            top16(CAND[:, h * 256:(h + 1) * 256], CANB, BV[:, h, :], BI[:, h * 16:(h + 1) * 16])
                        c.sync()
                        i4 = I16F.rearrange("p (h a) n -> p h a n", a=2)
                        oh = OH.rearrange("p (h k a) -> p h k a", h=8, k=TOPK)
                        for half in range(2):
                            if half == 0:
                                c.link(nc.vector.tensor_scalar(BA, BI, 4, None, ALU.logical_shift_right))
                            else:
                                c.link(nc.vector.tensor_scalar(BA, BI, TOPK - 1, None, ALU.bitwise_and))
                            c.link(nc.vector.tensor_copy(BF, BA))
                            bf = BF.rearrange("p (h k) -> p h k", h=8).unsqueeze(3).to_broadcast([P, 8, TOPK, TOPK])
                            io = POS[:, POS_IOTA:POS_IOTA + TOPK].unsqueeze(1).unsqueeze(1).to_broadcast([P, 8, TOPK, TOPK])
                            c.link(nc.vector.tensor_tensor(oh, bf, io, ALU.is_equal))
                            c.link(nc.vector.tensor_tensor(oh, oh, i4[:, :, half, :].unsqueeze(2).to_broadcast([P, 8, TOPK, TOPK]),
                                                           ALU.mult))
                            c.link(nc.vector.tensor_reduce(SEL[:, half, :], OH.rearrange("p (g a) -> p g a", a=TOPK), AX, ALU.add))
                        c.link(nc.vector.tensor_scalar(SEL[:, 0, :], SEL[:, 0, :], float(N_KEYS), LAMC[:, 2:3], ALU.mult, ALU.add))
                        c.link(nc.vector.tensor_tensor(IDX[:, t, :], SEL[:, 0, :], SEL[:, 1, :], ALU.add))
                        g3 = GATE[:, t, :].rearrange("p (h k) -> p h k", h=8)
                        c.link(nc.vector.tensor_tensor(g3, BV, BV[:, :, 0:1].to_broadcast([P, 8, TOPK]), ALU.subtract))
                        dve.sem_inc(s["dif"], 1)
                        dve.wait_ge(s["exp"], t + 1)
                        c.link(nc.vector.tensor_reduce(RS, g3, AX, ALU.add))
                        c.link(nc.vector.reciprocal(RS, RS))
                        c.link(nc.vector.tensor_tensor(g3, g3, bl(RS, TOPK), ALU.mult))

        def stage_experts(l):
            s = signals("staged chain dots acted used started loads"
                           "")
            seen = 16 * 2 * TILES * SLOTS // (2 * NB) * l
            UB = BIG[:, 0:2 * NB * D].rearrange("p (b n) -> p b n", b=2 * NB)
            JUNK = BIG[:, 2 * NB * D:2 * NB * D + D]
            Y = HT.rearrange("p k n -> p (k n)").rearrange("p (t n) -> p t n", t=TILES)
            G2 = MACC.rearrange("p t n -> p (t n)")[:, 0:2 * D].rearrange("p (g n) -> p g n", g=2)
            tables = [I["peer_u"].rearrange("l e d -> (l e) d"), I["peer_v"].rearrange("l e d -> (l e) d")]
            groups = SLOTS // (2 * NB)
            passes = 2 * TILES * groups
            with nc.Block(no_gpsimd_drain=True) as block:
                @block.sync
                def _(sp):
                    for g in range(2):
                        sp.dma_start(G2[:, g, :], modd[g, 5 * D:6 * D].partition_broadcast(P)).then_inc(s["loads"], 16)

                @block.gpsimd
                def _(pool):
                    for phase in range(2):
                        with pool.Fori(0, TILES * groups) as i:
                            pos = i + phase * TILES * groups
                            for half in range(2):
                                pool.wait_ge(s["used"], 2 * pos + half + 1)
                                nc.gpsimd.tensor_copy(IDS[:, half * NB:(half + 1) * NB],
                                                      IDX.rearrange("p t n -> p (t n)")[:, ds(2 * NB * i + half * NB, NB)])\
                                    .then_inc(s["staged"], 1)
                                pool.wait_ge(s["staged"], 2 * pos + half + 1)
                                pool.sem_inc(s["started"], 1)
                                for n in range(NB):
                                    b = half * NB + n
                                    nc.gpsimd.indirect_dma_start(
                                        out=UB[:, b, :], out_offset=None, in_=tables[phase],
                                        in_offset=bass.IndirectOffsetOnAxis(ap=IDS[:, b:b + 1], axis=0)).then_inc(got[b], 16)

                @block.scalar
                def _(act):
                    act.wait_ge(s["dots"], 1)
                    nc.scalar.activation(DOTS, DOTS, ACT.Gelu).then_inc(s["acted"], 1)

                @block.vector
                def _(dve):
                    clear_last_stage(dve, s)
                    c = Chain(dve, s["chain"])
                    dve.sem_inc(s["used"], 2)
                    c.link(nc.vector.memset(Y, 0.0))
                    dots = DOTS.rearrange("p t n -> p (t n)")
                    with dve.Fori(0, TILES) as t:
                        c.enter(t, groups * 2 * (NB + 1))
                        base = c.n
                        with dve.Fori(0, groups) as i:
                            c.n = base + i * (2 * (NB + 1))
                            for half in range(2):
                                for n in range(NB):
                                    b = half * NB + n
                                    dve.wait_ge(got[b], seen + 16 * groups * t + 16 * i + 16)
                                    c.link(nc.vector.scalar_tensor_tensor(JUNK, UB[:, b, :], 1.0, H[:, t, :], ALU.mult, ALU.mult,
                                                                          accum_out=DST[:, b:b + 1]))
                                dve.sem_inc(s["used"], 1)
                                c.mark(nc.vector.tensor_copy(dots[:, ds(SLOTS * t + 2 * NB * i + half * NB, NB)],
                                                             DST[:, half * NB:(half + 1) * NB]))
                        c.k = groups * 2 * (NB + 1)
                        c.leave(TILES)
                    c.sync()
                    dve.sem_inc(s["dots"], 1)
                    dve.wait_ge(s["acted"], 1)
                    c.link(nc.vector.tensor_tensor(DOTS, DOTS, GATE, ALU.mult))
                    turn = 16 * groups * TILES
                    with dve.Fori(0, TILES) as t:
                        c.enter(t, groups * 2 * (NB + 1))
                        base = c.n
                        with dve.Fori(0, groups) as i:
                            c.n = base + i * (2 * (NB + 1))
                            for half in range(2):
                                c.link(nc.vector.tensor_copy(DST[:, half * NB:(half + 1) * NB],
                                                             dots[:, ds(SLOTS * t + 2 * NB * i + half * NB, NB)]))
                                for n in range(NB):
                                    b = half * NB + n
                                    dve.wait_ge(got[b], seen + turn + 16 * groups * t + 16 * i + 16)
                                    c.link(nc.vector.scalar_tensor_tensor(Y[:, t, :], UB[:, b, :], DST[:, b:b + 1], Y[:, t, :],
                                                                          ALU.mult, ALU.add))
                                dve.sem_inc(s["used"], 1)
                        c.k = groups * 2 * (NB + 1)
                        c.leave(TILES)
                    dve.wait_ge(s["loads"], 32)
                    for t in range(TILES):
                        c.link(nc.vector.tensor_tensor(Y[:, t, :], Y[:, t, :], G2[:, int(t > 0), :], ALU.mult))
                        c.link(nc.vector.tensor_tensor(X[:, t, :], X[:, t, :], Y[:, t, :], ALU.add))

        ZB = sb("gdn_final_states", 2 * G_HEADS * G_DV)
        ZST = [ZB[:, v * 1024:(v + 1) * 1024].rearrange("p (h n) -> p h n", h=8) for v in range(2)]

        with nc.Fori(0, DEPTH) as l:
            stage_mod(l)
            stage_norm(l, 0)
            stage_project(l, [(COL_RET, 4, PRJ, ACT.Copy), (COL_RET_G, 2, Z, ACT.Silu)])
            stage_retention(l)
            stage_merge(l, 0)
            stage_project(l, [(COL_DIFF, 6, PRJ, ACT.Copy)])
            stage_diff(l)
            stage_merge(l, 1)
            stage_gdn_project(l)
            stage_gdn_prepare(l)
            stage_gdn(l)
            stage_merge(l, 2)
            stage_out(l)
            stage_norm(l, 1)
            stage_route(l)
            stage_experts(l)

        s = signals("loads squares mean root chain ready stored")
        with nc.Block(no_gpsimd_drain=True) as block:
            @block.sync
            def _(sp):
                sp.dma_start(UP[:, 0:D], I["norm_f_w"].partition_broadcast(P)).then_inc(s["loads"], 16)
                sp.wait_ge(s["ready"], 1)
                sp.dma_start(O["y_prompt"][0], H[:, 0, :]).then_inc(s["stored"], 16)
                sp.wait_ge(s["ready"], 3)
                sp.dma_start(O["y_sample"][0].rearrange("(t p) n -> p t n", p=P), H[:, 1:3, :]).then_inc(s["stored"], 16)
                sp.wait_ge(s["stored"], 32)

            @block.scalar
            def _(act):
                for t in range(TILES):
                    nc.scalar.activation(BIG[:, t * D:(t + 1) * D], X[:, t, :], ACT.Square, accum_out=SM[:, t:t + 1])\
                        .then_inc(s["squares"], 1)
                act.wait_ge(s["mean"], 1)
                nc.scalar.activation(SM[:, 4:7], SM[:, 0:3], ACT.Sqrt).then_inc(s["root"], 1)

            @block.vector
            def _(dve):
                c = Chain(dve, s["chain"])
                dve.wait_ge(s["squares"], TILES)
                nc.vector.tensor_scalar(SM[:, 0:3], SM[:, 0:3], 1.0 / D, EPS, ALU.mult, ALU.add).then_inc(s["mean"], 1)
                dve.wait_ge(s["root"], 1)
                c.link(nc.vector.reciprocal(SM[:, 4:7], SM[:, 4:7]))
                dve.wait_ge(s["loads"], 16)
                for t in range(TILES):
                    nc.vector.scalar_tensor_tensor(H[:, t, :], X[:, t, :], SM[:, 4 + t:5 + t], UP[:, 0:D],
                                                   ALU.mult, ALU.mult).then_inc(s["ready"], 1)


_INS = ["x_prompt", "x_sample", "cache_diff_k", "cache_diff_v", "state_ret", "state_gdn", "c", "c_ctx", "norm1_w",
        "norm2_w", "w_mod", "b_mod", "w_in", "ret_decay", "ret_norm", "diff_lambda", "diff_norm", "gdn_conv",
        "gdn_A_log", "gdn_dt_bias", "gdn_norm", "w_branch", "w_out", "peer_wq", "peer_keys", "peer_u", "peer_v",
        "norm_f_w"]
_OUTS = [("y_prompt", (1, SEQ, D)), ("y_sample", (1, DEC_SEQ, D)),
         ("new_cache_diff_k", (1, DEPTH, SEQ, D_HEADS, 2, D_HD)), ("new_cache_diff_v", (1, DEPTH, SEQ, D_HEADS, 2 * D_HD)),
         ("new_state_ret", (1, DEPTH, 2, R_HEADS, R_DK, R_DV)), ("new_state_gdn", (1, DEPTH, 2, G_HEADS, G_DK, G_DV))]


def kernel(**inputs):
    import numpy as _np
    import concourse.bacc as _bacc
    from concourse import mybir as _mybir
    from concourse.bass_utils import run_bass_kernel_spmd as _run

    nc = _bacc.Bacc("TRN2", target_bir_lowering=False, num_devices=1)
    arrays, ins, outs = {}, {}, {}
    for name, a in [(n, inputs[n]) for n in _INS] + list(shape_tables().items()):
        a = _np.ascontiguousarray(a)
        arrays[f"in_{name}_dram"] = a
        ins[name] = nc.dram_tensor(f"in_{name}_dram", a.shape, _mybir.dt.from_np(a.dtype), kind="ExternalInput").ap()
    for name, shape in _OUTS:
        outs[name] = nc.dram_tensor(f"out_{name}_dram", shape, _mybir.dt.float32, kind="ExternalOutput").ap()
    build(nc, ins, outs)
    r = _run(nc, [arrays], core_ids=[0])
    return tuple(r.results[0][f"out_{name}_dram"] for name, _ in _OUTS)
```

```python
import math
from contextlib import ExitStack

import numpy as np

import concourse.bass as bass
from concourse import mybir

F32 = mybir.dt.float32
U32 = mybir.dt.uint32
ALU = mybir.AluOpType
ACT = mybir.ActivationFunctionType
AX = mybir.AxisListType.X
ds = bass.ds

P = 128
D = 1024
KT = D // P
DEPTH = 2
SEQ = 128
DEC_SEQ = 256
TILES = (SEQ + DEC_SEQ) // P
TOK = TILES * P
PAST = 128
GRID_W = 64
ROPE_BASE = 10000.0
EPS = 1e-6
R_HEADS, R_DK, R_DV = 4, 128, 256
D_HEADS, D_HD = 8, 64
G_HEADS, G_DK, G_DV = 8, 128, 128
CONV_K = 7
G_QKV = G_HEADS * (2 * G_DK + G_DV)
N_BRANCH = 3
PEER_HEADS, PEER_DQ, N_KEYS, TOPK = 8, 256, 128, 16
N_EXPERTS = N_KEYS * N_KEYS
SLOTS = PEER_HEADS * TOPK
MOD = 6 * D
CHUNK = 512
COL_RET = 0
COL_RET_G = 2 * R_HEADS * R_DK + R_HEADS * R_DV
COL_DIFF = COL_RET_G + R_HEADS * R_DV
COL_GDN = COL_DIFF + 3 * D_HEADS * 2 * D_HD
COL_GDN_Z = COL_GDN + G_QKV
COL_GDN_AB = COL_GDN_Z + G_HEADS * G_DV
COL_GATES = COL_GDN_AB + 4 * G_HEADS
PAD = CONV_K // 2
XC_P = PAD
XC_S = PAD + SEQ + 2 * PAD
XC_W = XC_S + DEC_SEQ + PAD
CV_W = XC_W - 2 * PAD
CV_S = XC_S - PAD
QBLK = G_QKV // P
LEVELS = 7
LATENT = (1, 2)
BIGNEG = -3.0e38
POS_QF, POS_QB, POS_KF, POS_KB, POS_IOTA = 0, 2, 4, 5, 6
TRI_POS, TRI_NEG, TRI_UP, TRI_LO, TRI_ID, TRI_ONE, TRI_OFF_F, TRI_OFF_B = range(8)


def shape_tables():
    j = np.arange(P, dtype=np.float32)[:, None]
    i = np.arange(P, dtype=np.float32)[None, :]
    tri = np.stack([np.maximum(i - j, 0), np.maximum(j - i, 0), (i >= j) * 1.0, (j >= i) * 1.0,
                    np.eye(P), np.ones((P, P)), i - j + P, j - i + P], 1).astype(np.float32)
    lvl = np.zeros((P, 2, LEVELS, P), np.float32)
    jj, ii = np.arange(P)[:, None], np.arange(P)[None, :]
    for n in range(LEVELS):
        s = 1 << n
        same = (jj // (2 * s)) == (ii // (2 * s))
        lvl[:, 0, n] = same & (jj % (2 * s) < s) & (ii % (2 * s) >= s)
        lvl[:, 1, n] = same & (ii % (2 * s) < s) & (jj % (2 * s) >= s)
    p = np.arange(P, dtype=np.float32)
    pos = np.zeros((P, POS_IOTA + TOPK), np.float32)
    pos[:, POS_QF] = p + 1
    pos[:, POS_QF + 1] = p + P + 1
    pos[:, POS_QB] = DEC_SEQ - p
    pos[:, POS_QB + 1] = DEC_SEQ - P - p
    pos[:, POS_KF] = SEQ - 1 - p
    pos[:, POS_KB] = p
    pos[:, POS_IOTA:] = np.arange(TOPK)

    def rope(dim):
        nf = dim // 4
        rows = DEC_SEQ // GRID_W
        row = np.repeat(np.arange(rows), GRID_W).astype(np.float32)
        col = np.tile(np.arange(GRID_W), rows).astype(np.float32)
        inv = np.power(np.float32(ROPE_BASE), -np.arange(nf, dtype=np.float32) / np.float32(nf)).astype(np.float32)
        r, c = row[:, None] * inv, col[:, None] * inv
        ang = np.concatenate([r, r, c, c], -1).astype(np.float64)
        sign = np.repeat([-1.0, 1.0, -1.0, 1.0], nf)
        t = np.stack([np.cos(ang), np.sin(ang) * sign], 1).astype(np.float32)
        return t.reshape(len(LATENT), P, 2, dim).transpose(1, 0, 2, 3).copy()

    lam = np.zeros((DEPTH, 4), np.float32)
    for li in range(DEPTH):
        init = 0.8 - 0.6 * math.exp(-0.3 * li)
        lam[li] = [init, 1.0 - init, li * N_EXPERTS, 0]
    return {"tri": tri, "lvl": lvl, "pos": pos, "rope_ret": rope(R_DK), "rope_diff": rope(D_HD), "layer": lam}


class Chain:

    def __init__(self, eng, sem):
        self.eng, self.sem, self.n, self.k = eng, sem, 0, 0

    def mark(self, ins):
        ins.then_inc(self.sem, 1)
        self.n = self.n + 1
        self.k += 1

    def sync(self):
        self.eng.wait_ge(self.sem, self.n)

    def link(self, ins):
        self.mark(ins)
        self.sync()

    def enter(self, i, per):
        self.base, self.per, self.k = self.n, per, 0
        self.n = self.base + i * per

    def leave(self, passes):
        assert self.k == self.per, (self.k, self.per)
        self.n = self.base + passes * self.per


def bc(ap, n):
    return ap.unsqueeze(1).to_broadcast([ap.shape[0], n, ap.shape[1]])


def bl(ap, n):
    return ap.unsqueeze(2).to_broadcast([ap.shape[0], ap.shape[1], n])


def build(nc, I, O, debug=None):
    ctx = ExitStack()
    with ctx:
        def sb(name, cols, dt=F32):
            return ctx.enter_context(nc.sbuf_tensor(name, [P, cols], dt))[:, :]

        PS = [ctx.enter_context(nc.psum_tensor(f"bank{n}", [P, 512], F32))[:, :] for n in range(8)]
        X = sb("x_residual", TILES * D).rearrange("p (t n) -> p t n", t=TILES)
        H = sb("h_tokens", TILES * D).rearrange("p (t n) -> p t n", t=TILES)
        HT = sb("h_features", KT * TOK).rearrange("p (k n) -> p k n", k=KT)
        MACC = sb("merged", TILES * D).rearrange("p (t n) -> p t n", t=TILES)
        Zf = sb("gates_z", TILES * D)
        Z = Zf.rearrange("p (t n) -> p t n", t=TILES)
        RING = sb("weight_ring", 2 * KT * CHUNK)
        RW = RING.rearrange("p (s k n) -> p s k n", s=2, k=KT)
        BIG = sb("work", 18432)
        HALF = 9216
        SST = sb("gdn_states", 2 * G_HEADS * G_DV).rearrange("p (g n) -> p g n", g=2 * G_HEADS)
        TRI = sb("triangles", 8 * P).rearrange("p (a n) -> p a n", a=8)
        LVL = sb("levels", 2 * LEVELS * P).rearrange("p (d a n) -> p d a n", d=2, a=LEVELS)
        POS = sb("positions", POS_IOTA + TOPK)
        ROPR = sb("rope_ret", 2 * 2 * R_DK).rearrange("p (t a n) -> p t a n", t=2, a=2)
        ROPD = sb("rope_diff", 2 * 2 * D_HD).rearrange("p (t a n) -> p t a n", t=2, a=2)
        LAMC = sb("layer_constants", 4)
        COND = sb("conditions", KT * 2).rearrange("p (k g) -> p k g", g=2)
        SM = sb("small", 1024)
        modd = nc.dram_tensor("mod_rows", (2, MOD), F32).ap()

        ID = TRI[:, TRI_ID, :]
        PRJ = BIG[:, 0:HALF].rearrange("p (t n) -> p t n", t=TILES)
        UP = BIG[:, HALF:2 * HALF]

        pools = [[ctx.enter_context(nc.semaphore(f"stage{n}_{k}")) for k in range(40)] for n in range(2)]
        assert all([x.num for x in pool] == list(range(pool[0].num, pool[0].num + 40)) for pool in pools)
        got = [ctx.enter_context(nc.semaphore(f"row_gathered{n}")) for n in range(16)]
        turns = [1]

        def signals(names):
            turns[0] = 1 - turns[0]
            names = names.split()
            assert len(names) <= len(pools[0])
            return dict(zip(names, pools[turns[0]]))

        def clear_last_stage(dve, s):
            other = pools[1] if any(x.num == pools[0][0].num for x in s.values()) else pools[0]
            dve.sem_clear(range(other[0].num, other[-1].num + 1))

        def sp_weights(sp, src, chunks, base, free, loaded):
            with sp.Fori(0, chunks // 2) as i:
                for j in range(2):
                    sp.wait_ge(free, base + 2 * i + j + 1)
                    sp.dma_start(RW[:, j], src(2 * i + j)).then_inc(loaded[j], 16)

        def pe_project(pe, xt, chunks, base, free, loaded, banks_free, done):
            with pe.Fori(0, chunks // 2) as i:
                for j in range(2):
                    pe.wait_ge(loaded[j], 16 * (base // 2 + 1) + 16 * i)
                    pe.wait_ge(banks_free, base + 2 * i + j + 1)
                    for t in range(TILES):
                        for k in range(KT):
                            mm = nc.tensor.matmul(PS[3 * j + t], xt[j][:, k, t * P:(t + 1) * P], RW[:, j, k, :],
                                                  start=(k == 0), stop=(k == KT - 1))
                        mm.then_inc(done, 1)
                    pe.drain().then_inc(free, 1)

        def pe_transpose_tokens(pe, src, ready, banks_free, done):
            for t in range(TILES):
                pe.wait_ge(ready, t + 1)
                for b in range(2):
                    n = 2 * t + b
                    if n >= 2:
                        pe.wait_ge(banks_free, n - 1)
                    for k in range(4):
                        kk = 4 * b + k
                        mm = nc.tensor.transpose(PS[6 + b][:, k * P:(k + 1) * P], src[:, t, kk * P:(kk + 1) * P], ID)
                    mm.then_inc(done, 1)

        def act_transposed(act, dst, done, out_sem):
            for t in range(TILES):
                for b in range(2):
                    act.wait_ge(done, 2 * t + b + 1)
                    nc.scalar.activation(dst[:, 4 * b:4 * b + 4, t * P:(t + 1) * P],
                                         PS[6 + b].rearrange("p (k n) -> p k n", k=4), ACT.Copy).then_inc(out_sem, 1)

        with nc.Block(no_gpsimd_drain=True) as block:
            s = signals("loads silu")

            @block.sync
            def _(sp):
                sp.dma_start(X[:, 0, :], I["x_prompt"][0]).then_inc(s["loads"], 16)
                sp.dma_start(X[:, 1:3, :], I["x_sample"][0].rearrange("(t p) n -> p t n", p=P)).then_inc(s["loads"], 16)
                sp.dma_start(TRI, I["tri"]).then_inc(s["loads"], 16)
                sp.dma_start(LVL, I["lvl"]).then_inc(s["loads"], 16)
                sp.dma_start(POS, I["pos"]).then_inc(s["loads"], 16)
                sp.dma_start(ROPR, I["rope_ret"]).then_inc(s["loads"], 16)
                sp.dma_start(ROPD, I["rope_diff"]).then_inc(s["loads"], 16)
                with nc.allow_non_contiguous_dma(reason="two short vectors, laid over partitions"):
                    sp.dma_start(SM[:, 0:KT], I["c_ctx"].rearrange("(k p) -> p k", p=P)).then_inc(s["loads"], 16)
                    sp.dma_start(SM[:, KT:2 * KT], I["c"][0].rearrange("(k p) -> p k", p=P)).then_inc(s["loads"], 16)

            @block.scalar
            def _(act):
                act.wait_ge(s["loads"], 9 * 16)
                for g in range(2):
                    nc.scalar.activation(COND[:, :, g], SM[:, g * KT:(g + 1) * KT], ACT.Silu).then_inc(s["silu"], 1)

        def stage_mod(l):
            s = signals("free loaded0 loaded1 banks_free done added bias stored chain")
            loaded = [s["loaded0"], s["loaded1"]]
            w = I["w_mod"].rearrange("l (k p) n -> l p k n", p=P)
            rows, bias = BIG[0:2, 0:MOD], BIG[0:2, MOD:2 * MOD]
            chunks = MOD // CHUNK
            with nc.Block(no_gpsimd_drain=True) as block:
                @block.sync
                def _(sp):
                    sp.dma_start(bias, I["b_mod"][l].partition_broadcast(2)).then_inc(s["bias"], 16)
                    sp.dma_start(LAMC, I["layer"][l].partition_broadcast(P)).then_inc(s["bias"], 16)
                    sp_weights(sp, lambda n: w[l, :, :, ds(n * CHUNK, CHUNK)], chunks, 0, s["free"], loaded)
                    sp.wait_ge(s["added"], chunks)
                    sp.dma_start(modd, rows).then_inc(s["stored"], 16)
                    sp.wait_ge(s["stored"], 16)

                @block.tensor
                def _(pe):
                    pe.sem_inc(s["free"], 2)
                    with pe.Fori(0, chunks // 2) as i:
                        for j in range(2):
                            pe.wait_ge(loaded[j], 16 + 16 * i)
                            pe.wait_ge(s["banks_free"], 2 * i + j + 1)
                            for k in range(KT):
                                mm = nc.tensor.matmul(PS[j][0:2, :], COND[:, k, :], RW[:, j, k, :],
                                                      start=(k == 0), stop=(k == KT - 1))
                            mm.then_inc(s["done"], 1)
                            pe.drain().then_inc(s["free"], 1)

                @block.vector
                def _(dve):
                    clear_last_stage(dve, s)
                    dve.sem_inc(s["banks_free"], 2)
                    dve.wait_ge(s["bias"], 32)
                    with dve.Fori(0, chunks // 2) as i:
                        for j in range(2):
                            dve.wait_ge(s["done"], 2 * i + j + 1)
                            cols = ds(2 * CHUNK * i + j * CHUNK, CHUNK)
                            nc.vector.tensor_tensor(rows[:, cols], PS[j][0:2, :], bias[:, cols], ALU.add)\
                                .then_inc(s["added"], 1)
                            dve.drain().then_inc(s["banks_free"], 1)

        def stage_norm(l, which):
            s = signals("loads squares mean root ready free done copied chain")
            norm_w = I["norm1_w"] if which == 0 else I["norm2_w"]
            NW = UP[:, 0:D]
            SH = UP[:, D:3 * D].rearrange("p (g n) -> p g n", g=2)
            SC = UP[:, 3 * D:5 * D].rearrange("p (g n) -> p g n", g=2)
            SQ = UP[:, 5 * D:8 * D].rearrange("p (t n) -> p t n", t=TILES)
            SS = SM[:, 0:TILES]
            RS = SM[:, 4:4 + TILES]
            off = 3 * D * which
            with nc.Block(no_gpsimd_drain=True) as block:
                @block.sync
                def _(sp):
                    sp.dma_start(NW, norm_w[l].partition_broadcast(P)).then_inc(s["loads"], 16)
                    for g in range(2):
                        sp.dma_start(SH[:, g, :], modd[g, off:off + D].partition_broadcast(P)).then_inc(s["loads"], 16)
                        sp.dma_start(SC[:, g, :], modd[g, off + D:off + 2 * D].partition_broadcast(P))\
                            .then_inc(s["loads"], 16)

                @block.scalar
                def _(act):
                    for t in range(TILES):
                        nc.scalar.activation(SQ[:, t, :], X[:, t, :], ACT.Square, accum_out=SS[:, t:t + 1])\
                            .then_inc(s["squares"], 1)
                    act.wait_ge(s["mean"], 1)
                    nc.scalar.activation(RS, SS, ACT.Sqrt).then_inc(s["root"], 1)
                    act_transposed(act, HT, s["done"], s["free"])

                @block.vector
                def _(dve):
                    clear_last_stage(dve, s)
                    c = Chain(dve, s["chain"])
                    dve.wait_ge(s["squares"], TILES)
                    nc.vector.tensor_scalar(SS, SS, 1.0 / D, EPS, ALU.mult, ALU.add).then_inc(s["mean"], 1)
                    dve.wait_ge(s["loads"], 5 * 16)
                    for g in range(2):
                        c.mark(nc.vector.scalar_tensor_tensor(SC[:, g, :], SC[:, g, :], 1.0, NW, ALU.add, ALU.mult))
                    dve.wait_ge(s["root"], 1)
                    c.link(nc.vector.reciprocal(RS, RS))
                    for t in range(TILES):
                        g = int(t > 0)
                        c.link(nc.vector.scalar_tensor_tensor(H[:, t, :], X[:, t, :], RS[:, t:t + 1], SC[:, g, :],
                                                              ALU.mult, ALU.mult))
                        nc.vector.tensor_tensor(H[:, t, :], H[:, t, :], SH[:, g, :], ALU.add).then_inc(s["ready"], 1)

                @block.tensor
                def _(pe):
                    pe_transpose_tokens(pe, H, s["ready"], s["free"], s["done"])

        w_in = I["w_in"].rearrange("l (k p) n -> l p k n", p=P)

        def stage_project(l, parts):
            s = signals("free loaded0 loaded1 banks_free done")
            loaded = [s["loaded0"], s["loaded1"]]
            with nc.Block(no_gpsimd_drain=True) as block:
                @block.sync
                def _(sp):
                    base = 0
                    for col, chunks, _, _ in parts:
                        sp_weights(sp, lambda n: w_in[l, :, :, ds(n * CHUNK + col, CHUNK)], chunks, base, s["free"], loaded)
                        base += chunks

                @block.tensor
                def _(pe):
                    pe.sem_inc(s["free"], 2)
                    base = 0
                    for _, chunks, _, _ in parts:
                        pe_project(pe, (HT, HT), chunks, base, s["free"], loaded, s["banks_free"], s["done"])
                        base += chunks

                @block.scalar
                def _(act):
                    act.sem_inc(s["banks_free"], 2)
                    base = 0
                    for _, chunks, dst, func in parts:
                        with act.Fori(0, chunks // 2) as i:
                            for j in range(2):
                                for t in range(TILES):
                                    act.wait_ge(s["done"], 3 * base + 6 * i + 3 * j + t + 1)
                                    nc.scalar.activation(dst[:, t, ds(2 * CHUNK * i + j * CHUNK, CHUNK)],
                                                         PS[3 * j + t], func)
                                act.drain().then_inc(s["banks_free"], 1)
                        base += chunks

                @block.vector
                def _(dve):
                    clear_last_stage(dve, s)

        def rope(dve, c, view, table, groups, dim, tmp):
            q = dim // 4
            for n, t in enumerate(LATENT):
                x4 = view(t).rearrange("p (g a b n) -> p g a b n", g=groups, a=2, b=2)
                t4 = tmp.rearrange("p (g a b n) -> p g a b n", g=groups, a=2, b=2)
                sin = table[:, n, 1, :].rearrange("p (a b n) -> p a b n", a=2, b=2)
                for b in range(2):
                    sb_ = sin[:, :, b, :].unsqueeze(1).to_broadcast([P, groups, 2, q])
                    c.mark(nc.vector.tensor_tensor(t4[:, :, :, b, :], x4[:, :, :, 1 - b, :], sb_, ALU.mult))
                c.sync()
                x3 = view(t).rearrange("p (g n) -> p g n", g=groups)
                c.link(nc.vector.tensor_tensor(x3, x3, bc(table[:, n, 0, :], groups), ALU.mult))
                c.link(nc.vector.tensor_tensor(view(t), view(t), tmp, ALU.add))

        def log1p_parts(dve, c, z, s_, tmp, out, like):
            c.link(nc.vector.tensor_scalar(s_, z, 2.0, None, ALU.add))
            c.link(nc.vector.reciprocal(s_, s_))
            c.link(nc.vector.tensor_tensor(s_, s_, z, ALU.mult))
            c.link(nc.vector.tensor_tensor(tmp, s_, s_, ALU.mult))
            terms = 8
            c.link(nc.vector.tensor_scalar(out, tmp, 1.0 / (2 * terms + 1), 1.0 / (2 * terms - 1), ALU.mult, ALU.add))
            for n in range(terms - 1, 0, -1):
                c.link(nc.vector.tensor_tensor(out, out, tmp, ALU.mult))
                c.link(nc.vector.tensor_scalar(out, out, 1.0 / (2 * n - 1), None, ALU.add))
            c.link(nc.vector.scalar_tensor_tensor(out, out, 2.0, s_, ALU.mult, ALU.mult))

        def dve_head_norm(dve, c, s, OV, width, sq, cols, w, extra):
            groups = TILES * D // width
            ov = OV.rearrange("p (g n) -> p g n", n=width)
            c.link(nc.vector.tensor_tensor(sq, OV, OV, ALU.mult))
            c.link(nc.vector.tensor_reduce(cols, sq.rearrange("p (g n) -> p g n", n=width), AX, ALU.add))
            nc.vector.tensor_scalar(cols, cols, 1.0 / width, EPS, ALU.mult, ALU.add).then_inc(s["mean"], 1)
            dve.wait_ge(s["root"], 1)
            c.link(nc.vector.reciprocal(cols, cols))
            c.link(nc.vector.tensor_tensor(ov, ov, bl(cols, width), ALU.mult))
            c.link(nc.vector.tensor_tensor(ov, ov, bc(w, groups), ALU.mult))
            if extra is not None:
                c.link(nc.vector.tensor_tensor(OV, OV, extra, ALU.mult))

        def act_head_root(act, s, cols):
            act.wait_ge(s["mean"], 1)
            nc.scalar.activation(cols, cols, ACT.Sqrt).then_inc(s["root"], 1)

        OT_ = UP[:, 0:KT * TOK].rearrange("p (k n) -> p k n", k=KT)
        Hf = H.rearrange("p t n -> p (t n)")

        def stage_retention(l):
            s = signals("loads chain mean root lgin lgexp lg tables roped transposed copied scores masked"
                           " out intra evacuated kd states statecopy stored")
            QT = UP[:, 0:1536].rearrange("p (h n) -> p h n", h=R_HEADS)
            KTT = UP[:, 1536:3072].rearrange("p (h n) -> p h n", h=R_HEADS)
            DT = UP[:, 3072:4608].rearrange("p (h a n) -> p h a n", h=R_HEADS, a=3)
            AT = UP[:, 4608:5888].rearrange("p (b n) -> p b n", b=2)
            E2 = UP[:, 5888:6400].rearrange("p (h n) -> p h n", h=R_HEADS)
            KD = UP[:, 6400:7424].rearrange("p (g n) -> p g n", g=8)
            TMP = RING[:, 0:1024]
            S0 = RING[:, 1024:3072].rearrange("p (g n) -> p g n", g=8)
            ST = RING[:, 3072:5120].rearrange("p (g n) -> p g n", g=8)
            SQ = RING[:, 5120:8192]
            LG, LZ, LS, LT = SM[:, 0:8], SM[:, 8:16], SM[:, 16:24], SM[:, 24:32]
            DEC = SM[:, 32:80].rearrange("p (g n) -> p g n", g=8)
            NWR = SM[:, 128:384]
            COLS = SM[:, 384:396]
            scale = R_DK ** -0.5
            with nc.Block(no_gpsimd_drain=True) as block:
                @block.sync
                def _(sp):
                    sp.dma_start(LG, I["ret_decay"][l].rearrange("d h -> (d h)").partition_broadcast(P))\
                        .then_inc(s["loads"], 16)
                    sp.dma_start(NWR, I["ret_norm"][l].partition_broadcast(P)).then_inc(s["loads"], 16)
                    sp.dma_start(S0, I["state_ret"][0, l].rearrange("d h k v -> k (d h) v")).then_inc(s["loads"], 16)
                    sp.wait_ge(s["statecopy"], 4)
                    sp.dma_start(O["new_state_ret"][0, l].rearrange("d h k v -> k (d h) v"), ST).then_inc(s["stored"], 16)
                    sp.wait_ge(s["stored"], 16)

                @block.scalar
                def _(act):
                    act.wait_ge(s["lgin"], 1)
                    nc.scalar.activation(LZ, LT, ACT.Exp).then_inc(s["lgexp"], 1)
                    act.wait_ge(s["lg"], 1)
                    for h in range(R_HEADS):
                        f, b = LG[:, h:h + 1], LG[:, R_HEADS + h:R_HEADS + h + 1]
                        nc.scalar.activation(DT[:, h, 1, :], TRI[:, TRI_POS, :], ACT.Exp, scale=f)
                        nc.scalar.activation(DT[:, h, 2, :], TRI[:, TRI_OFF_F, :], ACT.Exp, scale=f)
                        nc.scalar.activation(E2[:, h, :], TRI[:, TRI_NEG, :], ACT.Exp, scale=b)
                        nc.scalar.activation(DT[:, h, 0, :], TRI[:, TRI_OFF_B, :], ACT.Exp, scale=b)
                    for g in range(8):
                        ins = nc.scalar.activation(DEC[:, g, :], POS[:, 0:6], ACT.Exp, scale=LG[:, g:g + 1])
                    ins.then_inc(s["tables"], 1)
                    for n in range(2 * R_HEADS):
                        h, isk = n // 2, n % 2
                        act.wait_ge(s["transposed"], n + 1)
                        nc.scalar.activation((KTT if isk else QT)[:, h, :], PS[n % 4][:, 0:TOK], ACT.Copy,
                                             scale=1.0 if isk else scale).then_inc(s["copied"], 1)
                    for h in range(R_HEADS):
                        act.wait_ge(s["out"], h + 1)
                        hs = slice(h * R_DV, (h + 1) * R_DV)
                        nc.scalar.activation(H[:, 0, hs], PS[6][:, 0:256], ACT.Copy)
                        nc.scalar.activation(H[:, 1, hs], PS[6][:, 256:512], ACT.Copy)
                        nc.scalar.activation(H[:, 2, hs], PS[7][:, 0:256], ACT.Copy).then_inc(s["intra"], 1)
                    for b in range(4):
                        act.wait_ge(s["states"], b + 1)
                        nc.scalar.activation(ST[:, 2 * b:2 * b + 2, :], PS[2 + b].rearrange("p (g n) -> p g n", g=2),
                                             ACT.Copy).then_inc(s["statecopy"], 1)
                    act_head_root(act, s, COLS)

                @block.vector
                def _(dve):
                    clear_last_stage(dve, s)
                    c = Chain(dve, s["chain"])
                    rope(dve, c, lambda t: PRJ[:, t, 0:1024], ROPR, 8, R_DK, TMP)
                    dve.sem_inc(s["roped"], 1)
                    dve.wait_ge(s["loads"], 3 * 16)
                    c.mark(nc.vector.tensor_scalar(LS, LG, -1.0, None, ALU.mult))
                    c.sync()
                    nc.vector.tensor_tensor(LT, LG, LS, ALU.min).then_inc(s["lgin"], 1)
                    dve.wait_ge(s["lgexp"], 1)
                    c.link(nc.vector.tensor_scalar(LG, LG, 0.0, None, ALU.min))
                    W1, W2, W3 = SM[:, 80:88], SM[:, 88:96], SM[:, 96:104]
                    log1p_parts(dve, c, LZ, W1, W2, W3, None)
                    nc.vector.tensor_tensor(LG, LG, W3, ALU.subtract).then_inc(s["lg"], 1)
                    dve.wait_ge(s["tables"], 1)
                    c.mark(nc.vector.tensor_tensor(DT[:, :, 1, :], DT[:, :, 1, :], bc(TRI[:, TRI_UP, :], R_HEADS), ALU.mult))
                    c.link(nc.vector.tensor_tensor(E2, E2, bc(TRI[:, TRI_LO, :], R_HEADS), ALU.mult))
                    c.link(nc.vector.tensor_tensor(DT[:, :, 1, :], DT[:, :, 1, :], E2, ALU.add))
                    for g in range(8):
                        d, h = divmod(g, R_HEADS)
                        ins = nc.vector.tensor_scalar(KD[:, g, :], PRJ[:, 0, 512 + h * P:512 + (h + 1) * P],
                                                      DEC[:, g, POS_KF + d:POS_KF + d + 1], None, ALU.mult)
                    ins.then_inc(s["kd"], 1)

                    def mask(h):
                        dve.wait_ge(s["scores"], h + 1)
                        if h >= 2:
                            dve.wait_ge(s["out"], h - 1)
                        a = AT[:, h % 2, :]
                        nc.vector.tensor_tensor(a[:, 0:128], PS[4][:, 0:128], DT[:, h, 1, :], ALU.mult)
                        nc.vector.tensor_tensor(a[:, 128:384], PS[4][:, 128:384],
                                                DT[:, h, 1:3, :].rearrange("p a n -> p (a n)"), ALU.mult)
                        nc.vector.tensor_tensor(a[:, 384:640], PS[5][:, 0:256],
                                                DT[:, h, 0:2, :].rearrange("p a n -> p (a n)"), ALU.mult)\
                            .then_inc(s["masked"], 1)

                    mask(0)
                    for h in range(R_HEADS):
                        if h + 1 < R_HEADS:
                            mask(h + 1)
                        dve.wait_ge(s["out"], h + 1)
                        dve.wait_ge(s["intra"], h + 1)
                        hs = slice(h * R_DV, (h + 1) * R_DV)
                        for d in range(2):
                            for n, t in enumerate(LATENT):
                                col = DEC[:, d * R_HEADS + h, 2 * d + n:2 * d + n + 1]
                                ins = nc.vector.scalar_tensor_tensor(H[:, t, hs], PS[n][:, d * 256:(d + 1) * 256], col,
                                                                     H[:, t, hs], ALU.mult, ALU.add)
                                c.mark(ins)
                            c.sync()
                        dve.sem_inc(s["evacuated"], 1)
                    dve_head_norm(dve, c, s, Hf, R_DV, SQ, COLS, NWR, Zf)

                @block.tensor
                def _(pe):
                    pe.wait_ge(s["roped"], 1)
                    for n in range(2 * R_HEADS):
                        h, isk = n // 2, n % 2
                        if n >= 4:
                            pe.wait_ge(s["copied"], n - 3)
                        for t in range(TILES):
                            o = isk * 512 + h * P
                            mm = nc.tensor.transpose(PS[n % 4][:, t * P:(t + 1) * P], PRJ[:, t, o:o + P], ID)
                        mm.then_inc(s["transposed"], 1)

                    def scores(h):
                        if h == 0:
                            pe.wait_ge(s["copied"], 2 * R_HEADS)
                        else:
                            pe.wait_ge(s["masked"], h)
                        nc.tensor.matmul(PS[4][:, 0:128], KTT[:, h, 0:P], QT[:, h, 0:P], start=True, stop=True)
                        nc.tensor.matmul(PS[4][:, 128:384], KTT[:, h, P:2 * P], QT[:, h, P:TOK], start=True, stop=True)
                        nc.tensor.matmul(PS[5][:, 0:256], KTT[:, h, 2 * P:TOK], QT[:, h, P:TOK], start=True, stop=True)\
                            .then_inc(s["scores"], 1)

                    scores(0)
                    for h in range(R_HEADS):
                        pe.wait_ge(s["masked"], h + 1)
                        if h + 1 < R_HEADS:
                            scores(h + 1)
                        if h >= 1:
                            pe.wait_ge(s["evacuated"], h)
                        a = AT[:, h % 2, :]
                        v = [PRJ[:, t, 1024 + h * R_DV:1024 + (h + 1) * R_DV] for t in range(TILES)]
                        nc.tensor.matmul(PS[6][:, 0:256], a[:, 0:128], v[0], start=True, stop=True)
                        for n, t in enumerate(LATENT):
                            dst = PS[6][:, 256:512] if n == 0 else PS[7][:, 0:256]
                            nc.tensor.matmul(dst, a[:, 128 + n * P:256 + n * P], v[1], start=True, stop=False)
                            nc.tensor.matmul(dst, a[:, 384 + n * P:512 + n * P], v[2], start=False, stop=True)
                            for d in range(2):
                                mm = nc.tensor.matmul(PS[n][:, d * 256:(d + 1) * 256], QT[:, h, t * P:(t + 1) * P],
                                                      S0[:, d * R_HEADS + h, :], start=True, stop=True)
                        mm.then_inc(s["out"], 1)
                    pe.wait_ge(s["kd"], 1)
                    for g in range(8):
                        h = g % R_HEADS
                        mm = nc.tensor.matmul(PS[2 + g // 2][:, (g % 2) * 256:(g % 2) * 256 + 256], KD[:, g, :],
                                              PRJ[:, 0, 1024 + h * R_DV:1024 + (h + 1) * R_DV], start=True, stop=True)
                        if g % 2:
                            mm.then_inc(s["states"], 1)

        def stage_diff(l):
            s = signals("loads chain mean root roped transposed copied lamsum lamexp scores maxes exps"
                           " weights turned wt out ocopy stored")
            QT = UP[:, 0:3072].rearrange("p (h n) -> p h n", h=D_HEADS)
            KTT = UP[:, 3072:7168].rearrange("p (h n) -> p h n", h=D_HEADS)
            CK, CVV = UP[:, 7168:8192], UP[:, 8192:9216]
            TMP = RING[:, 0:2048]
            PP = RING[:, 2048:3584].rearrange("p (b a n) -> p b a n", b=2, a=2)
            WW = RING[:, 3584:4352].rearrange("p (b n) -> p b n", b=2)
            WT = RING[:, 4352:5120].rearrange("p (b n) -> p b n", b=2)
            SQ = RING[:, 5120:8192]
            LP = SM[:, 0:256]
            LPR = SM[:, 256:384]
            NWD = SM[:, 384:512]
            MX = SM[:, 512:560].rearrange("p (u a) -> p u a", a=2)
            SS = SM[:, 560:608].rearrange("p (u a) -> p u a", a=2)
            LSUM, NLAM = SM[:, 608:610], SM[:, 610:611]
            COLS = SM[:, 640:664]
            scale = D_HD ** -0.5
            units = [(t, h) for t in range(TILES) for h in range(D_HEADS)]
            U = len(units)

            def span(t):
                return (0, P) if t == 0 else (P, 4 * P)

            with nc.Block(no_gpsimd_drain=True) as block:
                @block.sync
                def _(sp):
                    sp.dma_start(LP, I["diff_lambda"][l].rearrange("a n -> (a n)").partition_broadcast(P)).then_inc(s["loads"], 16)
                    sp.dma_start(NWD, I["diff_norm"][l].partition_broadcast(P)).then_inc(s["loads"], 16)
                    sp.dma_start(CK, I["cache_diff_k"][0, l].rearrange("n h a d -> n (h a d)")).then_inc(s["loads"], 16)
                    sp.dma_start(CVV, I["cache_diff_v"][0, l].rearrange("n h d -> n (h d)")).then_inc(s["loads"], 16)
                    sp.dma_start(O["new_cache_diff_k"][0, l].rearrange("n h a d -> n (h a d)"), PRJ[:, 0, 1024:2048])\
                        .then_inc(s["stored"], 16)
                    sp.dma_start(O["new_cache_diff_v"][0, l].rearrange("n h d -> n (h d)"), PRJ[:, 0, 2048:3072])\
                        .then_inc(s["stored"], 16)
                    sp.wait_ge(s["stored"], 32)

                @block.scalar
                def _(act):
                    act.wait_ge(s["lamsum"], 1)
                    nc.scalar.activation(LSUM, LSUM, ACT.Exp).then_inc(s["lamexp"], 1)
                    for n in range(2 * D_HEADS):
                        h, isk = n // 2, n % 2
                        act.wait_ge(s["transposed"], n + 1)
                        w = 512 if isk else TOK
                        nc.scalar.activation((KTT if isk else QT)[:, h, :], PS[n % 4][:, 0:w], ACT.Copy).then_inc(s["copied"], 1)

                    def exps(u):
                        t, h = units[u]
                        a, b = span(t)
                        act.wait_ge(s["maxes"], u + 1)
                        if u >= 2:
                            act.wait_ge(s["weights"], u - 1)
                        for p in range(2):
                            ins = nc.scalar.activation(PP[:, u % 2, p, 0:b - a], PS[4 + 2 * (u % 2) + p][:, 0:b - a],
                                                       ACT.Exp, bias=MX[:, u, p:p + 1], scale=scale,
                                                       accum_out=SS[:, u, p:p + 1])
                        ins.then_inc(s["exps"], 1)

                    exps(0)
                    for u in range(U):
                        if u + 1 < U:
                            exps(u + 1)
                        t, h = units[u]
                        a, b = span(t)
                        act.wait_ge(s["turned"], u + 1)
                        if u >= 2:
                            act.wait_ge(s["out"], u - 1)
                        nc.scalar.activation(WT[:, u % 2, 0:b - a], PS[u % 2][:, 0:b - a], ACT.Copy).then_inc(s["wt"], 1)
                    act_head_root(act, s, COLS)

                @block.vector
                def _(dve):
                    clear_last_stage(dve, s)
                    c = Chain(dve, s["chain"])
                    dve.wait_ge(s["loads"], 4 * 16)
                    lp = LP.rearrange("p (a b n) -> p a b n", a=2, b=2)
                    c.link(nc.vector.tensor_tensor(LPR.rearrange("p (a n) -> p a n", a=2), lp[:, :, 0, :], lp[:, :, 1, :],
                                                   ALU.mult))
                    nc.vector.tensor_reduce(LSUM, LPR.rearrange("p (a n) -> p a n", a=2), AX, ALU.add).then_inc(s["lamsum"], 1)
                    rope(dve, c, lambda t: PRJ[:, t, 0:2048], ROPD, 32, D_HD, TMP)
                    dve.sem_inc(s["roped"], 1)
                    dve.wait_ge(s["lamexp"], 1)
                    c.link(nc.vector.tensor_tensor(NLAM, LSUM[:, 1:2], LSUM[:, 0:1], ALU.subtract))
                    c.link(nc.vector.tensor_tensor(NLAM, NLAM, LAMC[:, 0:1], ALU.subtract))
                    c.link(nc.vector.tensor_scalar(NWD, NWD, LAMC[:, 1:2], None, ALU.mult))

                    def maxes(u):
                        t, h = units[u]
                        a, b = span(t)
                        dve.wait_ge(s["scores"], u + 1)
                        for p in range(2):
                            c.mark(nc.vector.tensor_reduce(MX[:, u, p:p + 1], PS[4 + 2 * (u % 2) + p][:, 0:b - a], AX, ALU.max))
                        c.sync()
                        nc.vector.tensor_scalar(MX[:, u, :], MX[:, u, :], -scale, None, ALU.mult).then_inc(s["maxes"], 1)

                    def ocopy(u):
                        t, h = units[u]
                        dve.wait_ge(s["out"], u + 1)
                        nc.vector.tensor_copy(H[:, t, h * P:(h + 1) * P], PS[2 + u % 2][:, 0:P]).then_inc(s["ocopy"], 1)

                    maxes(0)
                    for u in range(U):
                        if u + 1 < U:
                            maxes(u + 1)
                        t, h = units[u]
                        a, b = span(t)
                        dve.wait_ge(s["exps"], u + 1)
                        c.link(nc.vector.reciprocal(SS[:, u, :], SS[:, u, :]))
                        c.link(nc.vector.tensor_tensor(SS[:, u, 1:2], SS[:, u, 1:2], NLAM, ALU.mult))
                        pp = PP[:, u % 2]
                        c.link(nc.vector.tensor_scalar(pp[:, 1, 0:b - a], pp[:, 1, 0:b - a], SS[:, u, 1:2], None, ALU.mult))
                        if u >= 2:
                            dve.wait_ge(s["turned"], u - 1)
                        nc.vector.scalar_tensor_tensor(WW[:, u % 2, 0:b - a], pp[:, 0, 0:b - a], SS[:, u, 0:1],
                                                       pp[:, 1, 0:b - a], ALU.mult, ALU.add).then_inc(s["weights"], 1)
                        if u >= 1:
                            ocopy(u - 1)
                    ocopy(U - 1)
                    dve.wait_ge(s["ocopy"], U)
                    dve_head_norm(dve, c, s, Hf, 2 * D_HD, SQ, COLS, NWD, None)

                @block.tensor
                def _(pe):
                    pe.wait_ge(s["roped"], 1)
                    for n in range(2 * D_HEADS):
                        h, isk = n // 2, n % 2
                        if n >= 4:
                            pe.wait_ge(s["copied"], n - 3)
                        for t in range(TILES + isk):
                            o = isk * 1024 + h * P
                            src = PRJ[:, t, o:o + P] if t < TILES else CK[:, h * P:(h + 1) * P]
                            mm = nc.tensor.transpose(PS[n % 4][:, t * P:(t + 1) * P], src, ID)
                        mm.then_inc(s["transposed"], 1)
                    pe.wait_ge(s["copied"], 2 * D_HEADS)

                    def scores(u):
                        t, h = units[u]
                        a, b = span(t)
                        if u >= 2:
                            pe.wait_ge(s["exps"], u - 1)
                        for p in range(2):
                            hp = slice(p * D_HD, (p + 1) * D_HD)
                            mm = nc.tensor.matmul(PS[4 + 2 * (u % 2) + p][:, 0:b - a], QT[hp, h, t * P:(t + 1) * P],
                                                  KTT[hp, h, a:b], start=True, stop=True)
                        mm.then_inc(s["scores"], 1)

                    def turn(u):
                        t, h = units[u]
                        a, b = span(t)
                        pe.wait_ge(s["weights"], u + 1)
                        if u >= 2:
                            pe.wait_ge(s["wt"], u - 1)
                        for n in range((b - a) // P):
                            mm = nc.tensor.transpose(PS[u % 2][:, n * P:(n + 1) * P], WW[:, u % 2, n * P:(n + 1) * P], ID)
                        mm.then_inc(s["turned"], 1)

                    def values(u):
                        t, h = units[u]
                        a, b = span(t)
                        pe.wait_ge(s["wt"], u + 1)
                        if u >= 2:
                            pe.wait_ge(s["ocopy"], u - 1)
                        n = (b - a) // P
                        for k in range(n):
                            tt = a // P + k
                            v = (PRJ[:, tt, 2048 + h * P:2048 + (h + 1) * P] if tt < TILES else CVV[:, h * P:(h + 1) * P])
                            mm = nc.tensor.matmul(PS[2 + u % 2][:, 0:P], WT[:, u % 2, k * P:(k + 1) * P], v,
                                                  start=(k == 0), stop=(k == n - 1))
                        mm.then_inc(s["out"], 1)

                    scores(0)
                    for u in range(U):
                        if u + 1 < U:
                            scores(u + 1)
                        turn(u)
                        if u >= 1:
                            values(u - 1)
                    values(U - 1)

        TMK = UP.rearrange("p (t n) -> p t n", t=TILES)
        YC = BIG[:, 0:QBLK * TOK].rearrange("p (b n) -> p b n", b=QBLK)
        KQT = BIG[:, 0:16 * TOK].rearrange("p (b n) -> p b n", b=16)
        AB = SM[:, 512:608].rearrange("p (t n) -> p t n", t=TILES)

        def stage_gdn_project(l):
            s = signals("free loaded0 loaded1 banks_free done small taps tapcopy filled conv silu zdone zfree"
                           " abload abdone chain pads cbfree")
            loaded = [s["loaded0"], s["loaded1"]]
            XC = UP[:, 0:8 * XC_W].rearrange("p (b n) -> p b n", b=8)
            CB = UP[:, 3200:3200 + 8 * CV_W].rearrange("p (b n) -> p b n", b=8)
            WC = UP[:, 6400:6656]
            TW = UP[:, 6656:6912].rearrange("p (b n) -> p b n", b=2)
            WAB = UP[:, 6912:7168].rearrange("p (k n) -> p k n", k=KT)
            rows = CONV_K * QBLK
            chunks = G_QKV // CHUNK
            zchunks = G_HEADS * G_DV // CHUNK
            taps = I["gdn_conv"].rearrange("l t (b c) -> l (t b) c", c=P)
            with nc.Block(no_gpsimd_drain=True) as block:
                @block.sync
                def _(sp):
                    sp.wait_ge(s["pads"], 1)
                    sp.dma_start(TW[:, 0, :], taps[l, 0:P, :]).then_inc(s["small"], 16)
                    sp.dma_start(TW[0:rows - P, 1, :], taps[l, P:rows, :]).then_inc(s["small"], 16)
                    sp.dma_start(WAB, w_in[l, :, :, COL_GDN_AB:COL_GDN_AB + 32]).then_inc(s["abload"], 16)
                    sp_weights(sp, lambda n: w_in[l, :, :, ds(n * CHUNK + COL_GDN, CHUNK)], chunks, 0, s["free"], loaded)
                    sp_weights(sp, lambda n: w_in[l, :, :, ds(n * CHUNK + COL_GDN_Z, CHUNK)], zchunks, chunks, s["free"], loaded)

                @block.gpsimd
                def _(pool):
                    nc.gpsimd.memset(XC, 0.0)
                    nc.gpsimd.memset(TW, 0.0).then_inc(s["pads"], 1)

                @block.tensor
                def _(pe):
                    pe.sem_inc(s["free"], 2)
                    pe.wait_ge(s["small"], 32)
                    for b in range(2):
                        mm = nc.tensor.transpose(PS[7][:, b * P:(b + 1) * P], TW[:, b, :], ID)
                    mm.then_inc(s["taps"], 1)
                    pe.wait_ge(s["tapcopy"], 1)
                    with pe.Fori(0, chunks // 2) as i:
                        for j in range(2):
                            pe.wait_ge(loaded[j], 16 + 16 * i)
                            for b in range(4):
                                pe.wait_ge(s["banks_free"], 8 * i + 4 * j + b + 1)
                                for k in range(KT):
                                    mm = nc.tensor.matmul(PS[4 * j + b][:, 0:TOK], RW[:, j, k, b * P:(b + 1) * P], HT[:, k, :],
                                                          start=(k == 0), stop=(k == KT - 1))
                                mm.then_inc(s["done"], 1)
                            pe.drain().then_inc(s["free"], 1)
                    pe.wait_ge(s["filled"], 4 * chunks)
                    pe_project(pe, (HT, HT), zchunks, chunks, s["free"], loaded, s["zfree"], s["zdone"])
                    pe.wait_ge(s["abload"], 16)
                    for t in range(TILES):
                        for k in range(KT):
                            mm = nc.tensor.matmul(PS[6][:, t * 32:(t + 1) * 32], HT[:, k, t * P:(t + 1) * P], WAB[:, k, :],
                                                  start=(k == 0), stop=(k == KT - 1))
                    mm.then_inc(s["abdone"], 1)

                @block.scalar
                def _(act):
                    act.sem_inc(s["banks_free"], 8)
                    act.sem_inc(s["silu"], 8)
                    act.sem_inc(s["zfree"], chunks + 2)
                    act.wait_ge(s["taps"], 1)
                    nc.scalar.activation(WC, PS[7][:, 0:2 * P], ACT.Copy).then_inc(s["tapcopy"], 1)
                    with act.Fori(0, chunks // 2) as i:
                        for j in range(2):
                            for b in range(4):
                                n = 4 * j + b
                                act.wait_ge(s["done"], 8 * i + n + 1)
                                act.wait_ge(s["cbfree"], 8 * i + n + 1)
                                nc.scalar.activation(XC[:, n, XC_P:XC_P + SEQ], PS[n][:, 0:SEQ], ACT.Copy)
                                nc.scalar.activation(XC[:, n, XC_S:XC_S + DEC_SEQ], PS[n][:, SEQ:TOK], ACT.Copy)\
                                    .then_inc(s["filled"], 1)
                                act.drain().then_inc(s["banks_free"], 1)
                            for b in range(4):
                                n = 4 * j + b
                                act.wait_ge(s["conv"], 8 * i + n + 1)
                                blk = 8 * i + n
                                nc.scalar.activation(YC[:, blk, 0:SEQ], CB[:, n, 0:SEQ], ACT.Silu)
                                nc.scalar.activation(YC[:, blk, SEQ:TOK], CB[:, n, CV_S:CV_S + DEC_SEQ], ACT.Silu)\
                                    .then_inc(s["silu"], 1)
                    for j in range(zchunks):
                        for t in range(TILES):
                            act.wait_ge(s["zdone"], 3 * j + t + 1)
                            nc.scalar.activation(Z[:, t, j * CHUNK:(j + 1) * CHUNK], PS[3 * j + t], ACT.Silu)
                    act.wait_ge(s["abdone"], 1)
                    nc.scalar.activation(AB, PS[6][:, 0:TILES * 32].rearrange("p (t n) -> p t n", t=TILES), ACT.Copy)

                @block.vector
                def _(dve):
                    clear_last_stage(dve, s)
                    dve.sem_inc(s["cbfree"], 8)
                    c = Chain(dve, s["chain"])
                    dve.wait_ge(s["tapcopy"], 1)
                    with dve.Fori(0, chunks // 2) as i:
                        c.enter(i, 8 * CONV_K)
                        for n in range(8):
                            dve.wait_ge(s["filled"], 8 * i + n + 1)
                            dve.wait_ge(s["silu"], 8 * i + n + 1)
                            for tap in range(CONV_K):
                                w = WC[:, ds(8 * i + n + tap * QBLK, 1)]
                                x = XC[:, n, tap:tap + CV_W]
                                if tap == 0:
                                    ins = nc.vector.tensor_scalar(CB[:, n, :], x, w, None, ALU.mult)
                                else:
                                    ins = nc.vector.scalar_tensor_tensor(CB[:, n, :], x, w, CB[:, n, :], ALU.mult, ALU.add)
                                c.link(ins)
                            dve.sem_inc(s["conv"], 1)
                            dve.sem_inc(s["cbfree"], 1)
                        c.leave(chunks // 2)

        GLG = SM[:, 0:48].rearrange("p (t n) -> p t n", t=TILES)
        BTA = SM[:, 48:96].rearrange("p (t n) -> p t n", t=TILES)
        GC = SM[:, 96:144].rearrange("p (t n) -> p t n", t=TILES)
        EG = SM[:, 144:192].rearrange("p (t n) -> p t n", t=TILES)
        NEGG = SM[:, 192:240].rearrange("p (t n) -> p t n", t=TILES)
        EKD = SM[:, 240:288].rearrange("p (t n) -> p t n", t=TILES)
        EGL = SM[:, 288:336].rearrange("p (t n) -> p t n", t=TILES)

        def stage_gdn_prepare(l):
            s = signals("loads chain turned copied squares root normed back backcopy aexp spin spexp glog sums"
                           " exponents exps beta")
            SQ = RING[:, 0:2048]
            AL, DTB = SM[:, 336:352], SM[:, 352:368]
            T1, T2, T3, T4 = [RING[:, 2048 + 48 * n:2096 + 48 * n].rearrange("p (t n) -> p t n", t=TILES) for n in range(4)]
            T5 = RING[:, 2240:2288].rearrange("p (t n) -> p t n", t=TILES)
            T6 = RING[:, 2288:2336].rearrange("p (t n) -> p t n", t=TILES)
            RN = SM[:, 640:688].rearrange("p (t n) -> p t n", t=TILES)
            with nc.Block(no_gpsimd_drain=True) as block:
                @block.sync
                def _(sp):
                    sp.dma_start(AL, I["gdn_A_log"][l].rearrange("d h -> (d h)").partition_broadcast(P)).then_inc(s["loads"], 16)
                    sp.dma_start(DTB, I["gdn_dt_bias"][l].rearrange("d h -> (d h)").partition_broadcast(P)).then_inc(s["loads"], 16)
                    for d in range(2):
                        sp.dma_start(SST[:, d * G_HEADS:(d + 1) * G_HEADS, :],
                                     I["state_gdn"][0, l, d].rearrange("h k v -> k h v")).then_inc(s["loads"], 16)

                @block.tensor
                def _(pe):
                    for t in range(TILES):
                        for b in range(QBLK // 4):
                            n = t * (QBLK // 4) + b
                            if n >= 4:
                                pe.wait_ge(s["copied"], n - 3)
                            for k in range(4):
                                mm = nc.tensor.transpose(PS[n % 4][:, k * P:(k + 1) * P], YC[:, 4 * b + k, t * P:(t + 1) * P], ID)
                            mm.then_inc(s["turned"], 1)
                    pe.wait_ge(s["glog"], 1)
                    for t in range(TILES):
                        for d in range(2):
                            nc.tensor.matmul(PS[6][:, t * 16 + d * 8:t * 16 + d * 8 + 8], TRI[:, TRI_LO if d else TRI_UP, :],
                                             GLG[:, t, d * 8:d * 8 + 8], start=True, stop=True)
                        mm = nc.tensor.matmul(PS[7][:, t * 16:t * 16 + 16], TRI[:, TRI_ONE, :], GLG[:, t, :], start=True, stop=True)
                    mm.then_inc(s["sums"], 1)
                    pe.wait_ge(s["copied"], TILES * QBLK // 4)
                    for t in range(TILES):
                        pe.wait_ge(s["normed"], t + 1)
                        for b in range(4):
                            n = 4 * t + b
                            if n >= 4:
                                pe.wait_ge(s["backcopy"], n - 3)
                            for k in range(4):
                                g = 4 * b + k
                                mm = nc.tensor.transpose(PS[n % 4][:, k * P:(k + 1) * P], TMK[:, t, g * P:(g + 1) * P], ID)
                            mm.then_inc(s["back"], 1)

                @block.scalar
                def _(act):
                    act.wait_ge(s["loads"], 4 * 16)
                    nc.scalar.activation(AL, AL, ACT.Exp).then_inc(s["aexp"], 1)
                    act.wait_ge(s["spin"], 1)
                    nc.scalar.activation(T2, T2, ACT.Exp).then_inc(s["spexp"], 1)
                    nc.scalar.activation(BTA, AB[:, :, 16:32], ACT.Sigmoid).then_inc(s["beta"], 1)
                    for t in range(TILES):
                        for b in range(QBLK // 4):
                            n = t * (QBLK // 4) + b
                            act.wait_ge(s["turned"], n + 1)
                            nc.scalar.activation(TMK[:, t, 4 * b * P:4 * (b + 1) * P], PS[n % 4], ACT.Copy).then_inc(s["copied"], 1)
                    act.wait_ge(s["squares"], TILES)
                    nc.scalar.activation(RN, RN, ACT.Sqrt).then_inc(s["root"], 1)
                    for n in range(4 * TILES):
                        t, b = divmod(n, 4)
                        act.wait_ge(s["back"], n + 1)
                        nc.scalar.activation(KQT[:, 4 * b:4 * b + 4, t * P:(t + 1) * P],
                                             PS[n % 4].rearrange("p (k n) -> p k n", k=4), ACT.Copy).then_inc(s["backcopy"], 1)
                    act.wait_ge(s["exponents"], 1)
                    nc.scalar.activation(EG, EG, ACT.Exp)
                    nc.scalar.activation(EKD, EKD, ACT.Exp)
                    nc.scalar.activation(EGL, EGL, ACT.Exp).then_inc(s["exps"], 1)

                @block.vector
                def _(dve):
                    clear_last_stage(dve, s)
                    c = Chain(dve, s["chain"])
                    dve.wait_ge(s["loads"], 4 * 16)
                    c.link(nc.vector.tensor_tensor(T1, AB[:, :, 0:16], bc(DTB, TILES), ALU.add))
                    c.link(nc.vector.tensor_scalar(T2, T1, -1.0, None, ALU.mult))
                    nc.vector.tensor_tensor(T2, T1, T2, ALU.min).then_inc(s["spin"], 1)
                    dve.wait_ge(s["spexp"], 1)
                    log1p_parts(dve, c, T2, T3, T4, T5, None)
                    c.link(nc.vector.scalar_tensor_tensor(T1, T1, 0.0, T5, ALU.max, ALU.add))
                    dve.wait_ge(s["aexp"], 1)
                    c.link(nc.vector.tensor_scalar(AL, AL, -1.0, None, ALU.mult))
                    nc.vector.tensor_tensor(GLG, T1, bc(AL, TILES), ALU.mult).then_inc(s["glog"], 1)
                    for t in range(TILES):
                        dve.wait_ge(s["copied"], (t + 1) * QBLK // 4)
                        qk = TMK[:, t, 0:2048]
                        c.link(nc.vector.tensor_tensor(SQ, qk, qk, ALU.mult))
                        c.link(nc.vector.tensor_reduce(RN[:, t, :], SQ.rearrange("p (g n) -> p g n", n=P), AX, ALU.add))
                        nc.vector.tensor_scalar(RN[:, t, :], RN[:, t, :], EPS, None, ALU.add).then_inc(s["squares"], 1)
                    dve.wait_ge(s["root"], 1)
                    c.link(nc.vector.reciprocal(RN, RN))
                    c.link(nc.vector.tensor_scalar(RN[:, :, 0:8], RN[:, :, 0:8], G_DK ** -0.5, None, ALU.mult))
                    for t in range(TILES):
                        qk = TMK[:, t, 0:2048].rearrange("p (g n) -> p g n", n=P)
                        nc.vector.tensor_tensor(qk, qk, bl(RN[:, t, :], P), ALU.mult).then_inc(s["normed"], 1)
                    dve.wait_ge(s["sums"], 1)
                    c.link(nc.vector.tensor_copy(GC, PS[6][:, 0:48].rearrange("p (t n) -> p t n", t=TILES)))
                    c.link(nc.vector.tensor_copy(EGL, PS[7][:, 0:48].rearrange("p (t n) -> p t n", t=TILES)))
                    c.mark(nc.vector.tensor_copy(EG, GC))
                    c.link(nc.vector.tensor_tensor(EKD, EGL, GC, ALU.subtract))
                    dve.sem_inc(s["exponents"], 1)
                    dve.wait_ge(s["exps"], 1)
                    c.link(nc.vector.tensor_scalar(NEGG, EG, -1.0, None, ALU.mult))

        GUNITS = [(0, 0), (0, 1), (1, 0), (2, 1), (2, 0), (1, 1)]

        def stage_gdn(l):
            s = signals("nload chain mean root mg gb dec gram pair expd lv xdone xcopy ydone updated"
                        " turned tcopy ks r un u out kd snew state supd stored tail")
            BUF = RING.rearrange("p (b h n) -> p b h n", b=16, h=4)
            MTS = [[BUF[:, 4 * par + hg] for hg in range(2)] for par in range(2)]
            QDS = [[BUF[:, 4 * par + 2 + hg] for hg in range(2)] for par in range(2)]
            MOS, XSS, TS, TTS = [[BUF[:, 8 + 2 * k + hg] for hg in range(2)] for k in range(4)]
            SQ = RING[:, 0:3072]
            NWG = SM[:, 384:512]
            COLS = SM[:, 688:712]
            U = len(GUNITS)
            LAST = LEVELS - 1

            def bank(n):
                return PS[n].rearrange("p (h n) -> p h n", h=4)

            def latent(v):
                return GUNITS[v][0] > 0

            def ug(v, hg):
                return 2 * v + hg + 1

            def lev(v, n, hg):
                return 2 * LEVELS * v + 2 * n + hg + 1

            def lev1(v, n, hg):
                return 2 * (LEVELS - 1) * v + 2 * (n - 1) + hg + 1

            def lev2(v, n, hg):
                return 2 * (LEVELS - 2) * v + 2 * (n - 1) + hg + 1

            first = {}
            for v, (t, d) in enumerate(GUNITS):
                first.setdefault(t, v)

            with nc.Block(no_gpsimd_drain=True) as block:
                @block.sync
                def _(sp):
                    sp.dma_start(NWG, I["gdn_norm"][l].partition_broadcast(P)).then_inc(s["nload"], 16)
                    for v in range(2):
                        sp.wait_ge(s["snew"], 2 * v + 2)
                        sp.dma_start(O["new_state_gdn"][0, l, GUNITS[v][1]].rearrange("h k v -> k h v"), ZST[v])\
                            .then_inc(s["stored"], 16)
                    sp.wait_ge(s["stored"], 32)

                @block.gpsimd
                def _(pool):
                    def scaled_mask(v, hg):
                        t, d = GUNITS[v]
                        tri = TRI[:, TRI_LO if d else TRI_UP, :]
                        for h in range(4):
                            g = d * 8 + hg * 4 + h
                            ins = nc.gpsimd.tensor_scalar(MTS[v % 2][hg][:, h, :], tri, GLG[:, t, g:g + 1], None, ALU.mult)
                        ins.then_inc(s["mg"], 1)

                    scaled_mask(0, 0)
                    scaled_mask(0, 1)
                    for v, (t, d) in enumerate(GUNITS):
                        for n in range(LEVELS):
                            for hg in range(2):
                                if n == 0:
                                    pool.wait_ge(s["pair"], ug(v, hg))
                                    if v:
                                        pool.wait_ge(s["tail"], ug(v - 1, hg))
                                else:
                                    pool.wait_ge(s["xdone"], lev(v, n - 1, hg))
                                if n == 1:
                                    pool.wait_ge(s["updated"], lev(v, 0, hg))
                                nc.gpsimd.tensor_tensor(MOS[hg], MTS[v % 2][hg], bc(LVL[:, d, n, :], 4), ALU.mult)\
                                    .then_inc(s["lv"], 1)
                            if v + 1 < U and n in (1, 4):
                                scaled_mask(v + 1, int(n == 4))

                @block.tensor
                def _(pe):
                    def sums(v, hg):
                        pe.wait_ge(s["mg"], ug(v, hg))
                        if v or hg:
                            pe.wait_ge(s["pair"], ug(v, hg) - 1)
                        nc.tensor.matmul(PS[6], TRI[:, TRI_ONE, :], MTS[v % 2][hg].rearrange("p h n -> p (h n)"),
                                         start=True, stop=True).then_inc(s["gb"], 1)

                    def grams(v, hg):
                        ts_ = slice(GUNITS[v][0] * P, (GUNITS[v][0] + 1) * P)
                        pe.wait_ge(s["dec"], ug(v, hg))
                        for h in range(4):
                            k = KQT[:, 8 + hg * 4 + h, ts_]
                            nc.tensor.matmul(PS[6][:, h * P:(h + 1) * P], k, k, start=True, stop=True)
                        for h in range(4):
                            mm = nc.tensor.matmul(PS[7][:, h * P:(h + 1) * P], KQT[:, 8 + hg * 4 + h, ts_],
                                                  KQT[:, hg * 4 + h, ts_], start=True, stop=True)
                        mm.then_inc(s["gram"], 1)

                    def four(b, lhs, rhs):
                        for h in range(4):
                            mm = nc.tensor.matmul(PS[b][:, h * P:(h + 1) * P], lhs[:, h, :], rhs[:, h, :],
                                                  start=True, stop=True)
                        return mm

                    for hg in range(2):
                        sums(0, hg)
                        grams(0, hg)
                    for v, (t, d) in enumerate(GUNITS):
                        ts_ = slice(t * P, (t + 1) * P)
                        for n in range(LEVELS):
                            for hg in range(2):
                                pe.wait_ge(s["lv"], lev(v, n, hg))
                                if n == 0:
                                    for h in range(4):
                                        mm = nc.tensor.transpose(PS[hg][:, h * P:(h + 1) * P], MOS[hg][:, h, :], ID)
                                    mm.then_inc(s["xdone"], 1)
                                else:
                                    pe.wait_ge(s["updated"], lev(v, n - 1, hg))
                                    four(hg, MOS[hg], TS[hg]).then_inc(s["xdone"], 1)
                            if n >= 2:
                                for hg in range(2):
                                    for h in range(4):
                                        mm = nc.tensor.transpose(PS[4 + hg][:, h * P:(h + 1) * P], TS[hg][:, h, :], ID)
                                    mm.then_inc(s["turned"], 1)
                            if n:
                                for hg in range(2):
                                    pe.wait_ge(s["xcopy"], lev1(v, n, hg))
                                    if n >= 2:
                                        pe.wait_ge(s["tcopy"], lev2(v, n - 1, hg))
                                    if n < LAST:
                                        four(2 + hg, TTS[hg], XSS[hg]).then_inc(s["ydone"], 1)
                                    else:
                                        four(2 + hg, XSS[hg], TTS[hg]).then_inc(s["ydone"], 1)
                            if v + 1 < U:
                                if n in (1, 4):
                                    sums(v + 1, int(n == 4))
                                if n in (2, 5):
                                    grams(v + 1, int(n == 5))
                        if latent(v):
                            for hg in range(2):
                                if v >= 4:
                                    pe.wait_ge(s["state"], ug(v - 4, hg))
                                for h in range(4):
                                    hh = hg * 4 + h
                                    mm = nc.tensor.matmul(PS[hg][:, h * P:(h + 1) * P], KQT[:, 8 + hh, ts_],
                                                          SST[:, d * 8 + hh, :], start=True, stop=True)
                                mm.then_inc(s["ks"], 1)
                        for hg in range(2):
                            pe.wait_ge(s["updated"], lev(v, LAST, hg))
                            pe.wait_ge(s["r"], ug(v, hg))
                            four(2 + hg, TTS[hg], MOS[hg]).then_inc(s["un"], 1)
                        for hg in range(2):
                            pe.wait_ge(s["u"], ug(v, hg))
                            mm = four(4 + hg, QDS[v % 2][hg], XSS[hg])
                            if latent(v):
                                for h in range(4):
                                    hh = hg * 4 + h
                                    mm = nc.tensor.matmul(PS[2 + hg][:, h * P:(h + 1) * P], KQT[:, hh, ts_],
                                                          SST[:, d * 8 + hh, :], start=True, stop=True)
                            mm.then_inc(s["out"], 1)
                            pe.wait_ge(s["kd"], ug(v, hg))
                            four(hg, TS[hg], XSS[hg]).then_inc(s["supd"], 1)

                @block.scalar
                def _(act):
                    def exps(v, hg):
                        act.wait_ge(s["dec"], ug(v, hg))
                        q = QDS[v % 2][hg]
                        nc.scalar.activation(q, q, ACT.Exp).then_inc(s["expd"], 1)

                    exps(0, 0)
                    exps(0, 1)
                    for v, (t, d) in enumerate(GUNITS):
                        for n in range(1, LEVELS):
                            for hg in range(2):
                                act.wait_ge(s["xdone"], lev(v, n, hg))
                                nc.scalar.activation(XSS[hg], bank(hg), ACT.Copy).then_inc(s["xcopy"], 1)
                            if n >= 2:
                                for hg in range(2):
                                    act.wait_ge(s["turned"], lev2(v, n - 1, hg))
                                    nc.scalar.activation(TTS[hg], bank(4 + hg), ACT.Copy).then_inc(s["tcopy"], 1)
                            if v + 1 < U and n in (2, 5):
                                exps(v + 1, int(n == 5))
                        if t == 0:
                            for hg in range(2):
                                act.wait_ge(s["supd"], ug(v, hg))
                                nc.scalar.activation(ZST[v][:, hg * 4:hg * 4 + 4, :], bank(hg), ACT.Copy)\
                                    .then_inc(s["snew"], 1)
                    act_head_root(act, s, COLS)

                @block.vector
                def _(dve):
                    clear_last_stage(dve, s)
                    c = Chain(dve, s["chain"])
                    idb = bc(ID, 4)

                    def exponents(v, hg):
                        t, d = GUNITS[v]
                        dve.wait_ge(s["gb"], ug(v, hg))
                        for h in range(4):
                            g = d * 8 + hg * 4 + h
                            ins = nc.vector.tensor_scalar(QDS[v % 2][hg][:, h, :], bank(6)[:, h, :], GC[:, t, g:g + 1],
                                                          0.0, ALU.subtract, ALU.min)
                        ins.then_inc(s["dec"], 1)

                    def pairs(v, hg):
                        t, d = GUNITS[v]
                        incl = bc(TRI[:, TRI_LO if d else TRI_UP, :], 4)
                        q, m = QDS[v % 2][hg], MTS[v % 2][hg]
                        dve.wait_ge(s["expd"], ug(v, hg))
                        dve.wait_ge(s["gram"], ug(v, hg))
                        c.link(nc.vector.tensor_tensor(q, q, incl, ALU.mult))
                        c.link(nc.vector.tensor_tensor(m, q, bank(6), ALU.mult))
                        c.mark(nc.vector.tensor_tensor(q, q, bank(7), ALU.mult))
                        nc.vector.tensor_tensor(m, m, bl(BTA[:, t, d * 8 + hg * 4:d * 8 + hg * 4 + 4], P), ALU.mult)\
                            .then_inc(s["pair"], 1)

                    for hg in range(2):
                        exponents(0, hg)
                        pairs(0, hg)
                    for v, (t, d) in enumerate(GUNITS):
                        gss = [slice(d * 8 + hg * 4, d * 8 + hg * 4 + 4) for hg in range(2)]
                        for n in range(LEVELS):
                            for hg in range(2):
                                T, TT = TS[hg], TTS[hg]
                                if n == 0:
                                    dve.wait_ge(s["xdone"], lev(v, 0, hg))
                                    nc.vector.tensor_tensor(TT, idb, MOS[hg], ALU.subtract)
                                    nc.vector.tensor_tensor(T, idb, bank(hg), ALU.subtract).then_inc(s["updated"], 1)
                                else:
                                    dve.wait_ge(s["ydone"], lev1(v, n, hg))
                                    dst = T if n < LAST else TT
                                    nc.vector.tensor_tensor(dst, dst, bank(2 + hg), ALU.subtract).then_inc(s["updated"], 1)
                            if v + 1 < U:
                                if n in (1, 4):
                                    exponents(v + 1, int(n == 4))
                                if n == 3:
                                    pairs(v + 1, 0)
                        for hg in range(2):
                            MO = MOS[hg]
                            vv = TMK[:, t, 2048 + hg * 512:2048 + hg * 512 + 512].rearrange("p (h n) -> p h n", h=4)
                            kk = TMK[:, t, 1024 + hg * 512:1024 + hg * 512 + 512].rearrange("p (h n) -> p h n", h=4)
                            if latent(v):
                                dve.wait_ge(s["ks"], ug(v - 2, hg))
                                c.link(nc.vector.tensor_tensor(MO, bank(hg), bl(EG[:, t, gss[hg]], P), ALU.mult))
                                nc.vector.tensor_tensor(MO, vv, MO, ALU.subtract).then_inc(s["r"], 1)
                            else:
                                nc.vector.tensor_copy(MO, vv).then_inc(s["r"], 1)
                            nc.vector.tensor_tensor(TS[hg], kk, bl(EKD[:, t, gss[hg]], P), ALU.mult).then_inc(s["kd"], 1)
                        for hg in range(2):
                            dve.wait_ge(s["un"], ug(v, hg))
                            nc.vector.tensor_tensor(XSS[hg], bank(2 + hg), bl(BTA[:, t, gss[hg]], P), ALU.mult)\
                                .then_inc(s["u"], 1)
                        if v + 1 < U:
                            pairs(v + 1, 1)
                        for hg in range(2):
                            MO = MOS[hg]
                            oo = H[:, t, hg * 512:hg * 512 + 512].rearrange("p (h n) -> p h n", h=4)
                            dve.wait_ge(s["out"], ug(v, hg))
                            if first[t] == v:
                                c.mark(nc.vector.tensor_copy(oo, bank(4 + hg)))
                            else:
                                c.mark(nc.vector.tensor_tensor(oo, oo, bank(4 + hg), ALU.add))
                            if latent(v):
                                c.link(nc.vector.tensor_tensor(MO, bank(2 + hg), bl(EG[:, t, gss[hg]], P), ALU.mult))
                                c.mark(nc.vector.tensor_tensor(oo, oo, MO, ALU.add))
                                dve.wait_ge(s["supd"], ug(v, hg))
                                st = SST[:, d * 8 + hg * 4:d * 8 + hg * 4 + 4, :]
                                c.link(nc.vector.tensor_tensor(st, st, bl(EGL[:, t, gss[hg]], P), ALU.mult))
                                nc.vector.tensor_tensor(st, st, bank(hg), ALU.add).then_inc(s["state"], 1)
                                dve.wait_ge(s["state"], ug(v - 2, hg))
                            else:
                                c.sync()
                                dve.wait_ge(s["snew"], ug(v, hg))
                            dve.sem_inc(s["tail"], 1)
                    dve.wait_ge(s["nload"], 16)
                    dve_head_norm(dve, c, s, Hf, G_DV, SQ, COLS, NWG, Zf)

        ZB = sb("gdn_final_states", 2 * G_HEADS * G_DV)
        ZST = [ZB[:, v * 1024:(v + 1) * 1024].rearrange("p (h n) -> p h n", h=8) for v in range(2)]

        def stage_merge(l, n_branch):
            s = signals("free loaded0 loaded1 banks_free done turned free2 ready gate used chain")
            loaded = [s["loaded0"], s["loaded1"]]
            GT = BIG[:, 0:TILES * CHUNK].rearrange("p (t n) -> p t n", t=TILES)
            TM = BIG[:, 1536:3072].rearrange("p (t n) -> p t n", t=TILES)
            wb = I["w_branch"].rearrange("l b (k p) n -> l b p k n", p=P)
            chunks = D // CHUNK
            col = COL_GATES + n_branch * D
            with nc.Block(no_gpsimd_drain=True) as block:
                @block.sync
                def _(sp):
                    with sp.Fori(0, chunks) as i:
                        sp.wait_ge(s["free"], 2 * i + 1)
                        sp.dma_start(RW[:, 0], w_in[l, :, :, ds(i * CHUNK + col, CHUNK)]).then_inc(loaded[0], 16)
                        sp.wait_ge(s["free"], 2 * i + 2)
                        sp.dma_start(RW[:, 1], wb[l, n_branch, :, :, ds(i * CHUNK, CHUNK)]).then_inc(loaded[1], 16)

                @block.tensor
                def _(pe):
                    pe.sem_inc(s["free"], 2)
                    pe_transpose_tokens(pe, H, s["ready"], s["free2"], s["turned"])
                    pe.wait_ge(s["free2"], 2 * TILES)
                    pe_project(pe, (HT, OT_), 2 * chunks, 0, s["free"], loaded, s["banks_free"], s["done"])

                @block.scalar
                def _(act):
                    act_transposed(act, OT_, s["turned"], s["free2"])
                    with act.Fori(0, chunks) as i:
                        act.wait_ge(s["used"], i + 1)
                        for t in range(TILES):
                            act.wait_ge(s["done"], 6 * i + t + 1)
                            nc.scalar.activation(GT[:, t, :], PS[t], ACT.Sigmoid).then_inc(s["gate"], 1)

                @block.vector
                def _(dve):
                    clear_last_stage(dve, s)
                    c = Chain(dve, s["chain"])
                    dve.sem_inc(s["ready"], TILES)
                    dve.sem_inc(s["banks_free"], 2)
                    dve.sem_inc(s["used"], 1)
                    with dve.Fori(0, chunks) as i:
                        c.enter(i, TILES if n_branch == 0 else 2 * TILES)
                        dve.wait_ge(s["gate"], 3 * i + 3)
                        dve.wait_ge(s["done"], 6 * i + 6)
                        for t in range(TILES):
                            dst = MACC[:, t, ds(i * CHUNK, CHUNK)]
                            if n_branch == 0:
                                c.mark(nc.vector.tensor_tensor(dst, GT[:, t, :], PS[3 + t], ALU.mult))
                            else:
                                c.link(nc.vector.tensor_tensor(TM[:, t, :], GT[:, t, :], PS[3 + t], ALU.mult))
                                c.mark(nc.vector.tensor_tensor(dst, dst, TM[:, t, :], ALU.add))
                        c.sync()
                        dve.sem_inc(s["banks_free"], 2)
                        dve.sem_inc(s["used"], 1)
                        c.leave(chunks)

        def stage_out(l):
            s = signals("free loaded0 loaded1 banks_free done turned free2 ready loads chain")
            loaded = [s["loaded0"], s["loaded1"]]
            G1 = BIG[:, 0:2 * D].rearrange("p (g n) -> p g n", g=2)
            TM = BIG[:, 2 * D:2 * D + 1536].rearrange("p (t n) -> p t n", t=TILES)
            wo = I["w_out"].rearrange("l (k p) n -> l p k n", p=P)
            chunks = D // CHUNK
            with nc.Block(no_gpsimd_drain=True) as block:
                @block.sync
                def _(sp):
                    for g in range(2):
                        sp.dma_start(G1[:, g, :], modd[g, 2 * D:3 * D].partition_broadcast(P)).then_inc(s["loads"], 16)
                    sp_weights(sp, lambda n: wo[l, :, :, ds(n * CHUNK, CHUNK)], chunks, 0, s["free"], loaded)

                @block.tensor
                def _(pe):
                    pe.sem_inc(s["free"], 2)
                    pe_transpose_tokens(pe, MACC, s["ready"], s["free2"], s["turned"])
                    pe.wait_ge(s["free2"], 2 * TILES)
                    pe_project(pe, (OT_, OT_), chunks, 0, s["free"], loaded, s["banks_free"], s["done"])

                @block.scalar
                def _(act):
                    act_transposed(act, OT_, s["turned"], s["free2"])

                @block.vector
                def _(dve):
                    clear_last_stage(dve, s)
                    c = Chain(dve, s["chain"])
                    dve.sem_inc(s["ready"], TILES)
                    dve.sem_inc(s["banks_free"], 2)
                    dve.wait_ge(s["loads"], 32)
                    for j in range(chunks):
                        cs = slice(j * CHUNK, (j + 1) * CHUNK)
                        for t in range(TILES):
                            dve.wait_ge(s["done"], 3 * j + t + 1)
                            c.link(nc.vector.tensor_tensor(TM[:, t, :], PS[3 * j + t], G1[:, int(t > 0), cs], ALU.mult))
                            c.mark(nc.vector.tensor_tensor(X[:, t, cs], X[:, t, cs], TM[:, t, :], ALU.add))
                    c.sync()

        SC = RING[:, 0:6144].rearrange("p (t n) -> p t n", t=TILES)
        OH = RING[:, 6144:8192]
        QP = BIG[:, 6144:12288].rearrange("p (b n) -> p b n", b=16)
        IDX = Zf[:, 384:768].bitcast(U32).rearrange("p (t n) -> p t n", t=TILES)
        GATE = Zf[:, 768:1152].rearrange("p (t n) -> p t n", t=TILES)
        DOTS = Zf[:, 1152:1536].rearrange("p (t n) -> p t n", t=TILES)
        NB = 8
        IDS = Zf[:, 1536:1536 + 2 * NB].bitcast(U32)
        DST = Zf[:, 1600:1600 + 2 * NB]
        SSF = SST.rearrange("p g n -> p (g n)")
        SCW, SCX = SSF[:, 0:256], SSF[:, 256:384]
        V2 = SSF[:, 384:416].rearrange("p (a n) -> p a n", a=2)
        I2 = SSF[:, 416:448].bitcast(U32)
        CAND, CANX = SSF[:, 448:704], SSF[:, 704:960]
        BV1, BI1 = SSF[:, 960:976], SSF[:, 976:992].bitcast(U32)
        I16F = SSF[:, 992:1248]
        BV = SSF[:, 1248:1376]
        BI, BA = SSF[:, 1376:1504].bitcast(U32), SSF[:, 1504:1632].bitcast(U32)
        BF = SSF[:, 1632:1760]
        SEL = SSF[:, 1760:2016].rearrange("p (a n) -> p a n", a=2)
        RS8 = SSF[:, 2016:2024]

        TOP_PASS = 1 + 10 + 1 + 1 + 5 + 2

        def top_pass(dve, c, tick, t, i):

            def step(ins):
                c.link(ins)
                dve.sem_inc(tick, 1)

            def top16(vals, work, v16, i16):
                step(nc.vector.max(v16[:, 0:8], vals))
                step(nc.vector.max_index(i16[:, 0:8], v16[:, 0:8], vals))
                step(nc.vector.match_replace(work, v16[:, 0:8], vals, BIGNEG))
                step(nc.vector.max(v16[:, 8:16], work))
                step(nc.vector.max_index(i16[:, 8:16], v16[:, 8:16], work))

            step(nc.vector.tensor_copy(SCW, SC[:, t, ds(256 * i, 256)]))
            for half in range(2):
                top16(SCW[:, half * P:(half + 1) * P], SCX, V2[:, half, :], I2[:, half * TOPK:(half + 1) * TOPK])
            c.mark(nc.vector.tensor_copy(I16F[:, ds(2 * TOPK * i, 2 * TOPK)], I2))
            step(nc.vector.tensor_tensor(CAND.rearrange("p (a b) -> p a b", a=TOPK), bl(V2[:, 0, :], TOPK),
                                         bc(V2[:, 1, :], TOPK), ALU.add))
            top16(CAND, CANX, BV1, BI1)
            c.mark(nc.vector.tensor_copy(BV[:, ds(TOPK * i, TOPK)], BV1))
            c.link(nc.vector.tensor_copy(BI[:, ds(TOPK * i, TOPK)], BI1))

        def pick(dve, c, s, t):
            i4 = I16F.rearrange("p (h a n) -> p h a n", h=8, a=2)
            oh = OH.rearrange("p (h k a) -> p h k a", h=8, k=TOPK)
            g3 = GATE[:, t, :].rearrange("p (h k) -> p h k", h=8)
            b3 = BV.rearrange("p (h k) -> p h k", h=8)
            nc.vector.tensor_tensor(g3, b3, b3[:, :, 0:1].to_broadcast([P, 8, TOPK]), ALU.subtract).then_inc(s["dif"], 1)
            for half in range(2):
                if half == 0:
                    c.link(nc.vector.tensor_scalar(BA, BI, 4, None, ALU.logical_shift_right))
                else:
                    c.link(nc.vector.tensor_scalar(BA, BI, TOPK - 1, None, ALU.bitwise_and))
                c.link(nc.vector.tensor_copy(BF, BA))
                bf = BF.rearrange("p (h k) -> p h k", h=8).unsqueeze(3).to_broadcast([P, 8, TOPK, TOPK])
                io = POS[:, POS_IOTA:POS_IOTA + TOPK].unsqueeze(1).unsqueeze(1).to_broadcast([P, 8, TOPK, TOPK])
                c.link(nc.vector.tensor_tensor(oh, bf, io, ALU.is_equal))
                c.link(nc.vector.tensor_tensor(oh, oh, i4[:, :, half, :].unsqueeze(2).to_broadcast([P, 8, TOPK, TOPK]),
                                               ALU.mult))
                c.link(nc.vector.tensor_reduce(SEL[:, half, :], OH.rearrange("p (g a) -> p g a", a=TOPK), AX, ALU.add))
            c.link(nc.vector.tensor_scalar(SEL[:, 0, :], SEL[:, 0, :], float(N_KEYS), LAMC[:, 2:3], ALU.mult, ALU.add))
            nc.vector.tensor_tensor(IDX[:, t, :], SEL[:, 0, :], SEL[:, 1, :], ALU.add).then_inc(s["rows"], 1)
            dve.wait_ge(s["exp"], t + 1)
            c.link(nc.vector.tensor_reduce(RS8, g3, AX, ALU.add))
            c.link(nc.vector.reciprocal(RS8, RS8))
            c.link(nc.vector.tensor_tensor(g3, g3, bl(RS8, TOPK), ALU.mult))

        def stage_route(l):
            s = signals("free loaded0 loaded1 banks_free done filled keys kturned kcopy scored scopy")
            loaded = [s["loaded0"], s["loaded1"]]
            KY = BIG[:, 12288:12544].rearrange("p (a n) -> p a n", a=2)
            KYT = BIG[:, 12544:12800].rearrange("p (a n) -> p a n", a=2)
            wq = I["peer_wq"].rearrange("l (k p) n -> l p k n", p=P)
            chunks = PEER_HEADS * PEER_DQ // CHUNK
            with nc.Block(no_gpsimd_drain=True) as block:
                @block.sync
                def _(sp):
                    sp.dma_start(KY, I["peer_keys"][l].rearrange("a n d -> n a d")).then_inc(s["keys"], 16)
                    sp_weights(sp, lambda n: wq[l, :, :, ds(n * CHUNK, CHUNK)], chunks, 0, s["free"], loaded)

                @block.tensor
                def _(pe):
                    pe.sem_inc(s["free"], 2)
                    pe.wait_ge(s["keys"], 16)
                    for a in range(2):
                        mm = nc.tensor.transpose(PS[7][:, a * P:(a + 1) * P], KY[:, a, :], ID)
                    mm.then_inc(s["kturned"], 1)
                    pe.wait_ge(s["kcopy"], 1)
                    with pe.Fori(0, chunks // 2) as i:
                        for j in range(2):
                            pe.wait_ge(loaded[j], 16 + 16 * i)
                            for b in range(4):
                                pe.wait_ge(s["banks_free"], 8 * i + 4 * j + b + 1)
                                for k in range(KT):
                                    mm = nc.tensor.matmul(PS[4 * j + b][:, 0:TOK], RW[:, j, k, b * P:(b + 1) * P], HT[:, k, :],
                                                          start=(k == 0), stop=(k == KT - 1))
                                mm.then_inc(s["done"], 1)
                            pe.drain().then_inc(s["free"], 1)
                    pe.wait_ge(s["filled"], 4 * chunks)
                    for n in range(4 * TILES):
                        t, b = divmod(n, 4)
                        if n >= 8:
                            pe.wait_ge(s["scopy"], n - 7)
                        for k in range(4):
                            g = 4 * b + k
                            mm = nc.tensor.matmul(PS[n % 8][:, k * P:(k + 1) * P], QP[:, g, t * P:(t + 1) * P],
                                                  KYT[:, g % 2, :], start=True, stop=True)
                        mm.then_inc(s["scored"], 1)

                @block.scalar
                def _(act):
                    act.sem_inc(s["banks_free"], 8)
                    act.wait_ge(s["kturned"], 1)
                    nc.scalar.activation(KYT, PS[7][:, 0:256].rearrange("p (a n) -> p a n", a=2), ACT.Copy).then_inc(s["kcopy"], 1)
                    with act.Fori(0, chunks // 2) as i:
                        for n in range(8):
                            act.wait_ge(s["done"], 8 * i + n + 1)
                            nc.scalar.activation(QP[:, 8 * i + n, :], PS[n][:, 0:TOK], ACT.Copy).then_inc(s["filled"], 1)
                            act.drain().then_inc(s["banks_free"], 1)
                    for n in range(4 * TILES):
                        t, b = divmod(n, 4)
                        act.wait_ge(s["scored"], n + 1)
                        nc.scalar.activation(SC[:, t, b * 512:(b + 1) * 512], PS[n % 8], ACT.Copy).then_inc(s["scopy"], 1)

                @block.vector
                def _(dve):
                    clear_last_stage(dve, s)

        def stage_experts(l):
            s = signals("staged chain dots acted used_low used_high_dot used_high_sum started loads tick dif exp rows"
                        " weights diag diag_used summed zeros")
            per_tile = SLOTS // (2 * NB)
            seen = 16 * 2 * TILES * per_tile * l
            UB = BIG[:, 0:2 * NB * D].rearrange("p (b n) -> p b n", b=2 * NB)
            JUNK = BIG[:, 2 * NB * D:2 * NB * D + D]
            DIAG = BIG[:, 2 * NB * D + D:2 * NB * D + 2 * D].rearrange("p (b n) -> p b n", b=NB)
            ZERO = SM[:, 0:P]
            Y = HT.rearrange("p k n -> p (k n)").rearrange("p (t n) -> p t n", t=TILES)
            G2 = MACC.rearrange("p t n -> p (t n)")[:, 0:2 * D].rearrange("p (g n) -> p g n", g=2)
            tables = [I["peer_u"].rearrange("l e d -> (l e) d"), I["peer_v"].rearrange("l e d -> (l e) d")]
            with nc.Block(no_gpsimd_drain=True) as block:
                @block.sync
                def _(sp):
                    for g in range(2):
                        sp.dma_start(G2[:, g, :], modd[g, 5 * D:6 * D].partition_broadcast(P)).then_inc(s["loads"], 16)

                @block.gpsimd
                def _(pool):
                    for t in range(TILES):
                        pool.wait_ge(s["rows"], t + 1)
                        for phase in range(2):
                            with pool.Fori(0, per_tile) as i:
                                pos = i + (2 * t + phase) * per_tile
                                for half in range(2):
                                    if half == 0:
                                        pool.wait_ge(s["used_low"], pos + 1)
                                    else:
                                        pool.wait_ge(s["used_high_dot"], per_tile * (t + phase) + 1 + (0 if phase else i))
                                        pool.wait_ge(s["used_high_sum"], per_tile * t + 1 + (i if phase else 0))
                                    nc.gpsimd.tensor_copy(IDS[:, half * NB:(half + 1) * NB],
                                                          IDX[:, t, ds(2 * NB * i + half * NB, NB)]).then_inc(s["staged"], 1)
                                    pool.wait_ge(s["staged"], 2 * pos + half + 1)
                                    pool.sem_inc(s["started"], 1)
                                    for n in range(NB):
                                        b = half * NB + n
                                        nc.gpsimd.indirect_dma_start(
                                            out=UB[:, b, :], out_offset=None, in_=tables[phase],
                                            in_offset=bass.IndirectOffsetOnAxis(ap=IDS[:, b:b + 1], axis=0))\
                                            .then_inc(got[b], 16)

                @block.tensor
                def _(pe):
                    pe.sem_inc(s["used_high_sum"], 1)
                    pe.sem_inc(s["diag_used"], NB)
                    pe.wait_ge(s["zeros"], 1)
                    for t in range(TILES):
                        landed = seen + 16 * (2 * t + 1) * per_tile
                        for b in range(2):
                            nc.tensor.matmul(PS[2 * t + b], ZERO, H[:, t, b * 512:(b + 1) * 512], start=True, stop=False)
                        with pe.Fori(0, per_tile) as i:
                            for n in range(NB):
                                pe.wait_ge(s["diag"], NB * per_tile * t + NB * i + n + 1)
                                pe.wait_ge(got[NB + n], landed + 16 * i + 16)
                                for b in range(2):
                                    mm = nc.tensor.matmul(PS[2 * t + b], DIAG[:, n, :], UB[:, NB + n, b * 512:(b + 1) * 512],
                                                          start=False, stop=False)
                                mm.then_inc(s["diag_used"], 1)
                            pe.drain().then_inc(s["used_high_sum"], 1)
                        for b in range(2):
                            mm = nc.tensor.matmul(PS[2 * t + b], ZERO, H[:, t, b * 512:(b + 1) * 512], start=False, stop=True)
                        mm.then_inc(s["summed"], 1)

                @block.scalar
                def _(act):
                    def gates(t):
                        act.wait_ge(s["dif"], t + 1)
                        nc.scalar.activation(GATE[:, t, :], GATE[:, t, :], ACT.Exp).then_inc(s["exp"], 1)

                    gates(0)
                    for t in range(TILES):
                        act.wait_ge(s["dots"], t + 1)
                        nc.scalar.activation(DOTS[:, t, :], DOTS[:, t, :], ACT.Gelu).then_inc(s["acted"], 1)
                        act.wait_ge(s["weights"], t + 1)
                        for part in range(2):
                            with act.Fori(part * per_tile // 2, (part + 1) * per_tile // 2) as i:
                                for n in range(NB):
                                    act.wait_ge(s["diag_used"], NB * per_tile * t + NB * i + n + 1)
                                    w = DOTS[:, t, ds(2 * NB * i + NB + n, 1)]
                                    nc.scalar.activation(DIAG[:, n, :], ID, ACT.Copy, scale=w).then_inc(s["diag"], 1)
                            if part == 0 and t + 1 < TILES:
                                gates(t + 1)

                @block.vector
                def _(dve):
                    clear_last_stage(dve, s)
                    c = Chain(dve, s["chain"])
                    dve.sem_inc(s["used_low"], 1)
                    dve.sem_inc(s["used_high_dot"], 1)
                    nc.vector.memset(ZERO, 0.0).then_inc(s["zeros"], 1)
                    with dve.Fori(0, PEER_HEADS) as i:
                        c.enter(i, TOP_PASS)
                        top_pass(dve, c, s["tick"], 0, i)
                        c.leave(PEER_HEADS)
                    pick(dve, c, s, 0)
                    c.link(nc.vector.memset(Y, 0.0))
                    for t in range(TILES):
                        landed = seen + 16 * 2 * t * per_tile
                        with dve.Fori(0, per_tile) as i:
                            c.enter(i, 2 * (NB + 1))
                            for half in range(2):
                                for n in range(NB):
                                    b = half * NB + n
                                    dve.wait_ge(got[b], landed + 16 * i + 16)
                                    c.link(nc.vector.scalar_tensor_tensor(JUNK, UB[:, b, :], 1.0, H[:, t, :], ALU.mult, ALU.mult,
                                                                          accum_out=DST[:, b:b + 1]))
                                dve.sem_inc(s["used_high_dot" if half else "used_low"], 1)
                                c.mark(nc.vector.tensor_copy(DOTS[:, t, ds(2 * NB * i + half * NB, NB)],
                                                             DST[:, half * NB:(half + 1) * NB]))
                            c.leave(per_tile)
                        c.sync()
                        dve.sem_inc(s["dots"], 1)
                        dve.wait_ge(s["acted"], t + 1)
                        c.link(nc.vector.tensor_tensor(DOTS[:, t, :], DOTS[:, t, :], GATE[:, t, :], ALU.mult))
                        dve.sem_inc(s["weights"], 1)
                        landed = seen + 16 * (2 * t + 1) * per_tile
                        for part in range(2):
                            choose = part == 0 and t + 1 < TILES
                            with dve.Fori(0, per_tile // 2) as i:
                                c.enter(i, NB + 1 + (2 * TOP_PASS if choose else 0))
                                c.link(nc.vector.tensor_copy(DST[:, 0:NB], DOTS[:, t, ds(2 * NB * i + part * SLOTS // 2, NB)]))
                                for n in range(NB):
                                    dve.wait_ge(got[n], landed + 16 * i + 16 + part * 16 * per_tile // 2)
                                    c.link(nc.vector.scalar_tensor_tensor(Y[:, t, :], UB[:, n, :], DST[:, n:n + 1], Y[:, t, :],
                                                                          ALU.mult, ALU.add))
                                dve.sem_inc(s["used_low"], 1)
                                if choose:
                                    for k in range(2):
                                        top_pass(dve, c, s["tick"], t + 1, 2 * i + k)
                                c.leave(per_tile // 2)
                            if choose:
                                pick(dve, c, s, t + 1)
                    dve.wait_ge(s["loads"], 32)
                    for t in range(TILES):
                        dve.wait_ge(s["summed"], t + 1)
                        for b in range(2):
                            yb = Y[:, t, b * 512:(b + 1) * 512]
                            c.mark(nc.vector.tensor_tensor(yb, yb, PS[2 * t + b], ALU.add))
                        c.sync()
                        c.link(nc.vector.tensor_tensor(Y[:, t, :], Y[:, t, :], G2[:, int(t > 0), :], ALU.mult))
                        c.link(nc.vector.tensor_tensor(X[:, t, :], X[:, t, :], Y[:, t, :], ALU.add))

        with nc.Fori(0, DEPTH) as l:
            stage_mod(l)
            stage_norm(l, 0)
            stage_project(l, [(COL_RET, 4, PRJ, ACT.Copy), (COL_RET_G, 2, Z, ACT.Silu)])
            stage_retention(l)
            stage_merge(l, 0)
            stage_project(l, [(COL_DIFF, 6, PRJ, ACT.Copy)])
            stage_diff(l)
            stage_merge(l, 1)
            stage_gdn_project(l)
            stage_gdn_prepare(l)
            stage_gdn(l)
            stage_merge(l, 2)
            stage_out(l)
            stage_norm(l, 1)
            stage_route(l)
            stage_experts(l)

        s = signals("loads squares mean root chain ready stored")
        with nc.Block(no_gpsimd_drain=True) as block:
            @block.sync
            def _(sp):
                sp.dma_start(UP[:, 0:D], I["norm_f_w"].partition_broadcast(P)).then_inc(s["loads"], 16)
                sp.wait_ge(s["ready"], 1)
                sp.dma_start(O["y_prompt"][0], H[:, 0, :]).then_inc(s["stored"], 16)
                sp.wait_ge(s["ready"], 3)
                sp.dma_start(O["y_sample"][0].rearrange("(t p) n -> p t n", p=P), H[:, 1:3, :]).then_inc(s["stored"], 16)
                sp.wait_ge(s["stored"], 32)

            @block.scalar
            def _(act):
                for t in range(TILES):
                    nc.scalar.activation(BIG[:, t * D:(t + 1) * D], X[:, t, :], ACT.Square, accum_out=SM[:, t:t + 1])\
                        .then_inc(s["squares"], 1)
                act.wait_ge(s["mean"], 1)
                nc.scalar.activation(SM[:, 4:7], SM[:, 0:3], ACT.Sqrt).then_inc(s["root"], 1)

            @block.vector
            def _(dve):
                c = Chain(dve, s["chain"])
                dve.wait_ge(s["squares"], TILES)
                nc.vector.tensor_scalar(SM[:, 0:3], SM[:, 0:3], 1.0 / D, EPS, ALU.mult, ALU.add).then_inc(s["mean"], 1)
                dve.wait_ge(s["root"], 1)
                c.link(nc.vector.reciprocal(SM[:, 4:7], SM[:, 4:7]))
                dve.wait_ge(s["loads"], 16)
                for t in range(TILES):
                    nc.vector.scalar_tensor_tensor(H[:, t, :], X[:, t, :], SM[:, 4 + t:5 + t], UP[:, 0:D],
                                                   ALU.mult, ALU.mult).then_inc(s["ready"], 1)


_INS = ["x_prompt", "x_sample", "cache_diff_k", "cache_diff_v", "state_ret", "state_gdn", "c", "c_ctx", "norm1_w",
        "norm2_w", "w_mod", "b_mod", "w_in", "ret_decay", "ret_norm", "diff_lambda", "diff_norm", "gdn_conv",
        "gdn_A_log", "gdn_dt_bias", "gdn_norm", "w_branch", "w_out", "peer_wq", "peer_keys", "peer_u", "peer_v",
        "norm_f_w"]
_OUTS = [("y_prompt", (1, SEQ, D)), ("y_sample", (1, DEC_SEQ, D)),
         ("new_cache_diff_k", (1, DEPTH, SEQ, D_HEADS, 2, D_HD)), ("new_cache_diff_v", (1, DEPTH, SEQ, D_HEADS, 2 * D_HD)),
         ("new_state_ret", (1, DEPTH, 2, R_HEADS, R_DK, R_DV)), ("new_state_gdn", (1, DEPTH, 2, G_HEADS, G_DK, G_DV))]


def kernel(**inputs):
    import numpy as _np
    import concourse.bacc as _bacc
    from concourse import mybir as _mybir
    from concourse.bass_utils import run_bass_kernel_spmd as _run

    nc = _bacc.Bacc("TRN2", target_bir_lowering=False, num_devices=1)
    arrays, ins, outs = {}, {}, {}
    for name, a in [(n, inputs[n]) for n in _INS] + list(shape_tables().items()):
        a = _np.ascontiguousarray(a)
        arrays[f"in_{name}_dram"] = a
        ins[name] = nc.dram_tensor(f"in_{name}_dram", a.shape, _mybir.dt.from_np(a.dtype), kind="ExternalInput").ap()
    for name, shape in _OUTS:
        outs[name] = nc.dram_tensor(f"out_{name}_dram", shape, _mybir.dt.float32, kind="ExternalOutput").ap()
    build(nc, ins, outs)
    r = _run(nc, [arrays], core_ids=[0])
    return tuple(r.results[0][f"out_{name}_dram"] for name, _ in _OUTS)
```

```python
import math
from contextlib import ExitStack

import numpy as np

import concourse.bass as bass
from concourse import mybir

F32 = mybir.dt.float32
F32R = mybir.dt.float32r
U32 = mybir.dt.uint32
ALU = mybir.AluOpType
ACT = mybir.ActivationFunctionType
AX = mybir.AxisListType.X
ds = bass.ds

P = 128
D = 1024
KT = D // P
DEPTH = 2
SEQ = 128
DEC_SEQ = 256
TILES = (SEQ + DEC_SEQ) // P
TOK = TILES * P
PAST = 128
GRID_W = 64
ROPE_BASE = 10000.0
EPS = 1e-6
R_HEADS, R_DK, R_DV = 4, 128, 256
D_HEADS, D_HD = 8, 64
G_HEADS, G_DK, G_DV = 8, 128, 128
CONV_K = 7
G_QKV = G_HEADS * (2 * G_DK + G_DV)
N_BRANCH = 3
PEER_HEADS, PEER_DQ, N_KEYS, TOPK = 8, 256, 128, 16
N_EXPERTS = N_KEYS * N_KEYS
SLOTS = PEER_HEADS * TOPK
MOD = 6 * D
CHUNK = 512
COL_RET = 0
COL_RET_G = 2 * R_HEADS * R_DK + R_HEADS * R_DV
COL_DIFF = COL_RET_G + R_HEADS * R_DV
COL_GDN = COL_DIFF + 3 * D_HEADS * 2 * D_HD
COL_GDN_Z = COL_GDN + G_QKV
COL_GDN_AB = COL_GDN_Z + G_HEADS * G_DV
COL_GATES = COL_GDN_AB + 4 * G_HEADS
PAD = CONV_K // 2
XC_P = PAD
XC_S = PAD + SEQ + 2 * PAD
XC_W = XC_S + DEC_SEQ + PAD
CV_W = XC_W - 2 * PAD
CV_S = XC_S - PAD
QBLK = G_QKV // P
LEVELS = 7
LATENT = (1, 2)
BIGNEG = -3.0e38
POS_QF, POS_QB, POS_KF, POS_KB, POS_IOTA = 0, 2, 4, 5, 6
TRI_POS, TRI_NEG, TRI_UP, TRI_LO, TRI_ID, TRI_ONE, TRI_OFF_F, TRI_OFF_B = range(8)


def shape_tables():
    j = np.arange(P, dtype=np.float32)[:, None]
    i = np.arange(P, dtype=np.float32)[None, :]
    tri = np.stack([np.maximum(i - j, 0), np.maximum(j - i, 0), (i >= j) * 1.0, (j >= i) * 1.0,
                    np.eye(P), np.ones((P, P)), i - j + P, j - i + P], 1).astype(np.float32)
    lvl = np.zeros((P, 2, LEVELS, P), np.float32)
    jj, ii = np.arange(P)[:, None], np.arange(P)[None, :]
    for n in range(LEVELS):
        s = 1 << n
        same = (jj // (2 * s)) == (ii // (2 * s))
        lvl[:, 0, n] = same & (jj % (2 * s) < s) & (ii % (2 * s) >= s)
        lvl[:, 1, n] = same & (ii % (2 * s) < s) & (jj % (2 * s) >= s)
    p = np.arange(P, dtype=np.float32)
    pos = np.zeros((P, POS_IOTA + TOPK), np.float32)
    pos[:, POS_QF] = p + 1
    pos[:, POS_QF + 1] = p + P + 1
    pos[:, POS_QB] = DEC_SEQ - p
    pos[:, POS_QB + 1] = DEC_SEQ - P - p
    pos[:, POS_KF] = SEQ - 1 - p
    pos[:, POS_KB] = p
    pos[:, POS_IOTA:] = np.arange(TOPK)

    def rope(dim):
        nf = dim // 4
        rows = DEC_SEQ // GRID_W
        row = np.repeat(np.arange(rows), GRID_W).astype(np.float32)
        col = np.tile(np.arange(GRID_W), rows).astype(np.float32)
        inv = np.power(np.float32(ROPE_BASE), -np.arange(nf, dtype=np.float32) / np.float32(nf)).astype(np.float32)
        r, c = row[:, None] * inv, col[:, None] * inv
        ang = np.concatenate([r, r, c, c], -1).astype(np.float64)
        sign = np.repeat([-1.0, 1.0, -1.0, 1.0], nf)
        t = np.stack([np.cos(ang), np.sin(ang) * sign], 1).astype(np.float32)
        return t.reshape(len(LATENT), P, 2, dim).transpose(1, 0, 2, 3).copy()

    lam = np.zeros((DEPTH, 4), np.float32)
    for li in range(DEPTH):
        init = 0.8 - 0.6 * math.exp(-0.3 * li)
        lam[li] = [init, 1.0 - init, li * N_EXPERTS, 0]
    return {"tri": tri, "lvl": lvl, "pos": pos, "rope_ret": rope(R_DK), "rope_diff": rope(D_HD), "layer": lam}


class Chain:

    def __init__(self, eng, sem):
        self.eng, self.sem, self.n, self.k = eng, sem, 0, 0

    def mark(self, ins):
        ins.then_inc(self.sem, 1)
        self.n = self.n + 1
        self.k += 1

    def sync(self, but=0):
        self.eng.wait_ge(self.sem, self.n - but)

    def link(self, ins):
        self.mark(ins)
        self.sync()

    def enter(self, i, per):
        self.base, self.per, self.k = self.n, per, 0
        self.n = self.base + i * per

    def leave(self, passes):
        assert self.k == self.per, (self.k, self.per)
        self.n = self.base + passes * self.per


def bc(ap, n):
    return ap.unsqueeze(1).to_broadcast([ap.shape[0], n, ap.shape[1]])


def bl(ap, n):
    return ap.unsqueeze(2).to_broadcast([ap.shape[0], ap.shape[1], n])


def build(nc, I, O, debug=None):
    ctx = ExitStack()
    with ctx:
        def sb(name, cols, dt=F32):
            return ctx.enter_context(nc.sbuf_tensor(name, [P, cols], dt))[:, :]

        def rounded_view(name, offset, cols):
            return nc.alloc_sbuf_tensor_at(name, [P, cols], F32R, offset=offset)[:, :]

        PS = [ctx.enter_context(nc.psum_tensor(f"bank{n}", [P, 512], F32))[:, :] for n in range(8)]
        X = sb("x_residual", TILES * D).rearrange("p (t n) -> p t n", t=TILES)
        H = sb("h_tokens", TILES * D).rearrange("p (t n) -> p t n", t=TILES)
        HTH = sb("h_features_high", KT * TOK, F32R).rearrange("p (k n) -> p k n", k=KT)
        ht_at = nc.sbuf_base
        YSUM = sb("expert_sums", KT * TOK)
        HTL = rounded_view("h_features_low", ht_at, KT * TOK).rearrange("p (k n) -> p k n", k=KT)
        MACC = sb("merged", TILES * D).rearrange("p (t n) -> p t n", t=TILES)
        Zf = sb("gates_z", TILES * D)
        Z = Zf.rearrange("p (t n) -> p t n", t=TILES)
        ring_at = nc.sbuf_base
        RING = sb("weight_ring", 2 * KT * CHUNK)
        RWL = rounded_view("weight_ring_low", ring_at, 2 * KT * CHUNK).rearrange("p (s k n) -> p s k n", s=2, k=KT)
        RW = RING.rearrange("p (s k n) -> p s k n", s=2, k=KT)
        HALF = 9216
        HIGHS = 4
        big_at = nc.sbuf_base
        BIG = sb("work", 2 * HALF)
        WH = rounded_view("weights_high", big_at + 4 * (2 * HALF - HIGHS * CHUNK), HIGHS * CHUNK)\
            .rearrange("p (s n) -> p s n", s=HIGHS)
        OTH = rounded_view("branch_features_high", big_at + 4 * HALF, KT * TOK).rearrange("p (k n) -> p k n", k=KT)
        OTL = rounded_view("branch_features_low", big_at + 4 * (HALF + KT * TOK), KT * TOK)\
            .rearrange("p (k n) -> p k n", k=KT)
        SST = sb("gdn_states", 2 * G_HEADS * G_DV).rearrange("p (g n) -> p g n", g=2 * G_HEADS)
        TRI = sb("triangles", 8 * P).rearrange("p (a n) -> p a n", a=8)
        LVL = sb("levels", 2 * LEVELS * P).rearrange("p (d a n) -> p d a n", d=2, a=LEVELS)
        POS = sb("positions", POS_IOTA + TOPK)
        ROPR = sb("rope_ret", 2 * 2 * R_DK).rearrange("p (t a n) -> p t a n", t=2, a=2)
        ROPD = sb("rope_diff", 2 * 2 * D_HD).rearrange("p (t a n) -> p t a n", t=2, a=2)
        LAMC = sb("layer_constants", 4)
        COND = sb("conditions", KT * 2).rearrange("p (k g) -> p k g", g=2)
        CONDH = sb("conditions_high", KT * 2, F32R).rearrange("p (k g) -> p k g", g=2)
        CONDL = sb("conditions_low", KT * 2, F32R).rearrange("p (k g) -> p k g", g=2)
        small_at = nc.sbuf_base
        SM = sb("small", 1024)
        modd = nc.dram_tensor("mod_rows", (2, MOD), F32).ap()

        ID = TRI[:, TRI_ID, :]
        PRJ = BIG[:, 0:HALF].rearrange("p (t n) -> p t n", t=TILES)
        UP = BIG[:, HALF:2 * HALF]

        pools = [[ctx.enter_context(nc.semaphore(f"stage{n}_{k}")) for k in range(40)] for n in range(2)]
        assert all([x.num for x in pool] == list(range(pool[0].num, pool[0].num + 40)) for pool in pools)
        got = [ctx.enter_context(nc.semaphore(f"row_gathered{n}")) for n in range(16)]
        turns = [1]

        def signals(names):
            turns[0] = 1 - turns[0]
            names = names.split()
            assert len(names) <= len(pools[0])
            return dict(zip(names, pools[turns[0]]))

        def clear_last_stage(dve, s):
            other = pools[1] if any(x.num == pools[0][0].num for x in s.values()) else pools[0]
            dve.sem_clear(range(other[0].num, other[-1].num + 1))

        LOADS = [[f"loaded{j}{q}" for q in range(4)] for j in range(2)]
        STREAM = "free high high_free low " + " ".join(sum(LOADS, [])) + " "

        def load_chunk(sp, s, j, view):
            for q in range(4):
                sp.dma_start(RW[:, j, 2 * q:2 * q + 2, :], view[:, 2 * q:2 * q + 2, :]).then_inc(s[LOADS[j][q]], 16)

        def sp_weights(sp, s, src, chunks, base):
            with sp.Fori(0, chunks // 2) as i:
                for j in range(2):
                    sp.wait_ge(s["free"], base + 2 * i + j + 1)
                    load_chunk(sp, s, j, src(2 * i + j))

        def act_high(act, s, base, i, j, tiles):
            for k in tiles:
                if k % 2 == 0:
                    act.wait_ge(s[LOADS[j][k // 2]], 16 * (base // 2 + 1) + 16 * i)
                act.wait_ge(s["high_free"], KT * base + 2 * KT * i + KT * j + k + 1)
                nc.scalar.activation(WH[:, k % HIGHS, :], RW[:, j, k, :], ACT.Copy).then_inc(s["high"], 1)

        def act_split(act, s, base, chunks, use, more=False, loop=True):
            def pair(i, last):
                for j in range(2):
                    act_high(act, s, base, i, j, range(HIGHS, KT))
                    if not (last and j == 1):
                        act_high(act, s, base, i + j, 1 - j, range(HIGHS))
                    use(i, j)

            if base == 0:
                act_high(act, s, 0, 0, 0, range(HIGHS))
            passes = chunks // 2 if more else chunks // 2 - 1
            if passes == 1 or not loop:
                for i in range(passes):
                    pair(i, False)
            elif passes > 1:
                with act.Fori(0, passes) as i:
                    pair(i, False)
            if not more:
                pair(chunks // 2 - 1, True)

        def low_part(eng, ops, s, i, j, tiles):
            for k in tiles:
                eng.wait_ge(s["high"], 2 * KT * i + KT * j + k + 1)
                ops.tensor_tensor(RWL[:, j, k, :], RW[:, j, k, :], WH[:, k % HIGHS, :].bitcast(F32), ALU.subtract)\
                    .then_inc(s["low"], 1)

        def low_parts(eng, ops, s, chunks):
            with eng.Fori(0, chunks // 2) as i:
                for j in range(2):
                    low_part(eng, ops, s, i, j, range(KT))

        def pe_start(pe, s):
            pe.sem_inc(s["free"], 2)
            pe.sem_inc(s["high_free"], HIGHS)

        def pe_project(pe, s, xt, chunks, base, banks_free, done):
            with pe.Fori(0, chunks // 2) as i:
                for j in range(2):
                    xh, xl = xt[j]
                    pe.wait_ge(*banks_free(i, j))
                    for k in range(KT):
                        pe.wait_ge(s["low"], KT * base + 2 * KT * i + KT * j + k + 1)
                        for t in range(TILES):
                            rows = slice(t * P, (t + 1) * P)
                            nc.tensor.matmul(PS[3 * j + t], xh[:, k, rows], WH[:, k % HIGHS, :], start=(k == 0), stop=False)
                            mm = nc.tensor.matmul(PS[3 * j + t], xl[:, k, rows], WH[:, k % HIGHS, :], start=False, stop=False)
                            if t == TILES - 1:
                                mm.then_inc(s["high_free"], 1)
                            mm = nc.tensor.matmul(PS[3 * j + t], xh[:, k, rows], RWL[:, j, k, :],
                                                  start=False, stop=(k == KT - 1))
                            if k == KT - 1:
                                mm.then_inc(done, 1)
                    pe.drain().then_inc(s["free"], 1)

        def pe_chunk_features(pe, s, banks, i, j):
            for k in range(KT):
                pe.wait_ge(s["low"], 2 * KT * i + KT * j + k + 1)
                for b in range(4):
                    cols = slice(b * P, (b + 1) * P)
                    out = PS[banks + b][:, 0:TOK]
                    nc.tensor.matmul(out, WH[:, k % HIGHS, cols], HTH[:, k, :], start=(k == 0), stop=False)
                    mm = nc.tensor.matmul(out, WH[:, k % HIGHS, cols], HTL[:, k, :], start=False, stop=False)
                    if b == 3:
                        mm.then_inc(s["high_free"], 1)
                    mm = nc.tensor.matmul(out, RWL[:, j, k, cols], HTH[:, k, :], start=False, stop=(k == KT - 1))
                    if k == KT - 1:
                        mm.then_inc(s["done"], 1)
            pe.drain().then_inc(s["free"], 1)

        def pe_transpose_tokens(pe, src, ready, turned):
            for t in range(TILES):
                pe.wait_ge(ready, t + 1)
                for b in range(2):
                    for k in range(4):
                        kk = 4 * b + k
                        mm = nc.tensor.transpose(PS[2 * t + b][:, k * P:(k + 1) * P], src[:, t, kk * P:(kk + 1) * P], ID)
                    mm.then_inc(turned, 1)

        def features_view(dst, n):
            t, b = divmod(n, 2)
            return dst[:, 4 * b:4 * b + 4, t * P:(t + 1) * P]

        def act_turned_high(act, dst, s):
            for n in range(2 * TILES):
                act.wait_ge(s["turned"], n + 1)
                nc.scalar.activation(features_view(dst, n), PS[n].rearrange("p (k n) -> p k n", k=4), ACT.Copy)\
                    .then_inc(s["turned_high"], 1)

        def dve_turned_low(dve, high, low, s):
            for n in range(2 * TILES):
                dve.wait_ge(s["turned_high"], n + 1)
                nc.vector.tensor_tensor(features_view(low, n), PS[n].rearrange("p (k n) -> p k n", k=4),
                                        features_view(high, n).bitcast(F32), ALU.subtract).then_inc(s["turned_low"], 1)

        with nc.Block(no_gpsimd_drain=True) as block:
            s = signals("loads silu high low")

            @block.sync
            def _(sp):
                sp.dma_start(X[:, 0, :], I["x_prompt"][0]).then_inc(s["loads"], 16)
                sp.dma_start(X[:, 1:3, :], I["x_sample"][0].rearrange("(t p) n -> p t n", p=P)).then_inc(s["loads"], 16)
                sp.dma_start(TRI, I["tri"]).then_inc(s["loads"], 16)
                sp.dma_start(LVL, I["lvl"]).then_inc(s["loads"], 16)
                sp.dma_start(POS, I["pos"]).then_inc(s["loads"], 16)
                sp.dma_start(ROPR, I["rope_ret"]).then_inc(s["loads"], 16)
                sp.dma_start(ROPD, I["rope_diff"]).then_inc(s["loads"], 16)
                with nc.allow_non_contiguous_dma(reason="two short vectors, laid over partitions"):
                    sp.dma_start(SM[:, 0:KT], I["c_ctx"].rearrange("(k p) -> p k", p=P)).then_inc(s["loads"], 16)
                    sp.dma_start(SM[:, KT:2 * KT], I["c"][0].rearrange("(k p) -> p k", p=P)).then_inc(s["loads"], 16)

            @block.scalar
            def _(act):
                act.wait_ge(s["loads"], 9 * 16)
                for g in range(2):
                    nc.scalar.activation(COND[:, :, g], SM[:, g * KT:(g + 1) * KT], ACT.Silu).then_inc(s["silu"], 1)
                act.wait_ge(s["silu"], 2)
                nc.scalar.activation(CONDH, COND, ACT.Copy).then_inc(s["high"], 1)

            @block.vector
            def _(dve):
                dve.wait_ge(s["high"], 1)
                nc.vector.tensor_tensor(CONDL, COND, CONDH.bitcast(F32), ALU.subtract).then_inc(s["low"], 1)

        def stage_mod(l):
            s = signals(STREAM + "banks_free done added bias stored chain")
            w = I["w_mod"].rearrange("l (k p) n -> l p k n", p=P)
            rows, bias = BIG[0:2, 0:MOD], BIG[0:2, MOD:2 * MOD]
            chunks = MOD // CHUNK
            with nc.Block(no_gpsimd_drain=True) as block:
                @block.sync
                def _(sp):
                    sp.dma_start(bias, I["b_mod"][l].partition_broadcast(2)).then_inc(s["bias"], 16)
                    sp.dma_start(LAMC, I["layer"][l].partition_broadcast(P)).then_inc(s["bias"], 16)
                    sp_weights(sp, s, lambda n: w[l, :, :, ds(n * CHUNK, CHUNK)], chunks, 0)
                    sp.wait_ge(s["added"], chunks)
                    sp.dma_start(modd, rows).then_inc(s["stored"], 16)
                    sp.wait_ge(s["stored"], 16)

                @block.tensor
                def _(pe):
                    pe_start(pe, s)
                    with pe.Fori(0, chunks // 2) as i:
                        for j in range(2):
                            pe.wait_ge(s["banks_free"], 2 * i + j + 1)
                            out = PS[j][0:2, :]
                            for k in range(KT):
                                pe.wait_ge(s["low"], 2 * KT * i + KT * j + k + 1)
                                nc.tensor.matmul(out, CONDH[:, k, :], WH[:, k % HIGHS, :], start=(k == 0), stop=False)
                                nc.tensor.matmul(out, CONDL[:, k, :], WH[:, k % HIGHS, :], start=False, stop=False)\
                                    .then_inc(s["high_free"], 1)
                                mm = nc.tensor.matmul(out, CONDH[:, k, :], RWL[:, j, k, :], start=False, stop=(k == KT - 1))
                            mm.then_inc(s["done"], 1)
                            pe.drain().then_inc(s["free"], 1)

                @block.scalar
                def _(act):
                    act_split(act, s, 0, chunks, lambda i, j: None)

                @block.vector
                def _(dve):
                    clear_last_stage(dve, s)
                    dve.sem_inc(s["banks_free"], 2)
                    low_part(dve, nc.vector, s, 0, 0, range(HIGHS))
                    dve.wait_ge(s["bias"], 32)

                    def pair(i, last):
                        for j in range(2):
                            low_part(dve, nc.vector, s, i, j, range(HIGHS, KT))
                            if not (last and j == 1):
                                low_part(dve, nc.vector, s, i + j, 1 - j, range(HIGHS))
                            dve.wait_ge(s["done"], 2 * i + j + 1)
                            cols = ds(2 * CHUNK * i + j * CHUNK, CHUNK)
                            nc.vector.tensor_tensor(rows[:, cols], PS[j][0:2, :], bias[:, cols], ALU.add)\
                                .then_inc(s["added"], 1)
                            dve.drain().then_inc(s["banks_free"], 1)

                    with dve.Fori(0, chunks // 2 - 1) as i:
                        pair(i, False)
                    pair(chunks // 2 - 1, True)

        def stage_norm(l, which):
            s = signals("loads squares mean root ready turned turned_high turned_low chain")
            norm_w = I["norm1_w"] if which == 0 else I["norm2_w"]
            NW = UP[:, 0:D]
            SH = UP[:, D:3 * D].rearrange("p (g n) -> p g n", g=2)
            SC = UP[:, 3 * D:5 * D].rearrange("p (g n) -> p g n", g=2)
            SQ = UP[:, 5 * D:8 * D].rearrange("p (t n) -> p t n", t=TILES)
            SS = SM[:, 0:TILES]
            RS = SM[:, 4:4 + TILES]
            off = 3 * D * which
            with nc.Block(no_gpsimd_drain=True) as block:
                @block.sync
                def _(sp):
                    sp.dma_start(NW, norm_w[l].partition_broadcast(P)).then_inc(s["loads"], 16)
                    for g in range(2):
                        sp.dma_start(SH[:, g, :], modd[g, off:off + D].partition_broadcast(P)).then_inc(s["loads"], 16)
                        sp.dma_start(SC[:, g, :], modd[g, off + D:off + 2 * D].partition_broadcast(P))\
                            .then_inc(s["loads"], 16)

                @block.scalar
                def _(act):
                    for t in range(TILES):
                        nc.scalar.activation(SQ[:, t, :], X[:, t, :], ACT.Square, accum_out=SS[:, t:t + 1])\
                            .then_inc(s["squares"], 1)
                    act.wait_ge(s["mean"], 1)
                    nc.scalar.activation(RS, SS, ACT.Sqrt).then_inc(s["root"], 1)
                    act_turned_high(act, HTH, s)

                @block.vector
                def _(dve):
                    clear_last_stage(dve, s)
                    c = Chain(dve, s["chain"])
                    dve.wait_ge(s["squares"], TILES)
                    nc.vector.tensor_scalar(SS, SS, 1.0 / D, EPS, ALU.mult, ALU.add).then_inc(s["mean"], 1)
                    dve.wait_ge(s["loads"], 5 * 16)
                    for g in range(2):
                        c.mark(nc.vector.scalar_tensor_tensor(SC[:, g, :], SC[:, g, :], 1.0, NW, ALU.add, ALU.mult))
                    dve.wait_ge(s["root"], 1)
                    c.link(nc.vector.reciprocal(RS, RS))
                    for t in range(TILES):
                        g = int(t > 0)
                        c.link(nc.vector.scalar_tensor_tensor(H[:, t, :], X[:, t, :], RS[:, t:t + 1], SC[:, g, :],
                                                              ALU.mult, ALU.mult))
                        nc.vector.tensor_tensor(H[:, t, :], H[:, t, :], SH[:, g, :], ALU.add).then_inc(s["ready"], 1)
                    dve_turned_low(dve, HTH, HTL, s)

                @block.tensor
                def _(pe):
                    pe_transpose_tokens(pe, H, s["ready"], s["turned"])

        w_in = I["w_in"].rearrange("l (k p) n -> l p k n", p=P)

        def stage_project(l, parts, turn):
            s = signals(STREAM + "banks_free done chain")
            turn_chunks, table, groups, dim = turn
            half = turn_chunks // 2 * CHUNK
            TMP = UP[:, 0:half]
            total = sum(chunks for _, chunks, _, _ in parts)
            with nc.Block(no_gpsimd_drain=True) as block:
                @block.sync
                def _(sp):
                    base = 0
                    for col, chunks, _, _ in parts:
                        sp_weights(sp, s, lambda n: w_in[l, :, :, ds(n * CHUNK + col, CHUNK)], chunks, base)
                        base += chunks

                @block.tensor
                def _(pe):
                    pe_start(pe, s)
                    pe_project(pe, s, ((HTH, HTL), (HTH, HTL)), total, 0,
                               lambda i, j: (s["banks_free"], 2 * i + j + 1), s["done"])

                @block.scalar
                def _(act):
                    act.sem_inc(s["banks_free"], 2)
                    base = 0
                    for _, chunks, dst, func in parts:
                        def use(i, j):
                            for t in range(TILES):
                                act.wait_ge(s["done"], 3 * base + 6 * i + 3 * j + t + 1)
                                nc.scalar.activation(dst[:, t, ds(2 * CHUNK * i + j * CHUNK, CHUNK)], PS[3 * j + t], func)
                            act.drain().then_inc(s["banks_free"], 1)

                        act_split(act, s, base, chunks, use, more=base + chunks < total)
                        base += chunks

                @block.gpsimd
                def _(pool):
                    low_parts(pool, nc.gpsimd, s, total)

                @block.vector
                def _(dve):
                    clear_last_stage(dve, s)
                    c = Chain(dve, s["chain"])
                    for part in range(2):
                        dve.wait_ge(s["banks_free"], 2 + (part + 1) * turn_chunks // 2)
                        rope(dve, c, lambda t: PRJ[:, t, part * half:(part + 1) * half], table, groups, dim, TMP)

        def rope(dve, c, view, table, groups, dim, tmp):
            q = dim // 4
            for n, t in enumerate(LATENT):
                x4 = view(t).rearrange("p (g a b n) -> p g a b n", g=groups, a=2, b=2)
                t4 = tmp.rearrange("p (g a b n) -> p g a b n", g=groups, a=2, b=2)
                sin = table[:, n, 1, :].rearrange("p (a b n) -> p a b n", a=2, b=2)
                for b in range(2):
                    sb_ = sin[:, :, b, :].unsqueeze(1).to_broadcast([P, groups, 2, q])
                    c.mark(nc.vector.tensor_tensor(t4[:, :, :, b, :], x4[:, :, :, 1 - b, :], sb_, ALU.mult))
                c.sync()
                x3 = view(t).rearrange("p (g n) -> p g n", g=groups)
                c.link(nc.vector.tensor_tensor(x3, x3, bc(table[:, n, 0, :], groups), ALU.mult))
                c.link(nc.vector.tensor_tensor(view(t), view(t), tmp, ALU.add))

        def log1p_parts(dve, c, z, s_, tmp, out, like):
            c.link(nc.vector.tensor_scalar(s_, z, 2.0, None, ALU.add))
            c.link(nc.vector.reciprocal(s_, s_))
            c.link(nc.vector.tensor_tensor(s_, s_, z, ALU.mult))
            c.link(nc.vector.tensor_tensor(tmp, s_, s_, ALU.mult))
            terms = 8
            c.link(nc.vector.tensor_scalar(out, tmp, 1.0 / (2 * terms + 1), 1.0 / (2 * terms - 1), ALU.mult, ALU.add))
            for n in range(terms - 1, 0, -1):
                c.link(nc.vector.tensor_tensor(out, out, tmp, ALU.mult))
                c.link(nc.vector.tensor_scalar(out, out, 1.0 / (2 * n - 1), None, ALU.add))
            c.link(nc.vector.scalar_tensor_tensor(out, out, 2.0, s_, ALU.mult, ALU.mult))

        def act_squares(sq, cols, junk, t, g, width):
            groups = D // width
            if sq.n >= 2:
                sq.sync(but=1)
            slot = sq.n % 2 * width
            sq.mark(nc.scalar.activation(junk[:, slot:slot + width], H[:, t, g * width:(g + 1) * width], ACT.Square,
                                         accum_out=cols[:, t * groups + g:t * groups + g + 1]))

        def dve_head_norm(dve, c, s, width, cols, weight):
            groups = D // width
            dve.wait_ge(s["squares"], TILES * groups)
            nc.vector.tensor_scalar(cols, cols, 1.0 / width, EPS, ALU.mult, ALU.add).then_inc(s["mean"], 1)
            dve.wait_ge(s["root"], 1)
            c.link(nc.vector.reciprocal(cols, cols))
            for t in range(TILES):
                for g in range(groups):
                    h = H[:, t, g * width:(g + 1) * width]
                    c.mark(nc.vector.scalar_tensor_tensor(h, h, cols[:, t * groups + g:t * groups + g + 1], weight(t, g),
                                                          ALU.mult, ALU.mult))

        def act_head_root(act, s, cols):
            act.wait_ge(s["mean"], 1)
            nc.scalar.activation(cols, cols, ACT.Sqrt).then_inc(s["root"], 1)


        def stage_retention(l):
            s = signals("loads chain squares mean root lgin lgexp lg tables transposed copied scores masked"
                           " out intra evacuated kd states statecopy stored")
            QT = UP[:, 0:1536].rearrange("p (h n) -> p h n", h=R_HEADS)
            KTT = UP[:, 1536:3072].rearrange("p (h n) -> p h n", h=R_HEADS)
            DT = UP[:, 3072:4608].rearrange("p (h a n) -> p h a n", h=R_HEADS, a=3)
            AT = UP[:, 4608:5888].rearrange("p (b n) -> p b n", b=2)
            E2 = UP[:, 5888:6400].rearrange("p (h n) -> p h n", h=R_HEADS)
            KD = UP[:, 6400:7424].rearrange("p (g n) -> p g n", g=8)
            S0 = RING[:, 1024:3072].rearrange("p (g n) -> p g n", g=8)
            ST = RING[:, 3072:5120].rearrange("p (g n) -> p g n", g=8)
            JUNK = RING[:, 5120:5632]
            LG, LZ, LS, LT = SM[:, 0:8], SM[:, 8:16], SM[:, 16:24], SM[:, 24:32]
            DEC = SM[:, 32:80].rearrange("p (g n) -> p g n", g=8)
            NWR = SM[:, 128:384]
            COLS = SM[:, 384:396]
            scale = R_DK ** -0.5
            with nc.Block(no_gpsimd_drain=True) as block:
                @block.sync
                def _(sp):
                    sp.dma_start(LG, I["ret_decay"][l].rearrange("d h -> (d h)").partition_broadcast(P))\
                        .then_inc(s["loads"], 16)
                    sp.dma_start(NWR, I["ret_norm"][l].partition_broadcast(P)).then_inc(s["loads"], 16)
                    sp.dma_start(S0, I["state_ret"][0, l].rearrange("d h k v -> k (d h) v")).then_inc(s["loads"], 16)
                    sp.wait_ge(s["statecopy"], 4)
                    sp.dma_start(O["new_state_ret"][0, l].rearrange("d h k v -> k (d h) v"), ST).then_inc(s["stored"], 16)
                    sp.wait_ge(s["stored"], 16)

                @block.scalar
                def _(act):
                    act.wait_ge(s["lgin"], 1)
                    nc.scalar.activation(LZ, LT, ACT.Exp).then_inc(s["lgexp"], 1)
                    for n in range(2 * R_HEADS):
                        h, isk = n // 2, n % 2
                        act.wait_ge(s["transposed"], n + 1)
                        nc.scalar.activation((KTT if isk else QT)[:, h, :], PS[n % 4][:, 0:TOK], ACT.Copy,
                                             scale=1.0 if isk else scale).then_inc(s["copied"], 1)
                    act.wait_ge(s["lg"], 1)
                    for h in range(R_HEADS):
                        f, b = LG[:, h:h + 1], LG[:, R_HEADS + h:R_HEADS + h + 1]
                        nc.scalar.activation(DT[:, h, 1, :], TRI[:, TRI_POS, :], ACT.Exp, scale=f)
                        nc.scalar.activation(DT[:, h, 2, :], TRI[:, TRI_OFF_F, :], ACT.Exp, scale=f)
                        nc.scalar.activation(E2[:, h, :], TRI[:, TRI_NEG, :], ACT.Exp, scale=b)
                        nc.scalar.activation(DT[:, h, 0, :], TRI[:, TRI_OFF_B, :], ACT.Exp, scale=b)
                    for g in range(8):
                        ins = nc.scalar.activation(DEC[:, g, :], POS[:, 0:6], ACT.Exp, scale=LG[:, g:g + 1])
                    ins.then_inc(s["tables"], 1)

                    sq = Chain(act, s["squares"])

                    def squares(h):
                        act.wait_ge(s["evacuated"], h + 1)
                        for t in range(TILES):
                            act_squares(sq, COLS, JUNK, t, h, R_DV)

                    for h in range(R_HEADS):
                        act.wait_ge(s["out"], h + 1)
                        hs = slice(h * R_DV, (h + 1) * R_DV)
                        nc.scalar.activation(H[:, 0, hs], PS[6][:, 0:256], ACT.Copy)
                        nc.scalar.activation(H[:, 1, hs], PS[6][:, 256:512], ACT.Copy)
                        nc.scalar.activation(H[:, 2, hs], PS[7][:, 0:256], ACT.Copy).then_inc(s["intra"], 1)
                        if h:
                            squares(h - 1)
                    squares(R_HEADS - 1)
                    act_head_root(act, s, COLS)
                    for b in range(4):
                        act.wait_ge(s["states"], b + 1)
                        nc.scalar.activation(ST[:, 2 * b:2 * b + 2, :], PS[2 + b].rearrange("p (g n) -> p g n", g=2),
                                             ACT.Copy).then_inc(s["statecopy"], 1)

                @block.vector
                def _(dve):
                    clear_last_stage(dve, s)
                    c = Chain(dve, s["chain"])
                    dve.wait_ge(s["loads"], 3 * 16)
                    c.mark(nc.vector.tensor_scalar(LS, LG, -1.0, None, ALU.mult))
                    c.sync()
                    nc.vector.tensor_tensor(LT, LG, LS, ALU.min).then_inc(s["lgin"], 1)
                    dve.wait_ge(s["lgexp"], 1)
                    c.link(nc.vector.tensor_scalar(LG, LG, 0.0, None, ALU.min))
                    W1, W2, W3 = SM[:, 80:88], SM[:, 88:96], SM[:, 96:104]
                    log1p_parts(dve, c, LZ, W1, W2, W3, None)
                    nc.vector.tensor_tensor(LG, LG, W3, ALU.subtract).then_inc(s["lg"], 1)
                    zg = Zf.rearrange("p (g n) -> p g n", n=R_DV)
                    c.mark(nc.vector.tensor_tensor(zg, zg, bc(NWR, TILES * R_HEADS), ALU.mult))
                    dve.wait_ge(s["tables"], 1)
                    c.mark(nc.vector.tensor_tensor(DT[:, :, 1, :], DT[:, :, 1, :], bc(TRI[:, TRI_UP, :], R_HEADS), ALU.mult))
                    c.link(nc.vector.tensor_tensor(E2, E2, bc(TRI[:, TRI_LO, :], R_HEADS), ALU.mult))
                    c.link(nc.vector.tensor_tensor(DT[:, :, 1, :], DT[:, :, 1, :], E2, ALU.add))
                    for g in range(8):
                        d, h = divmod(g, R_HEADS)
                        ins = nc.vector.tensor_scalar(KD[:, g, :], PRJ[:, 0, 512 + h * P:512 + (h + 1) * P],
                                                      DEC[:, g, POS_KF + d:POS_KF + d + 1], None, ALU.mult)
                    ins.then_inc(s["kd"], 1)

                    def mask(h):
                        dve.wait_ge(s["scores"], h + 1)
                        if h >= 2:
                            dve.wait_ge(s["out"], h - 1)
                        a = AT[:, h % 2, :]
                        nc.vector.tensor_tensor(a[:, 0:128], PS[4][:, 0:128], DT[:, h, 1, :], ALU.mult)
                        nc.vector.tensor_tensor(a[:, 128:384], PS[4][:, 128:384],
                                                DT[:, h, 1:3, :].rearrange("p a n -> p (a n)"), ALU.mult)
                        nc.vector.tensor_tensor(a[:, 384:640], PS[5][:, 0:256],
                                                DT[:, h, 0:2, :].rearrange("p a n -> p (a n)"), ALU.mult)\
                            .then_inc(s["masked"], 1)

                    mask(0)
                    for h in range(R_HEADS):
                        if h + 1 < R_HEADS:
                            mask(h + 1)
                        dve.wait_ge(s["out"], h + 1)
                        dve.wait_ge(s["intra"], h + 1)
                        hs = slice(h * R_DV, (h + 1) * R_DV)
                        for d in range(2):
                            for n, t in enumerate(LATENT):
                                col = DEC[:, d * R_HEADS + h, 2 * d + n:2 * d + n + 1]
                                ins = nc.vector.scalar_tensor_tensor(H[:, t, hs], PS[n][:, d * 256:(d + 1) * 256], col,
                                                                     H[:, t, hs], ALU.mult, ALU.add)
                                c.mark(ins)
                            c.sync()
                        dve.sem_inc(s["evacuated"], 1)
                    dve_head_norm(dve, c, s, R_DV, COLS, lambda t, g: Z[:, t, g * R_DV:(g + 1) * R_DV])

                @block.tensor
                def _(pe):
                    for n in range(2 * R_HEADS):
                        h, isk = n // 2, n % 2
                        if n >= 4:
                            pe.wait_ge(s["copied"], n - 3)
                        for t in range(TILES):
                            o = isk * 512 + h * P
                            mm = nc.tensor.transpose(PS[n % 4][:, t * P:(t + 1) * P], PRJ[:, t, o:o + P], ID)
                        mm.then_inc(s["transposed"], 1)

                    def scores(h):
                        if h == 0:
                            pe.wait_ge(s["copied"], 2 * R_HEADS)
                        else:
                            pe.wait_ge(s["masked"], h)
                        nc.tensor.matmul(PS[4][:, 0:128], KTT[:, h, 0:P], QT[:, h, 0:P], start=True, stop=True)
                        nc.tensor.matmul(PS[4][:, 128:384], KTT[:, h, P:2 * P], QT[:, h, P:TOK], start=True, stop=True)
                        nc.tensor.matmul(PS[5][:, 0:256], KTT[:, h, 2 * P:TOK], QT[:, h, P:TOK], start=True, stop=True)\
                            .then_inc(s["scores"], 1)

                    scores(0)
                    for h in range(R_HEADS):
                        pe.wait_ge(s["masked"], h + 1)
                        if h + 1 < R_HEADS:
                            scores(h + 1)
                        if h >= 1:
                            pe.wait_ge(s["evacuated"], h)
                        a = AT[:, h % 2, :]
                        v = [PRJ[:, t, 1024 + h * R_DV:1024 + (h + 1) * R_DV] for t in range(TILES)]
                        nc.tensor.matmul(PS[6][:, 0:256], a[:, 0:128], v[0], start=True, stop=True)
                        for n, t in enumerate(LATENT):
                            dst = PS[6][:, 256:512] if n == 0 else PS[7][:, 0:256]
                            nc.tensor.matmul(dst, a[:, 128 + n * P:256 + n * P], v[1], start=True, stop=False)
                            nc.tensor.matmul(dst, a[:, 384 + n * P:512 + n * P], v[2], start=False, stop=True)
                            for d in range(2):
                                mm = nc.tensor.matmul(PS[n][:, d * 256:(d + 1) * 256], QT[:, h, t * P:(t + 1) * P],
                                                      S0[:, d * R_HEADS + h, :], start=True, stop=True)
                        mm.then_inc(s["out"], 1)
                    pe.wait_ge(s["kd"], 1)
                    for g in range(8):
                        h = g % R_HEADS
                        mm = nc.tensor.matmul(PS[2 + g // 2][:, (g % 2) * 256:(g % 2) * 256 + 256], KD[:, g, :],
                                              PRJ[:, 0, 1024 + h * R_DV:1024 + (h + 1) * R_DV], start=True, stop=True)
                        if g % 2:
                            mm.then_inc(s["states"], 1)

        def stage_diff(l):
            s = signals("loads chain squares mean root transposed copied lamsum lamexp scores maxes exps"
                           " weights turned wt out ocopy stored")
            QT = UP[:, 0:3072].rearrange("p (h n) -> p h n", h=D_HEADS)
            KTT = UP[:, 3072:7168].rearrange("p (h n) -> p h n", h=D_HEADS)
            CK, CVV = UP[:, 7168:8192], UP[:, 8192:9216]
            PP = RING[:, 2048:3584].rearrange("p (b a n) -> p b a n", b=2, a=2)
            WW = RING[:, 3584:4352].rearrange("p (b n) -> p b n", b=2)
            WT = RING[:, 4352:5120].rearrange("p (b n) -> p b n", b=2)
            JUNK = RING[:, 5120:5376]
            LP = SM[:, 0:256]
            LPR = SM[:, 256:384]
            NWD = SM[:, 384:512]
            MX = SM[:, 512:560].rearrange("p (u a) -> p u a", a=2)
            SS = SM[:, 560:608].rearrange("p (u a) -> p u a", a=2)
            LSUM, NLAM = SM[:, 608:610], SM[:, 610:611]
            COLS = SM[:, 640:664]
            scale = D_HD ** -0.5
            units = [(t, h) for t in range(TILES) for h in range(D_HEADS)]
            U = len(units)

            def span(t):
                return (0, P) if t == 0 else (P, 4 * P)

            with nc.Block(no_gpsimd_drain=True) as block:
                @block.sync
                def _(sp):
                    sp.dma_start(LP, I["diff_lambda"][l].rearrange("a n -> (a n)").partition_broadcast(P)).then_inc(s["loads"], 16)
                    sp.dma_start(NWD, I["diff_norm"][l].partition_broadcast(P)).then_inc(s["loads"], 16)
                    sp.dma_start(CK, I["cache_diff_k"][0, l].rearrange("n h a d -> n (h a d)")).then_inc(s["loads"], 16)
                    sp.dma_start(CVV, I["cache_diff_v"][0, l].rearrange("n h d -> n (h d)")).then_inc(s["loads"], 16)
                    sp.dma_start(O["new_cache_diff_k"][0, l].rearrange("n h a d -> n (h a d)"), PRJ[:, 0, 1024:2048])\
                        .then_inc(s["stored"], 16)
                    sp.dma_start(O["new_cache_diff_v"][0, l].rearrange("n h d -> n (h d)"), PRJ[:, 0, 2048:3072])\
                        .then_inc(s["stored"], 16)
                    sp.wait_ge(s["stored"], 32)

                @block.scalar
                def _(act):
                    act.wait_ge(s["lamsum"], 1)
                    nc.scalar.activation(LSUM, LSUM, ACT.Exp).then_inc(s["lamexp"], 1)
                    for n in range(2 * D_HEADS):
                        h, isk = n // 2, n % 2
                        act.wait_ge(s["transposed"], n + 1)
                        w = 512 if isk else TOK
                        nc.scalar.activation((KTT if isk else QT)[:, h, :], PS[n % 4][:, 0:w], ACT.Copy).then_inc(s["copied"], 1)

                    def exps(u):
                        t, h = units[u]
                        a, b = span(t)
                        act.wait_ge(s["maxes"], u + 1)
                        if u >= 2:
                            act.wait_ge(s["weights"], u - 1)
                        for p in range(2):
                            ins = nc.scalar.activation(PP[:, u % 2, p, 0:b - a], PS[4 + 2 * (u % 2) + p][:, 0:b - a],
                                                       ACT.Exp, bias=MX[:, u, p:p + 1], scale=scale,
                                                       accum_out=SS[:, u, p:p + 1])
                        ins.then_inc(s["exps"], 1)

                    sq = Chain(act, s["squares"])

                    def squares(u):
                        act.wait_ge(s["ocopy"], u + 1)
                        act_squares(sq, COLS, JUNK, *units[u], 2 * D_HD)

                    exps(0)
                    for u in range(U):
                        if u + 1 < U:
                            exps(u + 1)
                        t, h = units[u]
                        a, b = span(t)
                        act.wait_ge(s["turned"], u + 1)
                        if u >= 2:
                            act.wait_ge(s["out"], u - 1)
                        nc.scalar.activation(WT[:, u % 2, 0:b - a], PS[u % 2][:, 0:b - a], ACT.Copy).then_inc(s["wt"], 1)
                        if u >= 2:
                            squares(u - 2)
                    squares(U - 2)
                    squares(U - 1)
                    act_head_root(act, s, COLS)

                @block.vector
                def _(dve):
                    clear_last_stage(dve, s)
                    c = Chain(dve, s["chain"])
                    dve.wait_ge(s["loads"], 4 * 16)
                    lp = LP.rearrange("p (a b n) -> p a b n", a=2, b=2)
                    c.link(nc.vector.tensor_tensor(LPR.rearrange("p (a n) -> p a n", a=2), lp[:, :, 0, :], lp[:, :, 1, :],
                                                   ALU.mult))
                    nc.vector.tensor_reduce(LSUM, LPR.rearrange("p (a n) -> p a n", a=2), AX, ALU.add).then_inc(s["lamsum"], 1)
                    dve.wait_ge(s["lamexp"], 1)
                    c.link(nc.vector.tensor_tensor(NLAM, LSUM[:, 1:2], LSUM[:, 0:1], ALU.subtract))
                    c.link(nc.vector.tensor_tensor(NLAM, NLAM, LAMC[:, 0:1], ALU.subtract))
                    c.link(nc.vector.tensor_scalar(NWD, NWD, LAMC[:, 1:2], None, ALU.mult))

                    def maxes(u):
                        t, h = units[u]
                        a, b = span(t)
                        dve.wait_ge(s["scores"], u + 1)
                        for p in range(2):
                            c.mark(nc.vector.tensor_reduce(MX[:, u, p:p + 1], PS[4 + 2 * (u % 2) + p][:, 0:b - a], AX, ALU.max))
                        c.sync()
                        nc.vector.tensor_scalar(MX[:, u, :], MX[:, u, :], -scale, None, ALU.mult).then_inc(s["maxes"], 1)

                    def ocopy(u):
                        t, h = units[u]
                        dve.wait_ge(s["out"], u + 1)
                        nc.vector.tensor_copy(H[:, t, h * P:(h + 1) * P], PS[2 + u % 2][:, 0:P]).then_inc(s["ocopy"], 1)

                    maxes(0)
                    maxes(1)
                    for u in range(U):
                        t, h = units[u]
                        a, b = span(t)
                        dve.wait_ge(s["exps"], u + 1)
                        c.link(nc.vector.reciprocal(SS[:, u, :], SS[:, u, :]))
                        c.link(nc.vector.tensor_tensor(SS[:, u, 1:2], SS[:, u, 1:2], NLAM, ALU.mult))
                        pp = PP[:, u % 2]
                        c.link(nc.vector.tensor_scalar(pp[:, 1, 0:b - a], pp[:, 1, 0:b - a], SS[:, u, 1:2], None, ALU.mult))
                        if u >= 2:
                            dve.wait_ge(s["turned"], u - 1)
                        nc.vector.scalar_tensor_tensor(WW[:, u % 2, 0:b - a], pp[:, 0, 0:b - a], SS[:, u, 0:1],
                                                       pp[:, 1, 0:b - a], ALU.mult, ALU.add).then_inc(s["weights"], 1)
                        if u + 2 < U:
                            maxes(u + 2)
                        if u >= 1:
                            ocopy(u - 1)
                    ocopy(U - 1)
                    dve_head_norm(dve, c, s, 2 * D_HD, COLS, lambda t, g: NWD)

                @block.tensor
                def _(pe):
                    pe.wait_ge(s["loads"], 4 * 16)
                    for n in range(2 * D_HEADS):
                        h, isk = n // 2, n % 2
                        if n >= 4:
                            pe.wait_ge(s["copied"], n - 3)
                        for t in range(TILES + isk):
                            o = isk * 1024 + h * P
                            src = PRJ[:, t, o:o + P] if t < TILES else CK[:, h * P:(h + 1) * P]
                            mm = nc.tensor.transpose(PS[n % 4][:, t * P:(t + 1) * P], src, ID)
                        mm.then_inc(s["transposed"], 1)
                    pe.wait_ge(s["copied"], 2 * D_HEADS)

                    def scores(u):
                        t, h = units[u]
                        a, b = span(t)
                        if u >= 2:
                            pe.wait_ge(s["exps"], u - 1)
                        for p in range(2):
                            hp = slice(p * D_HD, (p + 1) * D_HD)
                            mm = nc.tensor.matmul(PS[4 + 2 * (u % 2) + p][:, 0:b - a], QT[hp, h, t * P:(t + 1) * P],
                                                  KTT[hp, h, a:b], start=True, stop=True)
                        mm.then_inc(s["scores"], 1)

                    def turn(u):
                        t, h = units[u]
                        a, b = span(t)
                        pe.wait_ge(s["weights"], u + 1)
                        if u >= 2:
                            pe.wait_ge(s["wt"], u - 1)
                        for n in range((b - a) // P):
                            mm = nc.tensor.transpose(PS[u % 2][:, n * P:(n + 1) * P], WW[:, u % 2, n * P:(n + 1) * P], ID)
                        mm.then_inc(s["turned"], 1)

                    def values(u):
                        t, h = units[u]
                        a, b = span(t)
                        pe.wait_ge(s["wt"], u + 1)
                        if u >= 2:
                            pe.wait_ge(s["ocopy"], u - 1)
                        n = (b - a) // P
                        for k in range(n):
                            tt = a // P + k
                            v = (PRJ[:, tt, 2048 + h * P:2048 + (h + 1) * P] if tt < TILES else CVV[:, h * P:(h + 1) * P])
                            mm = nc.tensor.matmul(PS[2 + u % 2][:, 0:P], WT[:, u % 2, k * P:(k + 1) * P], v,
                                                  start=(k == 0), stop=(k == n - 1))
                        mm.then_inc(s["out"], 1)

                    scores(0)
                    scores(1)
                    for u in range(U):
                        if u + 2 < U:
                            scores(u + 2)
                        turn(u)
                        if u >= 1:
                            values(u - 1)
                    values(U - 1)

        TMK = UP.rearrange("p (t n) -> p t n", t=TILES)
        YC = BIG[:, 0:QBLK * TOK].rearrange("p (b n) -> p b n", b=QBLK)
        KQT = BIG[:, 0:16 * TOK].rearrange("p (b n) -> p b n", b=16)

        WABS = rounded_view("gate_weights", small_at + 4 * 128, 2 * KT * 32)\
            .rearrange("p (a k n) -> p a k n", a=2, k=KT)
        AB = SM[:, 896:992].rearrange("p (t n) -> p t n", t=TILES)

        def stage_gdn_project(l):
            s = signals(STREAM + "abhigh ablow"
                        " banks_free done small taps tapcopy filled conv silu zdone zfree"
                           " abload abdone chain pads cbfree")
            XC = UP[:, 0:8 * XC_W].rearrange("p (b n) -> p b n", b=8)
            CB = UP[:, 3200:3200 + 8 * CV_W].rearrange("p (b n) -> p b n", b=8)
            WC = UP[:, 6400:6656]
            TW = UP[:, 6656:6912].rearrange("p (b n) -> p b n", b=2)
            WAB = UP[:, 6912:7168].rearrange("p (k n) -> p k n", k=KT)
            WABH, WABL = WABS[:, 0], WABS[:, 1]
            rows = CONV_K * QBLK
            chunks = G_QKV // CHUNK
            zchunks = G_HEADS * G_DV // CHUNK
            taps = I["gdn_conv"].rearrange("l t (b c) -> l (t b) c", c=P)
            with nc.Block(no_gpsimd_drain=True) as block:
                @block.sync
                def _(sp):
                    sp.dma_start(TW[:, 0, :], taps[l, 0:P, :]).then_inc(s["small"], 16)
                    sp.dma_start(TW[0:rows - P, 1, :], taps[l, P:rows, :]).then_inc(s["small"], 16)
                    sp.dma_start(WAB, w_in[l, :, :, COL_GDN_AB:COL_GDN_AB + 32]).then_inc(s["abload"], 16)
                    sp_weights(sp, s, lambda n: w_in[l, :, :, ds(n * CHUNK + COL_GDN, CHUNK)], chunks, 0)
                    sp_weights(sp, s, lambda n: w_in[l, :, :, ds(n * CHUNK + COL_GDN_Z, CHUNK)], zchunks, chunks)

                @block.gpsimd
                def _(pool):
                    nc.gpsimd.memset(XC, 0.0).then_inc(s["pads"], 1)
                    pool.wait_ge(s["abhigh"], 1)
                    nc.gpsimd.tensor_tensor(WABL, WAB, WABH.bitcast(F32), ALU.subtract).then_inc(s["ablow"], 1)
                    low_parts(pool, nc.gpsimd, s, chunks + zchunks)

                @block.tensor
                def _(pe):
                    pe_start(pe, s)
                    pe.wait_ge(s["small"], 32)
                    nc.tensor.transpose(PS[7][:, 0:P], TW[:, 0, :], ID)
                    nc.tensor.transpose(PS[7][:, P:rows], TW[0:rows - P, 1, :], ID[0:rows - P, 0:rows - P])\
                        .then_inc(s["taps"], 1)
                    pe.wait_ge(s["tapcopy"], 1)
                    with pe.Fori(0, chunks // 2) as i:
                        for j in range(2):
                            pe.wait_ge(s["banks_free"], 8 * i + 4 * j + 4)
                            pe_chunk_features(pe, s, 4 * j, i, j)
                    pe.wait_ge(s["filled"], 4 * chunks)
                    pe_project(pe, s, ((HTH, HTL), (HTH, HTL)), zchunks, chunks,
                               lambda i, j: (s["zfree"], 2 * i + j + 1), s["zdone"])
                    pe.wait_ge(s["ablow"], 1)
                    for t in range(TILES):
                        out, rows_t = PS[6][:, t * 32:(t + 1) * 32], slice(t * P, (t + 1) * P)
                        for k in range(KT):
                            nc.tensor.matmul(out, HTH[:, k, rows_t], WABH[:, k, :], start=(k == 0), stop=False)
                            nc.tensor.matmul(out, HTL[:, k, rows_t], WABH[:, k, :], start=False, stop=False)
                            mm = nc.tensor.matmul(out, HTH[:, k, rows_t], WABL[:, k, :], start=False, stop=(k == KT - 1))
                    mm.then_inc(s["abdone"], 1)

                @block.scalar
                def _(act):
                    act.sem_inc(s["banks_free"], 8)
                    act.sem_inc(s["silu"], 8)
                    act.sem_inc(s["zfree"], 2)
                    act.wait_ge(s["taps"], 1)
                    nc.scalar.activation(WC[:, 0:rows], PS[7][:, 0:rows], ACT.Copy).then_inc(s["tapcopy"], 1)
                    act.wait_ge(s["abload"], 16)
                    nc.scalar.activation(WABH, WAB, ACT.Copy).then_inc(s["abhigh"], 1)
                    act.wait_ge(s["pads"], 1)

                    def silu(chunk):
                        for b in range(4):
                            blk, n = 4 * chunk + b, 4 * (chunk % 2) + b
                            act.wait_ge(s["conv"], blk + 1)
                            nc.scalar.activation(YC[:, blk, 0:SEQ], CB[:, n, 0:SEQ], ACT.Silu)
                            nc.scalar.activation(YC[:, blk, SEQ:TOK], CB[:, n, CV_S:CV_S + DEC_SEQ], ACT.Silu)\
                                .then_inc(s["silu"], 1)

                    def use(i, j):
                        for b in range(4):
                            n = 4 * j + b
                            act.wait_ge(s["done"], 8 * i + n + 1)
                            act.wait_ge(s["cbfree"], 8 * i + n + 1)
                            nc.scalar.activation(XC[:, n, XC_P:XC_P + SEQ], PS[n][:, 0:SEQ], ACT.Copy)
                            nc.scalar.activation(XC[:, n, XC_S:XC_S + DEC_SEQ], PS[n][:, SEQ:TOK], ACT.Copy)\
                                .then_inc(s["filled"], 1)
                            act.drain().then_inc(s["banks_free"], 1)
                        if i + j > 0:
                            silu(2 * i + j - 1)

                    act_split(act, s, 0, chunks, use, more=True, loop=False)

                    def use_z(i, j):
                        if j == 1:
                            silu(chunks - 1)
                        for t in range(TILES):
                            act.wait_ge(s["zdone"], 6 * i + 3 * j + t + 1)
                            nc.scalar.activation(Z[:, t, ds(2 * CHUNK * i + j * CHUNK, CHUNK)], PS[3 * j + t], ACT.Silu)
                        act.drain().then_inc(s["zfree"], 1)

                    act_split(act, s, chunks, zchunks, use_z)
                    act.wait_ge(s["abdone"], 1)
                    nc.scalar.activation(AB, PS[6][:, 0:TILES * 32].rearrange("p (t n) -> p t n", t=TILES), ACT.Copy)

                @block.vector
                def _(dve):
                    clear_last_stage(dve, s)
                    dve.sem_inc(s["cbfree"], 8)
                    c = Chain(dve, s["chain"])
                    dve.wait_ge(s["tapcopy"], 1)
                    with dve.Fori(0, chunks // 2) as i:
                        c.enter(i, 8 * CONV_K)
                        for pair in range(4):
                            blocks = (2 * pair, 2 * pair + 1)
                            dve.wait_ge(s["filled"], 8 * i + blocks[1] + 1)
                            dve.wait_ge(s["silu"], 8 * i + blocks[1] + 1)
                            for tap in range(CONV_K):
                                for n in blocks:
                                    w = WC[:, ds(8 * i + n + tap * QBLK, 1)]
                                    x = XC[:, n, tap:tap + CV_W]
                                    if tap == 0:
                                        c.mark(nc.vector.tensor_scalar(CB[:, n, :], x, w, None, ALU.mult))
                                    else:
                                        c.sync(but=1)
                                        c.mark(nc.vector.scalar_tensor_tensor(CB[:, n, :], x, w, CB[:, n, :],
                                                                              ALU.mult, ALU.add))
                            c.sync()
                            dve.sem_inc(s["conv"], 2)
                            dve.sem_inc(s["cbfree"], 2)
                        c.leave(chunks // 2)

        GLG = SM[:, 0:48].rearrange("p (t n) -> p t n", t=TILES)
        BTA = SM[:, 48:96].rearrange("p (t n) -> p t n", t=TILES)
        GC = SM[:, 96:144].rearrange("p (t n) -> p t n", t=TILES)
        EG = SM[:, 144:192].rearrange("p (t n) -> p t n", t=TILES)
        NEGG = SM[:, 192:240].rearrange("p (t n) -> p t n", t=TILES)
        EKD = SM[:, 240:288].rearrange("p (t n) -> p t n", t=TILES)
        EGL = SM[:, 288:336].rearrange("p (t n) -> p t n", t=TILES)

        def stage_gdn_prepare(l):
            s = signals("loads nload weighted chain turned copied squares root normed back backcopy aexp spin spexp glog sums"
                           " exponents exps beta")
            SQ = RING[:, 0:2048]
            AL, DTB = SM[:, 336:352], SM[:, 352:368]
            T1, T2, T3, T4 = [RING[:, 2048 + 48 * n:2096 + 48 * n].rearrange("p (t n) -> p t n", t=TILES) for n in range(4)]
            T5 = RING[:, 2240:2288].rearrange("p (t n) -> p t n", t=TILES)
            T6 = RING[:, 2288:2336].rearrange("p (t n) -> p t n", t=TILES)
            RN = SM[:, 640:688].rearrange("p (t n) -> p t n", t=TILES)
            NWG = SM[:, 384:512]
            with nc.Block(no_gpsimd_drain=True) as block:
                @block.gpsimd
                def _(pool):
                    pool.wait_ge(s["nload"], 16)
                    zg = Zf.rearrange("p (g n) -> p g n", n=G_DV)
                    nc.gpsimd.tensor_tensor(zg, zg, bc(NWG, TILES * G_HEADS), ALU.mult).then_inc(s["weighted"], 1)

                @block.sync
                def _(sp):
                    sp.dma_start(AL, I["gdn_A_log"][l].rearrange("d h -> (d h)").partition_broadcast(P)).then_inc(s["loads"], 16)
                    sp.dma_start(DTB, I["gdn_dt_bias"][l].rearrange("d h -> (d h)").partition_broadcast(P)).then_inc(s["loads"], 16)
                    sp.dma_start(NWG, I["gdn_norm"][l].partition_broadcast(P)).then_inc(s["nload"], 16)
                    for d in range(2):
                        sp.dma_start(SST[:, d * G_HEADS:(d + 1) * G_HEADS, :],
                                     I["state_gdn"][0, l, d].rearrange("h k v -> k h v")).then_inc(s["loads"], 16)

                @block.tensor
                def _(pe):
                    for t in range(TILES):
                        for b in range(QBLK // 4):
                            n = t * (QBLK // 4) + b
                            if n >= 4:
                                pe.wait_ge(s["copied"], n - 3)
                            for k in range(4):
                                mm = nc.tensor.transpose(PS[n % 4][:, k * P:(k + 1) * P], YC[:, 4 * b + k, t * P:(t + 1) * P], ID)
                            mm.then_inc(s["turned"], 1)
                    pe.wait_ge(s["glog"], 1)
                    for t in range(TILES):
                        for d in range(2):
                            nc.tensor.matmul(PS[6][:, t * 16 + d * 8:t * 16 + d * 8 + 8], TRI[:, TRI_LO if d else TRI_UP, :],
                                             GLG[:, t, d * 8:d * 8 + 8], start=True, stop=True)
                        mm = nc.tensor.matmul(PS[7][:, t * 16:t * 16 + 16], TRI[:, TRI_ONE, :], GLG[:, t, :], start=True, stop=True)
                    mm.then_inc(s["sums"], 1)
                    pe.wait_ge(s["copied"], TILES * QBLK // 4)
                    for t in range(TILES):
                        pe.wait_ge(s["normed"], t + 1)
                        for b in range(4):
                            n = 4 * t + b
                            if n >= 4:
                                pe.wait_ge(s["backcopy"], n - 3)
                            for k in range(4):
                                g = 4 * b + k
                                mm = nc.tensor.transpose(PS[n % 4][:, k * P:(k + 1) * P], TMK[:, t, g * P:(g + 1) * P], ID)
                            mm.then_inc(s["back"], 1)

                @block.scalar
                def _(act):
                    act.wait_ge(s["loads"], 4 * 16)
                    nc.scalar.activation(AL, AL, ACT.Exp).then_inc(s["aexp"], 1)
                    act.wait_ge(s["spin"], 1)
                    nc.scalar.activation(T2, T2, ACT.Exp).then_inc(s["spexp"], 1)
                    nc.scalar.activation(BTA, AB[:, :, 16:32], ACT.Sigmoid).then_inc(s["beta"], 1)
                    for t in range(TILES):
                        for b in range(QBLK // 4):
                            n = t * (QBLK // 4) + b
                            act.wait_ge(s["turned"], n + 1)
                            nc.scalar.activation(TMK[:, t, 4 * b * P:4 * (b + 1) * P], PS[n % 4], ACT.Copy).then_inc(s["copied"], 1)
                    act.wait_ge(s["squares"], TILES)
                    nc.scalar.activation(RN, RN, ACT.Sqrt).then_inc(s["root"], 1)
                    for n in range(4 * TILES):
                        t, b = divmod(n, 4)
                        act.wait_ge(s["back"], n + 1)
                        nc.scalar.activation(KQT[:, 4 * b:4 * b + 4, t * P:(t + 1) * P],
                                             PS[n % 4].rearrange("p (k n) -> p k n", k=4), ACT.Copy).then_inc(s["backcopy"], 1)
                    act.wait_ge(s["exponents"], 1)
                    nc.scalar.activation(EG, EG, ACT.Exp)
                    nc.scalar.activation(EKD, EKD, ACT.Exp)
                    nc.scalar.activation(EGL, EGL, ACT.Exp).then_inc(s["exps"], 1)

                @block.vector
                def _(dve):
                    clear_last_stage(dve, s)
                    c = Chain(dve, s["chain"])
                    dve.wait_ge(s["loads"], 4 * 16)
                    c.link(nc.vector.tensor_tensor(T1, AB[:, :, 0:16], bc(DTB, TILES), ALU.add))
                    c.link(nc.vector.tensor_scalar(T2, T1, -1.0, None, ALU.mult))
                    nc.vector.tensor_tensor(T2, T1, T2, ALU.min).then_inc(s["spin"], 1)
                    dve.wait_ge(s["spexp"], 1)
                    log1p_parts(dve, c, T2, T3, T4, T5, None)
                    c.link(nc.vector.scalar_tensor_tensor(T1, T1, 0.0, T5, ALU.max, ALU.add))
                    dve.wait_ge(s["aexp"], 1)
                    c.link(nc.vector.tensor_scalar(AL, AL, -1.0, None, ALU.mult))
                    nc.vector.tensor_tensor(GLG, T1, bc(AL, TILES), ALU.mult).then_inc(s["glog"], 1)
                    for t in range(TILES):
                        dve.wait_ge(s["copied"], (t + 1) * QBLK // 4)
                        qk = TMK[:, t, 0:2048]
                        c.link(nc.vector.tensor_tensor(SQ, qk, qk, ALU.mult))
                        c.link(nc.vector.tensor_reduce(RN[:, t, :], SQ.rearrange("p (g n) -> p g n", n=P), AX, ALU.add))
                        nc.vector.tensor_scalar(RN[:, t, :], RN[:, t, :], EPS, None, ALU.add).then_inc(s["squares"], 1)
                    dve.wait_ge(s["root"], 1)
                    c.link(nc.vector.reciprocal(RN, RN))
                    c.link(nc.vector.tensor_scalar(RN[:, :, 0:8], RN[:, :, 0:8], G_DK ** -0.5, None, ALU.mult))
                    for t in range(TILES):
                        qk = TMK[:, t, 0:2048].rearrange("p (g n) -> p g n", n=P)
                        nc.vector.tensor_tensor(qk, qk, bl(RN[:, t, :], P), ALU.mult).then_inc(s["normed"], 1)
                    dve.wait_ge(s["sums"], 1)
                    c.link(nc.vector.tensor_copy(GC, PS[6][:, 0:48].rearrange("p (t n) -> p t n", t=TILES)))
                    c.link(nc.vector.tensor_copy(EGL, PS[7][:, 0:48].rearrange("p (t n) -> p t n", t=TILES)))
                    c.mark(nc.vector.tensor_copy(EG, GC))
                    c.link(nc.vector.tensor_tensor(EKD, EGL, GC, ALU.subtract))
                    dve.sem_inc(s["exponents"], 1)
                    dve.wait_ge(s["exps"], 1)
                    c.link(nc.vector.tensor_scalar(NEGG, EG, -1.0, None, ALU.mult))
                    dve.wait_ge(s["weighted"], 1)

        GUNITS = [(0, 0), (0, 1), (1, 0), (2, 1), (2, 0), (1, 1)]

        def stage_gdn(l):
            s = signals("chain squares mean root mg gb dec gram pair expd lv xdone xcopy ydone updated"
                        " turned tcopy ks r un u out kd snew state supd stored tail")
            BUF = RING.rearrange("p (b h n) -> p b h n", b=16, h=4)
            MTS = [[BUF[:, 4 * par + hg] for hg in range(2)] for par in range(2)]
            QDS = [[BUF[:, 4 * par + 2 + hg] for hg in range(2)] for par in range(2)]
            MOS, XSS, TS, TTS = [[BUF[:, 8 + 2 * k + hg] for hg in range(2)] for k in range(4)]
            JUNK = BIG[:, 16 * TOK + 2 * G_HEADS * G_DV:16 * TOK + 2 * (G_HEADS + 1) * G_DV]
            COLS = SM[:, 688:712]
            U = len(GUNITS)
            LAST = LEVELS - 1

            def bank(n):
                return PS[n].rearrange("p (h n) -> p h n", h=4)

            def latent(v):
                return GUNITS[v][0] > 0

            def ug(v, hg):
                return 2 * v + hg + 1

            def lev(v, n, hg):
                return 2 * LEVELS * v + 2 * n + hg + 1

            def lev1(v, n, hg):
                return 2 * (LEVELS - 1) * v + 2 * (n - 1) + hg + 1

            def lev2(v, n, hg):
                return 2 * (LEVELS - 2) * v + 2 * (n - 1) + hg + 1

            first = {}
            for v, (t, d) in enumerate(GUNITS):
                first.setdefault(t, v)
            last = {t: v for v, (t, d) in enumerate(GUNITS)}

            with nc.Block(no_gpsimd_drain=True) as block:
                @block.sync
                def _(sp):
                    for v in range(2):
                        sp.wait_ge(s["snew"], 2 * v + 2)
                        sp.dma_start(O["new_state_gdn"][0, l, GUNITS[v][1]].rearrange("h k v -> k h v"), ZST[v])\
                            .then_inc(s["stored"], 16)
                    sp.wait_ge(s["stored"], 32)

                @block.gpsimd
                def _(pool):
                    def scaled_mask(v, hg):
                        t, d = GUNITS[v]
                        tri = TRI[:, TRI_LO if d else TRI_UP, :]
                        for h in range(4):
                            g = d * 8 + hg * 4 + h
                            ins = nc.gpsimd.tensor_scalar(MTS[v % 2][hg][:, h, :], tri, GLG[:, t, g:g + 1], None, ALU.mult)
                        ins.then_inc(s["mg"], 1)

                    scaled_mask(0, 0)
                    scaled_mask(0, 1)
                    for v, (t, d) in enumerate(GUNITS):
                        for n in range(LEVELS):
                            for hg in range(2):
                                if n == 0:
                                    pool.wait_ge(s["pair"], ug(v, hg))
                                    if v:
                                        pool.wait_ge(s["tail"], ug(v - 1, hg))
                                else:
                                    pool.wait_ge(s["xdone"], lev(v, n - 1, hg))
                                if n == 1:
                                    pool.wait_ge(s["updated"], lev(v, 0, hg))
                                nc.gpsimd.tensor_tensor(MOS[hg], MTS[v % 2][hg], bc(LVL[:, d, n, :], 4), ALU.mult)\
                                    .then_inc(s["lv"], 1)
                            if v + 1 < U and n in (1, 4):
                                scaled_mask(v + 1, int(n == 4))

                @block.tensor
                def _(pe):
                    def sums(v, hg):
                        pe.wait_ge(s["mg"], ug(v, hg))
                        if v or hg:
                            pe.wait_ge(s["pair"], ug(v, hg) - 1)
                        nc.tensor.matmul(PS[6], TRI[:, TRI_ONE, :], MTS[v % 2][hg].rearrange("p h n -> p (h n)"),
                                         start=True, stop=True).then_inc(s["gb"], 1)

                    def grams(v, hg):
                        ts_ = slice(GUNITS[v][0] * P, (GUNITS[v][0] + 1) * P)
                        pe.wait_ge(s["dec"], ug(v, hg))
                        for h in range(4):
                            k = KQT[:, 8 + hg * 4 + h, ts_]
                            nc.tensor.matmul(PS[6][:, h * P:(h + 1) * P], k, k, start=True, stop=True)
                        for h in range(4):
                            mm = nc.tensor.matmul(PS[7][:, h * P:(h + 1) * P], KQT[:, 8 + hg * 4 + h, ts_],
                                                  KQT[:, hg * 4 + h, ts_], start=True, stop=True)
                        mm.then_inc(s["gram"], 1)

                    def four(b, lhs, rhs):
                        for h in range(4):
                            mm = nc.tensor.matmul(PS[b][:, h * P:(h + 1) * P], lhs[:, h, :], rhs[:, h, :],
                                                  start=True, stop=True)
                        return mm

                    for hg in range(2):
                        sums(0, hg)
                        grams(0, hg)
                    for v, (t, d) in enumerate(GUNITS):
                        ts_ = slice(t * P, (t + 1) * P)
                        for n in range(LEVELS):
                            for hg in range(2):
                                pe.wait_ge(s["lv"], lev(v, n, hg))
                                if n == 0:
                                    for h in range(4):
                                        mm = nc.tensor.transpose(PS[hg][:, h * P:(h + 1) * P], MOS[hg][:, h, :], ID)
                                    mm.then_inc(s["xdone"], 1)
                                else:
                                    pe.wait_ge(s["updated"], lev(v, n - 1, hg))
                                    four(hg, MOS[hg], TS[hg]).then_inc(s["xdone"], 1)
                            if n >= 2:
                                for hg in range(2):
                                    for h in range(4):
                                        mm = nc.tensor.transpose(PS[4 + hg][:, h * P:(h + 1) * P], TS[hg][:, h, :], ID)
                                    mm.then_inc(s["turned"], 1)
                            if n:
                                for hg in range(2):
                                    pe.wait_ge(s["xcopy"], lev1(v, n, hg))
                                    if n >= 2:
                                        pe.wait_ge(s["tcopy"], lev2(v, n - 1, hg))
                                    if n < LAST:
                                        four(2 + hg, TTS[hg], XSS[hg]).then_inc(s["ydone"], 1)
                                    else:
                                        four(2 + hg, XSS[hg], TTS[hg]).then_inc(s["ydone"], 1)
                            if v + 1 < U:
                                if n in (1, 4):
                                    sums(v + 1, int(n == 4))
                                if n in (2, 5):
                                    grams(v + 1, int(n == 5))
                        if latent(v):
                            for hg in range(2):
                                if v >= 4:
                                    pe.wait_ge(s["state"], ug(v - 4, hg))
                                for h in range(4):
                                    hh = hg * 4 + h
                                    mm = nc.tensor.matmul(PS[hg][:, h * P:(h + 1) * P], KQT[:, 8 + hh, ts_],
                                                          SST[:, d * 8 + hh, :], start=True, stop=True)
                                mm.then_inc(s["ks"], 1)
                        for hg in range(2):
                            pe.wait_ge(s["updated"], lev(v, LAST, hg))
                            pe.wait_ge(s["r"], ug(v, hg))
                            four(2 + hg, TTS[hg], MOS[hg]).then_inc(s["un"], 1)
                        for hg in range(2):
                            pe.wait_ge(s["u"], ug(v, hg))
                            mm = four(4 + hg, QDS[v % 2][hg], XSS[hg])
                            if latent(v):
                                for h in range(4):
                                    hh = hg * 4 + h
                                    mm = nc.tensor.matmul(PS[2 + hg][:, h * P:(h + 1) * P], KQT[:, hh, ts_],
                                                          SST[:, d * 8 + hh, :], start=True, stop=True)
                            mm.then_inc(s["out"], 1)
                            pe.wait_ge(s["kd"], ug(v, hg))
                            four(hg, TS[hg], XSS[hg]).then_inc(s["supd"], 1)

                @block.scalar
                def _(act):
                    def exps(v, hg):
                        act.wait_ge(s["dec"], ug(v, hg))
                        q = QDS[v % 2][hg]
                        nc.scalar.activation(q, q, ACT.Exp).then_inc(s["expd"], 1)

                    sq = Chain(act, s["squares"])

                    def squares(v):
                        act.wait_ge(s["tail"], ug(v, 1))
                        for g in range(G_HEADS):
                            act_squares(sq, COLS, JUNK, GUNITS[v][0], g, G_DV)

                    exps(0, 0)
                    exps(0, 1)
                    for v, (t, d) in enumerate(GUNITS):
                        for n in range(1, LEVELS):
                            for hg in range(2):
                                act.wait_ge(s["xdone"], lev(v, n, hg))
                                nc.scalar.activation(XSS[hg], bank(hg), ACT.Copy).then_inc(s["xcopy"], 1)
                            if n >= 2:
                                for hg in range(2):
                                    act.wait_ge(s["turned"], lev2(v, n - 1, hg))
                                    nc.scalar.activation(TTS[hg], bank(4 + hg), ACT.Copy).then_inc(s["tcopy"], 1)
                            if v + 1 < U and n in (2, 5):
                                exps(v + 1, int(n == 5))
                            if n == 3 and v and last[GUNITS[v - 1][0]] == v - 1:
                                squares(v - 1)
                        if t == 0:
                            for hg in range(2):
                                act.wait_ge(s["supd"], ug(v, hg))
                                nc.scalar.activation(ZST[v][:, hg * 4:hg * 4 + 4, :], bank(hg), ACT.Copy)\
                                    .then_inc(s["snew"], 1)
                    squares(U - 1)
                    act_head_root(act, s, COLS)

                @block.vector
                def _(dve):
                    clear_last_stage(dve, s)
                    c = Chain(dve, s["chain"])
                    idb = bc(ID, 4)

                    def exponents(v, hg):
                        t, d = GUNITS[v]
                        dve.wait_ge(s["gb"], ug(v, hg))
                        for h in range(4):
                            g = d * 8 + hg * 4 + h
                            ins = nc.vector.tensor_scalar(QDS[v % 2][hg][:, h, :], bank(6)[:, h, :], GC[:, t, g:g + 1],
                                                          0.0, ALU.subtract, ALU.min)
                        ins.then_inc(s["dec"], 1)

                    def pairs(v, hg):
                        t, d = GUNITS[v]
                        incl = bc(TRI[:, TRI_LO if d else TRI_UP, :], 4)
                        q, m = QDS[v % 2][hg], MTS[v % 2][hg]
                        dve.wait_ge(s["expd"], ug(v, hg))
                        dve.wait_ge(s["gram"], ug(v, hg))
                        c.link(nc.vector.tensor_tensor(q, q, incl, ALU.mult))
                        c.link(nc.vector.tensor_tensor(m, q, bank(6), ALU.mult))
                        c.mark(nc.vector.tensor_tensor(q, q, bank(7), ALU.mult))
                        nc.vector.tensor_tensor(m, m, bl(BTA[:, t, d * 8 + hg * 4:d * 8 + hg * 4 + 4], P), ALU.mult)\
                            .then_inc(s["pair"], 1)

                    for hg in range(2):
                        exponents(0, hg)
                        pairs(0, hg)
                    for v, (t, d) in enumerate(GUNITS):
                        gss = [slice(d * 8 + hg * 4, d * 8 + hg * 4 + 4) for hg in range(2)]
                        for n in range(LEVELS):
                            for hg in range(2):
                                T, TT = TS[hg], TTS[hg]
                                if n == 0:
                                    dve.wait_ge(s["xdone"], lev(v, 0, hg))
                                    nc.vector.tensor_tensor(TT, idb, MOS[hg], ALU.subtract)
                                    nc.vector.tensor_tensor(T, idb, bank(hg), ALU.subtract).then_inc(s["updated"], 1)
                                else:
                                    dve.wait_ge(s["ydone"], lev1(v, n, hg))
                                    dst = T if n < LAST else TT
                                    nc.vector.tensor_tensor(dst, dst, bank(2 + hg), ALU.subtract).then_inc(s["updated"], 1)
                            if v + 1 < U:
                                if n in (1, 4):
                                    exponents(v + 1, int(n == 4))
                                if n == 3:
                                    pairs(v + 1, 0)
                        for hg in range(2):
                            MO = MOS[hg]
                            vv = TMK[:, t, 2048 + hg * 512:2048 + hg * 512 + 512].rearrange("p (h n) -> p h n", h=4)
                            kk = TMK[:, t, 1024 + hg * 512:1024 + hg * 512 + 512].rearrange("p (h n) -> p h n", h=4)
                            if latent(v):
                                dve.wait_ge(s["ks"], ug(v - 2, hg))
                                c.link(nc.vector.tensor_tensor(MO, bank(hg), bl(EG[:, t, gss[hg]], P), ALU.mult))
                                nc.vector.tensor_tensor(MO, vv, MO, ALU.subtract).then_inc(s["r"], 1)
                            else:
                                nc.vector.tensor_copy(MO, vv).then_inc(s["r"], 1)
                            nc.vector.tensor_tensor(TS[hg], kk, bl(EKD[:, t, gss[hg]], P), ALU.mult).then_inc(s["kd"], 1)
                        for hg in range(2):
                            dve.wait_ge(s["un"], ug(v, hg))
                            nc.vector.tensor_tensor(XSS[hg], bank(2 + hg), bl(BTA[:, t, gss[hg]], P), ALU.mult)\
                                .then_inc(s["u"], 1)
                        if v + 1 < U:
                            pairs(v + 1, 1)
                        for hg in range(2):
                            MO = MOS[hg]
                            oo = H[:, t, hg * 512:hg * 512 + 512].rearrange("p (h n) -> p h n", h=4)
                            dve.wait_ge(s["out"], ug(v, hg))
                            if first[t] == v:
                                c.mark(nc.vector.tensor_copy(oo, bank(4 + hg)))
                            else:
                                c.mark(nc.vector.tensor_tensor(oo, oo, bank(4 + hg), ALU.add))
                            if latent(v):
                                c.link(nc.vector.tensor_tensor(MO, bank(2 + hg), bl(EG[:, t, gss[hg]], P), ALU.mult))
                                c.mark(nc.vector.tensor_tensor(oo, oo, MO, ALU.add))
                                dve.wait_ge(s["supd"], ug(v, hg))
                                st = SST[:, d * 8 + hg * 4:d * 8 + hg * 4 + 4, :]
                                c.link(nc.vector.tensor_tensor(st, st, bl(EGL[:, t, gss[hg]], P), ALU.mult))
                                nc.vector.tensor_tensor(st, st, bank(hg), ALU.add).then_inc(s["state"], 1)
                                dve.wait_ge(s["state"], ug(v - 2, hg))
                            else:
                                c.sync()
                                dve.wait_ge(s["snew"], ug(v, hg))
                            dve.sem_inc(s["tail"], 1)
                    dve_head_norm(dve, c, s, G_DV, COLS, lambda t, g: Z[:, t, g * G_DV:(g + 1) * G_DV])

        ZB = BIG[:, 16 * TOK:16 * TOK + 2 * G_HEADS * G_DV]
        ZST = [ZB[:, v * 1024:(v + 1) * 1024].rearrange("p (h n) -> p h n", h=8) for v in range(2)]

        def stage_merge(l, n_branch):
            s = signals(STREAM + "gate_banks_free branch_banks_free done"
                        " turned turned_high turned_low ready gate used chain")
            GT = BIG[:, 0:TILES * CHUNK].rearrange("p (t n) -> p t n", t=TILES)
            TM = BIG[:, 1536:3072].rearrange("p (t n) -> p t n", t=TILES)
            wb = I["w_branch"].rearrange("l b (k p) n -> l b p k n", p=P)
            chunks = D // CHUNK
            col = COL_GATES + n_branch * D
            with nc.Block(no_gpsimd_drain=True) as block:
                @block.sync
                def _(sp):
                    with sp.Fori(0, chunks) as i:
                        sp.wait_ge(s["free"], 2 * i + 1)
                        load_chunk(sp, s, 0, w_in[l, :, :, ds(i * CHUNK + col, CHUNK)])
                        sp.wait_ge(s["free"], 2 * i + 2)
                        load_chunk(sp, s, 1, wb[l, n_branch, :, :, ds(i * CHUNK, CHUNK)])

                @block.tensor
                def _(pe):
                    pe_start(pe, s)
                    pe_transpose_tokens(pe, H, s["ready"], s["turned"])
                    pe.wait_ge(s["turned_low"], 2 * TILES)
                    pe_project(pe, s, ((HTH, HTL), (OTH, OTL)), 2 * chunks, 0,
                               lambda i, j: (s["branch_banks_free" if j else "gate_banks_free"], i + 1), s["done"])

                @block.gpsimd
                def _(pool):
                    low_parts(pool, nc.gpsimd, s, 2 * chunks)

                @block.scalar
                def _(act):
                    act.sem_inc(s["gate_banks_free"], 1)
                    act_turned_high(act, OTH, s)

                    def use(i, j):
                        if j == 1:
                            return
                        act.wait_ge(s["used"], i + 1)
                        for t in range(TILES):
                            act.wait_ge(s["done"], 6 * i + t + 1)
                            nc.scalar.activation(GT[:, t, :], PS[t], ACT.Sigmoid).then_inc(s["gate"], 1)
                        act.drain().then_inc(s["gate_banks_free"], 1)

                    act_split(act, s, 0, 2 * chunks, use)

                @block.vector
                def _(dve):
                    clear_last_stage(dve, s)
                    c = Chain(dve, s["chain"])
                    dve.sem_inc(s["ready"], TILES)
                    dve.sem_inc(s["branch_banks_free"], 1)
                    dve.sem_inc(s["used"], 1)
                    dve_turned_low(dve, OTH, OTL, s)
                    with dve.Fori(0, chunks) as i:
                        c.enter(i, TILES if n_branch == 0 else 2 * TILES)
                        dve.wait_ge(s["gate"], 3 * i + 3)
                        dve.wait_ge(s["done"], 6 * i + 6)
                        for t in range(TILES):
                            dst = MACC[:, t, ds(i * CHUNK, CHUNK)]
                            if n_branch == 0:
                                c.mark(nc.vector.tensor_tensor(dst, GT[:, t, :], PS[3 + t], ALU.mult))
                            else:
                                c.link(nc.vector.tensor_tensor(TM[:, t, :], GT[:, t, :], PS[3 + t], ALU.mult))
                                c.mark(nc.vector.tensor_tensor(dst, dst, TM[:, t, :], ALU.add))
                        c.sync()
                        dve.sem_inc(s["branch_banks_free"], 1)
                        dve.sem_inc(s["used"], 1)
                        c.leave(chunks)

        def stage_out(l):
            s = signals(STREAM + "banks_free done turned turned_high turned_low ready loads"
                        " chain")
            G1 = BIG[:, 0:2 * D].rearrange("p (g n) -> p g n", g=2)
            TM = BIG[:, 2 * D:2 * D + 1536].rearrange("p (t n) -> p t n", t=TILES)
            wo = I["w_out"].rearrange("l (k p) n -> l p k n", p=P)
            chunks = D // CHUNK
            with nc.Block(no_gpsimd_drain=True) as block:
                @block.sync
                def _(sp):
                    for g in range(2):
                        sp.dma_start(G1[:, g, :], modd[g, 2 * D:3 * D].partition_broadcast(P)).then_inc(s["loads"], 16)
                    sp_weights(sp, s, lambda n: wo[l, :, :, ds(n * CHUNK, CHUNK)], chunks, 0)

                @block.tensor
                def _(pe):
                    pe_start(pe, s)
                    pe_transpose_tokens(pe, MACC, s["ready"], s["turned"])
                    pe.wait_ge(s["turned_low"], 2 * TILES)
                    pe_project(pe, s, ((OTH, OTL), (OTH, OTL)), chunks, 0,
                               lambda i, j: (s["banks_free"], 2 * i + j + 1), s["done"])

                @block.gpsimd
                def _(pool):
                    low_parts(pool, nc.gpsimd, s, chunks)

                @block.scalar
                def _(act):
                    act_turned_high(act, OTH, s)
                    act_split(act, s, 0, chunks, lambda i, j: None)

                @block.vector
                def _(dve):
                    clear_last_stage(dve, s)
                    c = Chain(dve, s["chain"])
                    dve.sem_inc(s["ready"], TILES)
                    dve.sem_inc(s["banks_free"], 2)
                    dve_turned_low(dve, OTH, OTL, s)
                    dve.wait_ge(s["loads"], 32)
                    for j in range(chunks):
                        cs = slice(j * CHUNK, (j + 1) * CHUNK)
                        for t in range(TILES):
                            dve.wait_ge(s["done"], 3 * j + t + 1)
                            c.link(nc.vector.tensor_tensor(TM[:, t, :], PS[3 * j + t], G1[:, int(t > 0), cs], ALU.mult))
                            c.mark(nc.vector.tensor_tensor(X[:, t, cs], X[:, t, cs], TM[:, t, :], ALU.add))
                    c.sync()

        MACCf = MACC.rearrange("p t n -> p (t n)")
        SC = [BIG[:, 0:2048], MACCf[:, 0:2048], Zf[:, 1024:3072]]
        OH = RING[:, 6144:8192]
        IDX = Zf[:, 0:384].bitcast(U32).rearrange("p (t n) -> p t n", t=TILES)
        GATE = Zf[:, 384:768].rearrange("p (t n) -> p t n", t=TILES)
        DOTS = MACCf[:, 2048:2432].rearrange("p (t n) -> p t n", t=TILES)
        NB = 8
        IDS = MACCf[:, 2432:2432 + 2 * NB].bitcast(U32)
        DST = MACCf[:, 2496:2496 + 2 * NB]
        SSF = SST.rearrange("p g n -> p (g n)")
        SCW, SCX = SSF[:, 0:256], SSF[:, 256:384]
        V2 = SSF[:, 384:416].rearrange("p (a n) -> p a n", a=2)
        I2 = SSF[:, 416:448].bitcast(U32)
        CAND, CANX = SSF[:, 448:704], SSF[:, 704:960]
        BV1, BI1 = SSF[:, 960:976], SSF[:, 976:992].bitcast(U32)
        I16F = SSF[:, 992:1248]
        BV = SSF[:, 1248:1376]
        BI, BA = SSF[:, 1376:1504].bitcast(U32), SSF[:, 1504:1632].bitcast(U32)
        BF = SSF[:, 1632:1760]
        SEL = SSF[:, 1760:2016].rearrange("p (a n) -> p a n", a=2)
        RS8 = SSF[:, 2016:2024]

        TOP_PASS = 1 + 10 + 1 + 1 + 5 + 2

        def top_pass(dve, c, tick, t, i):

            def step(ins):
                c.link(ins)
                dve.sem_inc(tick, 1)

            def top16(vals, work, v16, i16):
                step(nc.vector.max(v16[:, 0:8], vals))
                step(nc.vector.max_index(i16[:, 0:8], v16[:, 0:8], vals))
                step(nc.vector.match_replace(work, v16[:, 0:8], vals, BIGNEG))
                step(nc.vector.max(v16[:, 8:16], work))
                step(nc.vector.max_index(i16[:, 8:16], v16[:, 8:16], work))

            step(nc.vector.tensor_copy(SCW, SC[t][:, ds(256 * i, 256)]))
            for half in range(2):
                top16(SCW[:, half * P:(half + 1) * P], SCX, V2[:, half, :], I2[:, half * TOPK:(half + 1) * TOPK])
            c.mark(nc.vector.tensor_copy(I16F[:, ds(2 * TOPK * i, 2 * TOPK)], I2))
            step(nc.vector.tensor_tensor(CAND.rearrange("p (a b) -> p a b", a=TOPK), bl(V2[:, 0, :], TOPK),
                                         bc(V2[:, 1, :], TOPK), ALU.add))
            top16(CAND, CANX, BV1, BI1)
            c.mark(nc.vector.tensor_copy(BV[:, ds(TOPK * i, TOPK)], BV1))
            c.link(nc.vector.tensor_copy(BI[:, ds(TOPK * i, TOPK)], BI1))

        def pick_half(dve, c, s, t, half):
            i4 = I16F.rearrange("p (h a n) -> p h a n", h=8, a=2)
            oh = OH.rearrange("p (h k a) -> p h k a", h=8, k=TOPK)
            if half == 0:
                g3 = GATE[:, t, :].rearrange("p (h k) -> p h k", h=8)
                b3 = BV.rearrange("p (h k) -> p h k", h=8)
                nc.vector.tensor_tensor(g3, b3, b3[:, :, 0:1].to_broadcast([P, 8, TOPK]), ALU.subtract)\
                    .then_inc(s["dif"], 1)
                c.link(nc.vector.tensor_scalar(BA, BI, 4, None, ALU.logical_shift_right))
            else:
                c.link(nc.vector.tensor_scalar(BA, BI, TOPK - 1, None, ALU.bitwise_and))
            c.link(nc.vector.tensor_copy(BF, BA))
            bf = BF.rearrange("p (h k) -> p h k", h=8).unsqueeze(3).to_broadcast([P, 8, TOPK, TOPK])
            io = POS[:, POS_IOTA:POS_IOTA + TOPK].unsqueeze(1).unsqueeze(1).to_broadcast([P, 8, TOPK, TOPK])
            c.link(nc.vector.tensor_tensor(oh, bf, io, ALU.is_equal))
            c.link(nc.vector.tensor_tensor(oh, oh, i4[:, :, half, :].unsqueeze(2).to_broadcast([P, 8, TOPK, TOPK]),
                                           ALU.mult))
            c.link(nc.vector.tensor_reduce(SEL[:, half, :], OH.rearrange("p (g a) -> p g a", a=TOPK), AX, ALU.add))

        def pick_rows(dve, c, s, t, picked):
            g3 = GATE[:, t, :].rearrange("p (h k) -> p h k", h=8)
            c.link(nc.vector.tensor_scalar(SEL[:, 0, :], SEL[:, 0, :], float(N_KEYS), LAMC[:, 2:3], ALU.mult, ALU.add))
            nc.vector.tensor_tensor(IDX[:, t, :], SEL[:, 0, :], SEL[:, 1, :], ALU.add).then_inc(s["rows"], 1)
            dve.wait_ge(s["exp"], picked)
            c.link(nc.vector.tensor_reduce(RS8, g3, AX, ALU.add))
            c.link(nc.vector.reciprocal(RS8, RS8))
            c.link(nc.vector.tensor_tensor(g3, g3, bl(RS8, TOPK), ALU.mult))

        def act_gates(act, s, t, picked):
            act.wait_ge(s["dif"], picked)
            nc.scalar.activation(GATE[:, t, :], GATE[:, t, :], ACT.Exp).then_inc(s["exp"], 1)

        def stage_route(l):
            s = signals(STREAM + "banks_free done filled keys kturned kcopy scored scopy score_banks_free"
                        " chain tick dif exp rows")
            QP = BIG[:, 6144:9216].rearrange("p (j b n) -> p j b n", j=2, b=4)
            KY = BIG[:, 12288:12544].rearrange("p (a n) -> p a n", a=2)
            KYT = BIG[:, 12544:12800].rearrange("p (a n) -> p a n", a=2)
            wq = I["peer_wq"].rearrange("l (k p) n -> l p k n", p=P)
            chunks = PEER_HEADS * PEER_DQ // CHUNK
            with nc.Block(no_gpsimd_drain=True) as block:
                @block.sync
                def _(sp):
                    sp.dma_start(KY, I["peer_keys"][l].rearrange("a n d -> n a d")).then_inc(s["keys"], 16)
                    sp_weights(sp, s, lambda n: wq[l, :, :, ds(n * CHUNK, CHUNK)], chunks, 0)

                @block.tensor
                def _(pe):
                    pe_start(pe, s)
                    pe.wait_ge(s["keys"], 16)
                    for a in range(2):
                        mm = nc.tensor.transpose(PS[7][:, a * P:(a + 1) * P], KY[:, a, :], ID)
                    mm.then_inc(s["kturned"], 1)
                    pe.wait_ge(s["kcopy"], 1)
                    with pe.Fori(0, chunks // 2) as i:
                        for j in range(2):
                            pe.wait_ge(s["banks_free"], 8 * i + 4 * j + 4)
                            pe_chunk_features(pe, s, 0, i, j)
                            pe.wait_ge(s["filled"], 8 * i + 4 * j + 4)
                            for t in range(TILES):
                                pe.wait_ge(s["score_banks_free"], 6 * i + 3 * j + t + 1)
                                for k in range(4):
                                    mm = nc.tensor.matmul(PS[4 + t][:, k * P:(k + 1) * P], QP[:, j, k, t * P:(t + 1) * P],
                                                          KYT[:, k % 2, :], start=True, stop=True)
                                mm.then_inc(s["scored"], 1)

                @block.scalar
                def _(act):
                    act.sem_inc(s["banks_free"], 4)
                    act.sem_inc(s["score_banks_free"], TILES)
                    act.wait_ge(s["kturned"], 1)
                    nc.scalar.activation(KYT, PS[7][:, 0:256].rearrange("p (a n) -> p a n", a=2), ACT.Copy).then_inc(s["kcopy"], 1)

                    def use(i, j):
                        for b in range(4):
                            act.wait_ge(s["done"], 8 * i + 4 * j + b + 1)
                            nc.scalar.activation(QP[:, j, b, :], PS[b][:, 0:TOK], ACT.Copy).then_inc(s["filled"], 1)
                            act.drain().then_inc(s["banks_free"], 1)
                        for t in range(TILES):
                            act.wait_ge(s["scored"], 6 * i + 3 * j + t + 1)
                            nc.scalar.activation(SC[t][:, ds(1024 * i + 512 * j, 512)], PS[4 + t], ACT.Copy)\
                                .then_inc(s["scopy"], 1)
                            act.drain().then_inc(s["score_banks_free"], 1)

                    act_split(act, s, 0, chunks, use)
                    act_gates(act, s, 0, 1)

                @block.gpsimd
                def _(pool):
                    low_parts(pool, nc.gpsimd, s, chunks)

                @block.vector
                def _(dve):
                    clear_last_stage(dve, s)
                    c = Chain(dve, s["chain"])
                    with dve.Fori(0, chunks) as i:
                        c.enter(i, 2 * TOP_PASS)
                        dve.wait_ge(s["scopy"], TILES * i + 1)
                        dve.sem_inc(s["tick"], 1)
                        for k in range(2):
                            top_pass(dve, c, s["tick"], 0, 2 * i + k)
                        c.leave(chunks)
                    for half in range(2):
                        pick_half(dve, c, s, 0, half)
                    pick_rows(dve, c, s, 0, 1)

        def stage_experts(l):
            s = signals("staged chain dots acted used_low used_high_dot used_high_sum started loads tick dif exp rows"
                        " weights diag diag_used summed zeros")
            per_tile = SLOTS // (2 * NB)
            seen = 16 * 2 * TILES * per_tile * l
            UB = BIG[:, 0:2 * NB * D].rearrange("p (b n) -> p b n", b=2 * NB)
            JUNK = BIG[:, 2 * NB * D:2 * NB * D + D]
            DIAG = BIG[:, 2 * NB * D + D:2 * NB * D + 2 * D].rearrange("p (b n) -> p b n", b=NB)
            ZERO = SM[:, 0:P]
            Y = YSUM.rearrange("p (t n) -> p t n", t=TILES)
            G2 = RING[:, 0:2 * D].rearrange("p (g n) -> p g n", g=2)
            tables = [I["peer_u"].rearrange("l e d -> (l e) d"), I["peer_v"].rearrange("l e d -> (l e) d")]
            with nc.Block(no_gpsimd_drain=True) as block:
                @block.sync
                def _(sp):
                    for g in range(2):
                        sp.dma_start(G2[:, g, :], modd[g, 5 * D:6 * D].partition_broadcast(P)).then_inc(s["loads"], 16)

                @block.gpsimd
                def _(pool):
                    for t in range(TILES):
                        if t > 0:
                            pool.wait_ge(s["rows"], t)
                        for phase in range(2):
                            with pool.Fori(0, per_tile) as i:
                                pos = i + (2 * t + phase) * per_tile
                                for half in range(2):
                                    if half == 0:
                                        pool.wait_ge(s["used_low"], pos + 1)
                                    else:
                                        pool.wait_ge(s["used_high_dot"], per_tile * (t + phase) + 1 + (0 if phase else i))
                                        pool.wait_ge(s["used_high_sum"], per_tile * t + 1 + (i if phase else 0))
                                    nc.gpsimd.tensor_copy(IDS[:, half * NB:(half + 1) * NB],
                                                          IDX[:, t, ds(2 * NB * i + half * NB, NB)]).then_inc(s["staged"], 1)
                                    pool.wait_ge(s["staged"], 2 * pos + half + 1)
                                    pool.sem_inc(s["started"], 1)
                                    for n in range(NB):
                                        b = half * NB + n
                                        nc.gpsimd.indirect_dma_start(
                                            out=UB[:, b, :], out_offset=None, in_=tables[phase],
                                            in_offset=bass.IndirectOffsetOnAxis(ap=IDS[:, b:b + 1], axis=0))\
                                            .then_inc(got[b], 16)

                @block.tensor
                def _(pe):
                    pe.sem_inc(s["used_high_sum"], 1)
                    pe.sem_inc(s["diag_used"], NB)
                    pe.wait_ge(s["zeros"], 1)
                    for t in range(TILES):
                        landed = seen + 16 * (2 * t + 1) * per_tile
                        for b in range(2):
                            nc.tensor.matmul(PS[2 * t + b], ZERO, H[:, t, b * 512:(b + 1) * 512], start=True, stop=False)
                        with pe.Fori(0, per_tile) as i:
                            for n in range(NB):
                                pe.wait_ge(s["diag"], NB * per_tile * t + NB * i + n + 1)
                                pe.wait_ge(got[NB + n], landed + 16 * i + 16)
                                for b in range(2):
                                    mm = nc.tensor.matmul(PS[2 * t + b], DIAG[:, n, :], UB[:, NB + n, b * 512:(b + 1) * 512],
                                                          start=False, stop=False)
                                mm.then_inc(s["diag_used"], 1)
                            pe.drain().then_inc(s["used_high_sum"], 1)
                        for b in range(2):
                            mm = nc.tensor.matmul(PS[2 * t + b], ZERO, H[:, t, b * 512:(b + 1) * 512], start=False, stop=True)
                        mm.then_inc(s["summed"], 1)

                @block.scalar
                def _(act):
                    for t in range(TILES):
                        act.wait_ge(s["dots"], t + 1)
                        nc.scalar.activation(DOTS[:, t, :], DOTS[:, t, :], ACT.Gelu).then_inc(s["acted"], 1)
                        act.wait_ge(s["weights"], t + 1)
                        for lo, hi in ((0, per_tile - 2), (per_tile - 2, per_tile)):
                            with act.Fori(lo, hi) as i:
                                for n in range(NB):
                                    act.wait_ge(s["diag_used"], NB * per_tile * t + NB * i + n + 1)
                                    w = DOTS[:, t, ds(2 * NB * i + NB + n, 1)]
                                    nc.scalar.activation(DIAG[:, n, :], ID, ACT.Copy, scale=w).then_inc(s["diag"], 1)
                            if lo == 0 and t + 1 < TILES:
                                act_gates(act, s, t + 1, t + 1)

                @block.vector
                def _(dve):
                    clear_last_stage(dve, s)
                    c = Chain(dve, s["chain"])
                    dve.sem_inc(s["used_low"], 1)
                    dve.sem_inc(s["used_high_dot"], 1)
                    nc.vector.memset(ZERO, 0.0).then_inc(s["zeros"], 1)
                    c.link(nc.vector.memset(Y, 0.0))

                    def finish(t):
                        dve.wait_ge(s["summed"], t + 1)
                        for b in range(2):
                            yb = Y[:, t, b * 512:(b + 1) * 512]
                            c.mark(nc.vector.tensor_tensor(yb, yb, PS[2 * t + b], ALU.add))
                        c.sync()
                        c.link(nc.vector.tensor_tensor(Y[:, t, :], Y[:, t, :], G2[:, int(t > 0), :], ALU.mult))
                        c.link(nc.vector.tensor_tensor(X[:, t, :], X[:, t, :], Y[:, t, :], ALU.add))

                    def sum_low(t, first, passes, heads=0, head=0):
                        landed = seen + 16 * ((2 * t + 1) * per_tile + first)
                        with dve.Fori(0, passes) as i:
                            c.enter(i, NB + 1 + heads * TOP_PASS)
                            c.link(nc.vector.tensor_copy(DST[:, 0:NB], DOTS[:, t, ds(2 * NB * i + 2 * NB * first, NB)]))
                            for n in range(NB):
                                dve.wait_ge(got[n], landed + 16 * i + 16)
                                c.link(nc.vector.scalar_tensor_tensor(Y[:, t, :], UB[:, n, :], DST[:, n:n + 1], Y[:, t, :],
                                                                      ALU.mult, ALU.add))
                            dve.sem_inc(s["used_low"], 1)
                            for k in range(heads):
                                top_pass(dve, c, s["tick"], t + 1, heads * i + head + k)
                            c.leave(passes)

                    for t in range(TILES):
                        landed = seen + 16 * 2 * t * per_tile
                        with dve.Fori(0, per_tile) as i:
                            c.enter(i, 2 * (NB + 1))
                            for half in range(2):
                                for n in range(NB):
                                    b = half * NB + n
                                    dve.wait_ge(got[b], landed + 16 * i + 16)
                                    c.link(nc.vector.scalar_tensor_tensor(JUNK, UB[:, b, :], 1.0, H[:, t, :], ALU.mult, ALU.mult,
                                                                          accum_out=DST[:, b:b + 1]))
                                dve.sem_inc(s["used_high_dot" if half else "used_low"], 1)
                                c.mark(nc.vector.tensor_copy(DOTS[:, t, ds(2 * NB * i + half * NB, NB)],
                                                             DST[:, half * NB:(half + 1) * NB]))
                            c.leave(per_tile)
                        c.sync()
                        dve.sem_inc(s["dots"], 1)
                        if t == 1:
                            dve.wait_ge(s["loads"], 32)
                        if t > 0:
                            finish(t - 1)
                        dve.wait_ge(s["acted"], t + 1)
                        c.link(nc.vector.tensor_tensor(DOTS[:, t, :], DOTS[:, t, :], GATE[:, t, :], ALU.mult))
                        dve.sem_inc(s["weights"], 1)
                        if t + 1 == TILES:
                            sum_low(t, 0, per_tile)
                        else:
                            sum_low(t, 0, 2, heads=2)
                            sum_low(t, 2, 4, heads=1, head=4)
                            pick_half(dve, c, s, t + 1, 0)
                            sum_low(t, 6, 1)
                            pick_half(dve, c, s, t + 1, 1)
                            pick_rows(dve, c, s, t + 1, t + 1)
                            sum_low(t, 7, 1)
                    finish(TILES - 1)

        with nc.Fori(0, DEPTH) as l:
            stage_mod(l)
            stage_norm(l, 0)
            stage_project(l, [(COL_RET, 4, PRJ, ACT.Copy), (COL_RET_G, 2, Z, ACT.Silu)], (2, ROPR, R_HEADS, R_DK))
            stage_retention(l)
            stage_merge(l, 0)
            stage_project(l, [(COL_DIFF, 6, PRJ, ACT.Copy)], (4, ROPD, 2 * D_HEADS, D_HD))
            stage_diff(l)
            stage_merge(l, 1)
            stage_gdn_project(l)
            stage_gdn_prepare(l)
            stage_gdn(l)
            stage_merge(l, 2)
            stage_out(l)
            stage_norm(l, 1)
            stage_route(l)
            stage_experts(l)

        s = signals("loads squares mean root chain ready stored")
        with nc.Block(no_gpsimd_drain=True) as block:
            @block.sync
            def _(sp):
                sp.dma_start(UP[:, 0:D], I["norm_f_w"].partition_broadcast(P)).then_inc(s["loads"], 16)
                sp.wait_ge(s["ready"], 1)
                sp.dma_start(O["y_prompt"][0], H[:, 0, :]).then_inc(s["stored"], 16)
                sp.wait_ge(s["ready"], 3)
                sp.dma_start(O["y_sample"][0].rearrange("(t p) n -> p t n", p=P), H[:, 1:3, :]).then_inc(s["stored"], 16)
                sp.wait_ge(s["stored"], 32)

            @block.scalar
            def _(act):
                for t in range(TILES):
                    nc.scalar.activation(BIG[:, t * D:(t + 1) * D], X[:, t, :], ACT.Square, accum_out=SM[:, t:t + 1])\
                        .then_inc(s["squares"], 1)
                act.wait_ge(s["mean"], 1)
                nc.scalar.activation(SM[:, 4:7], SM[:, 0:3], ACT.Sqrt).then_inc(s["root"], 1)

            @block.vector
            def _(dve):
                c = Chain(dve, s["chain"])
                dve.wait_ge(s["squares"], TILES)
                nc.vector.tensor_scalar(SM[:, 0:3], SM[:, 0:3], 1.0 / D, EPS, ALU.mult, ALU.add).then_inc(s["mean"], 1)
                dve.wait_ge(s["root"], 1)
                c.link(nc.vector.reciprocal(SM[:, 4:7], SM[:, 4:7]))
                dve.wait_ge(s["loads"], 16)
                for t in range(TILES):
                    nc.vector.scalar_tensor_tensor(H[:, t, :], X[:, t, :], SM[:, 4 + t:5 + t], UP[:, 0:D],
                                                   ALU.mult, ALU.mult).then_inc(s["ready"], 1)


_INS = ["x_prompt", "x_sample", "cache_diff_k", "cache_diff_v", "state_ret", "state_gdn", "c", "c_ctx", "norm1_w",
        "norm2_w", "w_mod", "b_mod", "w_in", "ret_decay", "ret_norm", "diff_lambda", "diff_norm", "gdn_conv",
        "gdn_A_log", "gdn_dt_bias", "gdn_norm", "w_branch", "w_out", "peer_wq", "peer_keys", "peer_u", "peer_v",
        "norm_f_w"]
_OUTS = [("y_prompt", (1, SEQ, D)), ("y_sample", (1, DEC_SEQ, D)),
         ("new_cache_diff_k", (1, DEPTH, SEQ, D_HEADS, 2, D_HD)), ("new_cache_diff_v", (1, DEPTH, SEQ, D_HEADS, 2 * D_HD)),
         ("new_state_ret", (1, DEPTH, 2, R_HEADS, R_DK, R_DV)), ("new_state_gdn", (1, DEPTH, 2, G_HEADS, G_DK, G_DV))]


def kernel(**inputs):
    import numpy as _np
    import concourse.bacc as _bacc
    from concourse import mybir as _mybir
    from concourse.bass_utils import run_bass_kernel_spmd as _run

    nc = _bacc.Bacc("TRN2", target_bir_lowering=False, num_devices=1)
    arrays, ins, outs = {}, {}, {}
    for name, a in [(n, inputs[n]) for n in _INS] + list(shape_tables().items()):
        a = _np.ascontiguousarray(a)
        arrays[f"in_{name}_dram"] = a
        ins[name] = nc.dram_tensor(f"in_{name}_dram", a.shape, _mybir.dt.from_np(a.dtype), kind="ExternalInput").ap()
    for name, shape in _OUTS:
        outs[name] = nc.dram_tensor(f"out_{name}_dram", shape, _mybir.dt.float32, kind="ExternalOutput").ap()
    build(nc, ins, outs)
    r = _run(nc, [arrays], core_ids=[0])
    return tuple(r.results[0][f"out_{name}_dram"] for name, _ in _OUTS)
```
